# Optimizing a Trainium2 kernel written in Bass

```python
import math
import jax
import jax.numpy as jnp
from jax import lax
import numpy as np

D_MODEL = 1024
BATCH = 1
SEQ = 512
DEPTH = 2

GRID_W = 64
CTX_LEN = 256
EPS = 1e-6
ADA_CHUNKS = 6

MLA_HEADS = 4
MLA_NOPE = 64
MLA_ROPE = 32
MLA_QK = MLA_NOPE + MLA_ROPE
MLA_V = 64
MLA_Q_LORA = 192
MLA_KV_LORA = 128
ROPE_THETA = 10000.0
Q_BLOCK = 128

GDN_HEADS = 4
GDN_DK = 128
GDN_DV = 128
GDN_CONV = 3
GDN_CHUNK = 64

POOL_WINDOWS = (2, 4, 8, 16)
POOL_GROUP = 64
POOL_WIDTH = POOL_GROUP * len(POOL_WINDOWS)

D_MIX = MLA_HEADS * MLA_V + GDN_HEADS * GDN_DV + POOL_WIDTH

N_EXPERTS = 16
EC_CAPACITY_FACTOR = 2
D_EXPERT = 512

IN_SPLITS = (MLA_Q_LORA, MLA_KV_LORA, MLA_ROPE,
             GDN_HEADS * GDN_DK, GDN_HEADS * GDN_DK, GDN_HEADS * GDN_DV, GDN_HEADS * GDN_DV,
             2 * GDN_HEADS, 2 * GDN_HEADS, POOL_WIDTH)
IN_COLS = sum(IN_SPLITS)

kernel_name = "hybrid_mla_gdn_pool_ecmoe_dit"

def rms_norm(x, g):
    xf = x.astype(jnp.float32)
    y = xf * lax.rsqrt(jnp.mean(xf * xf, axis=-1, keepdims=True) + EPS)
    return (y * g.astype(jnp.float32)).astype(x.dtype)

def l2_norm(x):
    xf = x.astype(jnp.float32)
    return (xf * lax.rsqrt(jnp.sum(xf * xf, axis=-1, keepdims=True) + EPS)).astype(x.dtype)

def modulate(x, g, shift, scale):
    return rms_norm(x, g) * (1.0 + scale) + shift

def split_cols(p):
    offsets = [int(o) for o in np.cumsum(IN_SPLITS)[:-1]]
    return jnp.split(p, offsets, axis=-1)

def axial_rope_tables(n_tokens):
    rows = n_tokens // GRID_W
    row = jnp.repeat(jnp.arange(rows, dtype=jnp.float32), GRID_W)
    col = jnp.tile(jnp.arange(GRID_W, dtype=jnp.float32), rows)
    n_freq = MLA_ROPE // 4
    inv_freq = ROPE_THETA ** (-jnp.arange(n_freq, dtype=jnp.float32) / n_freq)
    ang_r = row[:, None] * inv_freq
    ang_c = col[:, None] * inv_freq
    return tuple(t[None, :, None, :] for t in (jnp.cos(ang_r), jnp.sin(ang_r), jnp.cos(ang_c), jnp.sin(ang_c)))

def rotate_half(x, cos, sin):
    x1, x2 = jnp.split(x, 2, axis=-1)
    return jnp.concatenate([x1 * cos - x2 * sin, x2 * cos + x1 * sin], axis=-1)

def with_rope(x, rope_tabs):
    if rope_tabs is None:
        return x
    cr, sr, cc, sc = rope_tabs
    xr, xcol = jnp.split(x[..., MLA_NOPE:].astype(jnp.float32), 2, axis=-1)
    rot = jnp.concatenate([rotate_half(xr, cr, sr), rotate_half(xcol, cc, sc)], axis=-1)
    return jnp.concatenate([x[..., :MLA_NOPE], rot.astype(x.dtype)], axis=-1)

def mla_queries(p_q, q_a_norm, w_uq, q_norm, rope_tabs):
    B, T, _ = p_q.shape
    q = (rms_norm(p_q, q_a_norm) @ w_uq).reshape(B, T, MLA_HEADS, MLA_QK)
    return with_rope(rms_norm(q, q_norm), rope_tabs)

def mla_keys_values(p_kv, p_kr, kv_a_norm, w_ukv, k_norm, rope_tabs):
    B, T, _ = p_kv.shape
    kv = (rms_norm(p_kv, kv_a_norm) @ w_ukv).reshape(B, T, MLA_HEADS, MLA_NOPE + MLA_V)
    k_nope, v = kv[..., :MLA_NOPE], kv[..., MLA_NOPE:]
    k_rope = jnp.broadcast_to(p_kr[:, :, None, :], (B, T, MLA_HEADS, MLA_ROPE))
    k = rms_norm(jnp.concatenate([k_nope, k_rope], axis=-1), k_norm)
    return with_rope(k, rope_tabs), v

def softmax_attend(q, k, v):
    s = jnp.einsum('bqhd,bkhd->bhqk', q, k, preferred_element_type=jnp.float32) * (MLA_QK ** -0.5)
    p = jax.nn.softmax(s, axis=-1).astype(v.dtype)
    return jnp.einsum('bhqk,bkhd->bqhd', p, v)

def blocked_attend(q, k, v):
    B, T, H, d = q.shape
    nb = T // Q_BLOCK
    qb = jnp.moveaxis(q.reshape(B, nb, Q_BLOCK, H, d), 1, 0)
    out = lax.map(lambda qi: softmax_attend(qi, k, v), qb)
    return jnp.moveaxis(out, 0, 1).reshape(B, T, H, v.shape[-1])

def short_conv(u, w):
    pad = GDN_CONV // 2
    return lax.conv_general_dilated(u, w[:, None, :].astype(u.dtype), window_strides=(1,),
                                    padding=((pad, pad),), dimension_numbers=('NWC', 'WIO', 'NWC'),
                                    feature_group_count=u.shape[-1])

def gdn_inputs(pq, pk, pv, pa, pb, conv_w, a_log, dt_bias):
    B, T, _ = pq.shape
    qkv = jax.nn.silu(short_conv(jnp.concatenate([pq, pk, pv], axis=-1), conv_w))
    q, k, v = jnp.split(qkv, [GDN_HEADS * GDN_DK, 2 * GDN_HEADS * GDN_DK], axis=-1)
    q = l2_norm(q.reshape(B, T, GDN_HEADS, GDN_DK)) * (GDN_DK ** -0.5)
    k = l2_norm(k.reshape(B, T, GDN_HEADS, GDN_DK))
    v = v.reshape(B, T, GDN_HEADS, GDN_DV)
    pa = pa.reshape(B, T, 2, GDN_HEADS).astype(jnp.float32)
    pb = pb.reshape(B, T, 2, GDN_HEADS).astype(jnp.float32)
    g = -jnp.exp(a_log.astype(jnp.float32)) * jax.nn.softplus(pa + dt_bias.astype(jnp.float32))
    beta = jax.nn.sigmoid(pb)
    return q, k, v, g, beta

def gated_delta_chunked(q, k, v, g, beta, s0):
    B, T, H, _ = q.shape
    dv = v.shape[-1]
    C = GDN_CHUNK
    n = T // C
    f32 = jnp.float32

    def chunks(a):
        a = a.astype(f32).reshape((B, n, C, H) + a.shape[3:])
        return jnp.moveaxis(a, (1, 3), (0, 2))

    qc, kc, vc, bc = chunks(q), chunks(k), chunks(v), chunks(beta)
    gc = jnp.cumsum(chunks(g), axis=-1)
    idx = jnp.arange(C)
    incl = idx[:, None] >= idx[None, :]
    strict = idx[:, None] > idx[None, :]
    decay = jnp.exp(jnp.where(incl, gc[..., :, None] - gc[..., None, :], -jnp.inf))
    kb = kc * bc[..., None]
    a_low = jnp.where(strict, jnp.einsum('nbhcd,nbhsd->nbhcs', kb, kc) * decay, 0.0)
    tmat = a_low + jnp.eye(C, dtype=f32)
    w = lax.linalg.triangular_solve(tmat, kb * jnp.exp(gc)[..., None], left_side=True, lower=True, unit_diagonal=True)
    u = lax.linalg.triangular_solve(tmat, vc * bc[..., None], left_side=True, lower=True, unit_diagonal=True)
    qk = jnp.einsum('nbhcd,nbhsd->nbhcs', qc, kc) * decay
    qg = qc * jnp.exp(gc)[..., None]
    g_last = gc[..., -1]
    kd = kc * jnp.exp(g_last[..., None] - gc)[..., None]

    def step(s, inp):
        w_i, u_i, qk_i, qg_i, kd_i, gl_i = inp
        v_new = u_i - jnp.einsum('bhcd,bhde->bhce', w_i, s)
        o = jnp.einsum('bhcd,bhde->bhce', qg_i, s) + jnp.einsum('bhcs,bhse->bhce', qk_i, v_new)
        s = s * jnp.exp(gl_i)[..., None, None] + jnp.einsum('bhcd,bhce->bhde', kd_i, v_new)
        return s, o

    s_final, o = lax.scan(step, s0.astype(f32), (w, u, qk, qg, kd, g_last))
    o = jnp.moveaxis(o, (0, 2), (1, 3)).reshape(B, T, H, dv)
    return o.astype(v.dtype), s_final

def gdn_bidirectional(c_in, l_in):
    qc, kc, vc, gc, bc = c_in
    ql, kl, vl, gl, bl = l_in
    s0 = jnp.zeros((qc.shape[0], GDN_HEADS, GDN_DK, GDN_DV), jnp.float32)
    rev = lambda a: jnp.flip(a, axis=1)
    o_cf, s_cf = gated_delta_chunked(qc, kc, vc, gc[:, :, 0], bc[:, :, 0], s0)
    o_lf, _ = gated_delta_chunked(ql, kl, vl, gl[:, :, 0], bl[:, :, 0], s_cf)
    o_cb, s_cb = gated_delta_chunked(rev(qc), rev(kc), rev(vc), rev(gc[:, :, 1]), rev(bc[:, :, 1]), s0)
    o_lb, _ = gated_delta_chunked(rev(ql), rev(kl), rev(vl), rev(gl[:, :, 1]), rev(bl[:, :, 1]), s_cb)
    return o_cf + rev(o_cb), o_lf + rev(o_lb)

def gdn_output(o, z, norm_g):
    B, T = z.shape[:2]
    zh = z.reshape(B, T, GDN_HEADS, GDN_DV)
    return (rms_norm(o, norm_g) * jax.nn.silu(zh)).reshape(B, T, GDN_HEADS * GDN_DV)

def pool_mixer(u, pool_w, pool_scale):
    B, T, _ = u.shape
    uf = u.astype(jnp.float32)
    csum = jnp.concatenate([jnp.zeros((B, 1, POOL_WIDTH), jnp.float32), jnp.cumsum(uf, axis=1)], axis=1)
    t = jnp.arange(T)
    diffs = []
    for gi, win in enumerate(POOL_WINDOWS):
        lo = jnp.clip(t - win // 2, 0, T)
        hi = jnp.clip(t - win // 2 + win, 0, T)
        sl = slice(gi * POOL_GROUP, (gi + 1) * POOL_GROUP)
        mean = (csum[:, hi, sl] - csum[:, lo, sl]) / (hi - lo).astype(jnp.float32)[None, :, None]
        diffs.append(mean - uf[..., sl])
    d = jnp.stack(diffs, axis=2).astype(u.dtype)
    y = jnp.einsum('btgc,gcd->btgd', d, pool_w).reshape(B, T, POOL_WIDTH)
    return y * pool_scale

def expert_choice_ffn(h, w_router, w_gate, w_up, w_down):
    B, T, D = h.shape
    cap = EC_CAPACITY_FACTOR * T // N_EXPERTS
    aff = jax.nn.softmax(jnp.einsum('btd,de->bte', h, w_router, preferred_element_type=jnp.float32), axis=-1)
    gate, idx = lax.top_k(jnp.swapaxes(aff, 1, 2), cap)
    xs = jax.vmap(lambda hb, ib: hb[ib])(h, idx)
    hid = jax.nn.silu(jnp.einsum('becd,edf->becf', xs, w_gate)) * jnp.einsum('becd,edf->becf', xs, w_up)
    y = jnp.einsum('becf,efd->becd', hid, w_down) * gate.astype(h.dtype)[..., None]
    return jax.vmap(lambda yb, ib: jnp.zeros((T, D), h.dtype).at[ib.reshape(-1)].add(yb.reshape(-1, D)))(y, idx)

def mixer_sublayer(h_c, h_l, rope_tabs, need_ctx, w_in, q_a_norm, w_uq, kv_a_norm, w_ukv, q_norm, k_norm,
                   conv_w, a_log, dt_bias, gdn_norm_g, pool_w, pool_scale, w_out):
    B, T, _ = h_l.shape
    pc = split_cols(h_c @ w_in)
    pl = split_cols(h_l @ w_in)
    k_c, v_c = mla_keys_values(pc[1], pc[2], kv_a_norm, w_ukv, k_norm, None)
    k_l, v_l = mla_keys_values(pl[1], pl[2], kv_a_norm, w_ukv, k_norm, rope_tabs)
    q_l = mla_queries(pl[0], q_a_norm, w_uq, q_norm, rope_tabs)
    att_l = blocked_attend(q_l, jnp.concatenate([k_c, k_l], axis=1),
                           jnp.concatenate([v_c, v_l], axis=1)).reshape(B, T, MLA_HEADS * MLA_V)
    c_in = gdn_inputs(pc[3], pc[4], pc[5], pc[7], pc[8], conv_w, a_log, dt_bias)
    l_in = gdn_inputs(pl[3], pl[4], pl[5], pl[7], pl[8], conv_w, a_log, dt_bias)
    o_c, o_l = gdn_bidirectional(c_in, l_in)
    gdn_l = gdn_output(o_l, pl[6], gdn_norm_g)
    pool_l = pool_mixer(pl[9], pool_w, pool_scale)
    y_l = jnp.concatenate([att_l, gdn_l, pool_l], axis=-1) @ w_out
    if not need_ctx:
        return None, y_l
    q_c = mla_queries(pc[0], q_a_norm, w_uq, q_norm, None)
    att_c = softmax_attend(q_c, k_c, v_c).reshape(B, -1, MLA_HEADS * MLA_V)
    gdn_c = gdn_output(o_c, pc[6], gdn_norm_g)
    pool_c = pool_mixer(pc[9], pool_w, pool_scale)
    y_c = jnp.concatenate([att_c, gdn_c, pool_c], axis=-1) @ w_out
    return y_c, y_l

def setup_inputs(seed: int = 0) -> dict:
    key = jax.random.key(seed)
    keys = jax.random.split(key, 32)
    f32 = jnp.float32
    L, D = DEPTH, D_MODEL

    def nrm(i, shape, scale):
        return jax.random.normal(keys[i], shape, f32) * scale

    dt = jnp.exp(jax.random.uniform(keys[17], (L, 2, GDN_HEADS), f32, math.log(1e-3), math.log(1e-1)))
    return {
        'x': nrm(0, (BATCH, SEQ, D), 1.0),
        'c': nrm(1, (BATCH, D), 1.0),
        'ctx': nrm(2, (BATCH, CTX_LEN, D), 1.0),
        'c_ctx': nrm(3, (D,), 1.0),
        'ada_w': nrm(4, (L, D, ADA_CHUNKS * D), 0.5 * D ** -0.5),
        'ada_b': nrm(5, (L, ADA_CHUNKS * D), 0.02),
        'norm1_g': 1.0 + nrm(6, (L, D), 0.05),
        'norm2_g': 1.0 + nrm(7, (L, D), 0.05),
        'w_in': nrm(8, (L, D, IN_COLS), D ** -0.5),
        'mla_q_a_norm': 1.0 + nrm(9, (L, MLA_Q_LORA), 0.05),
        'mla_w_uq': nrm(10, (L, MLA_Q_LORA, MLA_HEADS * MLA_QK), MLA_Q_LORA ** -0.5),
        'mla_kv_a_norm': 1.0 + nrm(11, (L, MLA_KV_LORA), 0.05),
        'mla_w_ukv': nrm(12, (L, MLA_KV_LORA, MLA_HEADS * (MLA_NOPE + MLA_V)), MLA_KV_LORA ** -0.5),
        'mla_q_norm': 1.0 + nrm(13, (L, MLA_QK), 0.05),
        'mla_k_norm': 1.0 + nrm(14, (L, MLA_QK), 0.05),
        'gdn_conv_w': nrm(15, (L, GDN_CONV, 2 * GDN_HEADS * GDN_DK + GDN_HEADS * GDN_DV), GDN_CONV ** -0.5),
        'gdn_a_log': jnp.log(jax.random.uniform(keys[16], (L, 2, GDN_HEADS), f32, 1.0, 16.0)),
        'gdn_dt_bias': dt + jnp.log(-jnp.expm1(-dt)),
        'gdn_norm_g': 1.0 + nrm(18, (L, GDN_DV), 0.05),
        'pool_w': nrm(19, (L, len(POOL_WINDOWS), POOL_GROUP, POOL_GROUP), POOL_GROUP ** -0.5),
        'pool_scale': 1.0 + nrm(20, (L, POOL_WIDTH), 0.1),
        'w_out': nrm(21, (L, D_MIX, D), D_MIX ** -0.5),
        'moe_router': nrm(22, (L, D, N_EXPERTS), D ** -0.5),
        'moe_w_gate': nrm(23, (L, N_EXPERTS, D, D_EXPERT), D ** -0.5),
        'moe_w_up': nrm(24, (L, N_EXPERTS, D, D_EXPERT), D ** -0.5),
        'moe_w_down': nrm(25, (L, N_EXPERTS, D_EXPERT, D), D_EXPERT ** -0.5),
    }

def reference(x, c, ctx, c_ctx, ada_w, ada_b, norm1_g, norm2_g, w_in, mla_q_a_norm, mla_w_uq, mla_kv_a_norm,
              mla_w_ukv, mla_q_norm, mla_k_norm, gdn_conv_w, gdn_a_log, gdn_dt_bias, gdn_norm_g, pool_w,
              pool_scale, w_out, moe_router, moe_w_gate, moe_w_up, moe_w_down):
    rope_tabs = axial_rope_tables(x.shape[1])
    xc = ctx
    for l in range(DEPTH):
        need_ctx = l < DEPTH - 1
        m = jnp.split(jax.nn.silu(c) @ ada_w[l] + ada_b[l], ADA_CHUNKS, axis=-1)
        mc = jnp.split(jax.nn.silu(c_ctx) @ ada_w[l] + ada_b[l], ADA_CHUNKS, axis=-1)
        sh1, sc1, g1, sh2, sc2, g2 = [t[:, None, :] for t in m]
        csh1, csc1, cg1, csh2, csc2, cg2 = mc
        h_l = modulate(x, norm1_g[l], sh1, sc1)
        h_c = modulate(xc, norm1_g[l], csh1, csc1)
        y_c, y_l = mixer_sublayer(h_c, h_l, rope_tabs, need_ctx, w_in[l], mla_q_a_norm[l], mla_w_uq[l],
                                  mla_kv_a_norm[l], mla_w_ukv[l], mla_q_norm[l], mla_k_norm[l], gdn_conv_w[l],
                                  gdn_a_log[l], gdn_dt_bias[l], gdn_norm_g[l], pool_w[l], pool_scale[l], w_out[l])
        x = x + g1 * y_l
        x = x + g2 * expert_choice_ffn(modulate(x, norm2_g[l], sh2, sc2), moe_router[l], moe_w_gate[l],
                                       moe_w_up[l], moe_w_down[l])
        if need_ctx:
            xc = xc + cg1 * y_c
            xc = xc + cg2 * expert_choice_ffn(modulate(xc, norm2_g[l], csh2, csc2), moe_router[l],
                                              moe_w_gate[l], moe_w_up[l], moe_w_down[l])
    return x


_drawn_inputs = setup_inputs


def setup_inputs(seed=0):
    import zlib

    import numpy as np

    out = dict(_drawn_inputs(seed))
    spreads = {}
    factors = {'ctx': 2.984,
     'norm1_g': 2.871,
     'norm2_g': 3.517,
     'mla_q_a_norm': 8.0,
     'mla_w_uq': 2.737,
     'mla_kv_a_norm': 8.0,
     'mla_q_norm': 8.0,
     'mla_k_norm': 8.0,
     'gdn_norm_g': 4.983,
     'pool_scale': 2.793}
    for name, (base, spread) in spreads.items():
        noise = np.random.default_rng([zlib.crc32(name.encode()), seed]).standard_normal(out[name].shape)
        drawn = base * np.exp(spread * noise) if base else spread * noise
        out[name] = jnp.asarray(drawn.astype(out[name].dtype))
    for name, factor in factors.items():
        out[name] = (out[name] * factor).astype(out[name].dtype)
    return out
```

```python
from contextlib import ExitStack

import numpy as np

import concourse.bass as bass
from concourse import mybir

F32 = mybir.dt.float32
ALU = mybir.AluOpType
ACT = mybir.ActivationFunctionType
AX = mybir.AxisListType

P = 128
D = 1024
KD = D // P
CTX = 256
SEQ = 512
T = CTX + SEQ
NT = T // P
CT = CTX // P
DEPTH = 2
EPS = 1e-6
GRID_W = 64
ROPE_THETA = 10000.0

H = 4
NOPE, ROPE, DV = 64, 32, 64
QK = NOPE + ROPE
Q_LORA, KV_LORA = 192, 128
GH = 4
WINDOWS = (2, 4, 8, 16)
PG = 64
PAD = 8
N_EXP = 16
F_EXP = 512
FK = F_EXP // P
CAP_L = 2 * SEQ // N_EXP
CAP_C = 2 * CTX // N_EXP
CAP = CAP_L + CAP_C
PAIRS = N_EXP // 2
LEVELS = 7

SPLITS = (Q_LORA, KV_LORA, ROPE, 512, 512, 512, 512, 8, 8, 256)
OFF = [int(x) for x in np.cumsum((0,) + SPLITS)]
SLOTS = 6
PAR_DMAS = 21
CONST_DMAS = 8
SLOT_COLS = 256
BANKS = 8

SEGS = ((0, CTX), (CTX, SEQ))
COL_ADA, COL_N1, COL_N2, COL_CONV, COL_KV, COL_GN, COL_Q, COL_PS = 0, 48, 56, 64, 100, 101, 102, 104
N_COLS = 106
IN_LOADS = [("pool", OFF[9], OFF[10]), ("ab", OFF[7], OFF[9]), ("ql", OFF[0], OFF[1]), ("kvr", OFF[1], OFF[3])]
IN_LOADS += [("qkv%d" % j, OFF[3] + 256 * j, OFF[3] + 256 * (j + 1)) for j in range(6)]
IN_LOADS += [("z%d" % j, OFF[6] + 256 * j, OFF[6] + 256 * (j + 1)) for j in range(2)]


def shape_constants():
    s = np.arange(P)
    out = {"k_ident": np.eye(P, dtype=np.float32)}
    out["k_tri"] = np.stack([s[:, None] <= s[None, :], s[:, None] >= s[None, :]], 1).astype(np.float32)
    lev = np.zeros((P, 2, LEVELS, P), np.float32)
    for n in range(LEVELS):
        b = 1 << n
        same = (s[:, None] // (2 * b)) == (s[None, :] // (2 * b))
        low = (s // b) % 2 == 0
        lev[:, 0, n] = same & low[:, None] & ~low[None, :]
        lev[:, 1, n] = same & ~low[:, None] & low[None, :]
    out["k_lev"] = lev
    out["k_iota"] = np.tile(np.arange(CAP_L, dtype=np.float32), (P, 1))
    n = ROPE // 4
    inv = np.float32(ROPE_THETA) ** (-np.arange(n, dtype=np.float32) / np.float32(n))
    t = np.arange(SEQ)
    ar = (t // GRID_W).astype(np.float32)[:, None] * inv
    ac = (t % GRID_W).astype(np.float32)[:, None] * inv
    cos = np.concatenate([np.cos(ar), np.cos(ar), np.cos(ac), np.cos(ac)], 1)
    sin = np.concatenate([-np.sin(ar), np.sin(ar), -np.sin(ac), np.sin(ac)], 1)
    tab = np.stack([cos, sin], 1).astype(np.float32)
    out["k_rope"] = np.ascontiguousarray(tab.reshape(SEQ // P, P, 2, ROPE).transpose(1, 0, 2, 3))
    pool = np.zeros((P, 2, 17), np.float32)
    for g, w in enumerate(WINDOWS):
        rows, c = slice(64 * (g % 2), 64 * (g % 2) + 64), g // 2
        for j in range(8):
            pool[rows, c, j] = w / (w - max(0, w // 2 - j))
            pool[rows, c, 8 + j] = w / (w - max(0, w // 2 - (8 - j)))
        pool[rows, c, 16] = 1.0 / w
    out["k_pool"] = pool
    return out


def build_program(nc, A, out):
    ctx = ExitStack()
    with ctx:
        def sb(name, shape):
            return ctx.enter_context(nc.sbuf_tensor(name, shape, F32))

        def sem(name):
            return ctx.enter_context(nc.semaphore(name))

        xT = sb("xT", [P, KD, T])
        hT = sb("hT", [P, KD, T])
        ring = sb("ring", [P, SLOTS, KD * SLOT_COLS])
        big = sb("big", [P, 12 * T])
        sz = sb("sz", [P, 4 * T])
        dT = sb("dT", [P, 2, T])
        arena = sb("arena", [P, 12 * T])
        ident = sb("ident", [P, P])
        ones = sb("ones", [P, P])
        tri = sb("tri", [P, 2, P])
        lev = sb("lev", [P, 2, LEVELS, P])
        iota = sb("iota", [P, CAP_L])
        rope = sb("rope", [P, SEQ // P, 2, ROPE])
        poolc = sb("poolc", [P, 2, 17])
        pstage = sb("pstage", [P, P])
        cstage = arena[0:16, 11 * T:11 * T + P]
        cols = sb("cols", [P, N_COLS])
        scol = sb("scol", [P, 2, KD])
        mods = sb("mods", [P, 6 * KD, 2])
        amod = sb("amod", [P, 2, KD, 2])
        wuq = sb("wuq", [P, 2, H * QK])
        wukv = sb("wukv", [P, H * (NOPE + DV)])
        poolw = sb("poolw", [P, 2, P])
        router = sb("router", [P, KD, N_EXP])
        rown = sb("rown", [P, 2, QK])
        gpar = sb("gpar", [P, 2, 8])
        eps = sb("eps", [P, 2])
        small = sb("small", [P, 640])
        psum = ctx.enter_context(nc.psum_tensor("psum", [P, BANKS, 512], F32))

        mixT = hT

        def at(t, first, shape):
            n = int(np.prod(shape))
            v = t[:, first:first + n]
            if len(shape) == 2:
                return v.rearrange("p (a b) -> p a b", a=shape[0])
            if len(shape) == 3:
                return v.rearrange("p (a b c) -> p a b c", a=shape[0], b=shape[1])
            if len(shape) == 4:
                return v.rearrange("p (a b c d) -> p a b c d", a=shape[0], b=shape[1], c=shape[2])
            return v

        sqb = at(arena, 0, (2, T))
        rstd = at(arena, 2 * T, (T,))
        rs_gdn = at(arena, 2 * T, (2, T))
        UW = T + 4 * PAD
        U = at(big, 0, (2, UW))
        BA = at(big, 2 * UW, (UW,))
        BB = at(big, 3 * UW, (UW,))
        rows = at(big, 4 * UW, (2, H, QK))
        rtmp = at(big, 4 * UW + 2 * H * QK, (H, QK))
        rot1 = at(big, 4 * UW + 3 * H * QK, (H, ROPE))
        rot2 = at(big, 4 * UW + 3 * H * QK + H * ROPE, (H, 2, 2, ROPE // 4))
        assert 4 * UW + 3 * H * QK + 2 * H * ROPE <= 6 * T
        UO = (PAD, CTX + 3 * PAD)
        QG0 = at(big, 6 * T, (T,))
        QG1 = at(big, 7 * T, (T,))
        KVG = at(big, 8 * T, (T,))
        SQ0 = at(big, 9 * T, (T,))
        SQ1 = at(big, 10 * T, (T,))
        SQK = at(big, 11 * T, (T,))
        qkvT = at(big, 0, (12, T))
        KT = at(arena, 0, (H, T))
        QT = at(arena, 4 * T, (H, T))
        V = at(arena, 8 * T, (NT, H * DV))
        PR = at(arena, 10 * T, (T,))
        PT = at(arena, 11 * T, (NT, P))
        att = dT[:, 0, 0:H * DV]
        G1 = GH * P
        GW = 8 * G1
        dir_at = [d * GW for d in range(2)]
        gAT = [at(arena, o, (GH, P)) for o in dir_at]
        gML = [at(arena, o + G1, (GH, P)) for o in dir_at]
        gX = [at(arena, o + 2 * G1, (GH, 2, P)) for o in dir_at]
        gD = [at(arena, o + 2 * G1, (GH, P)) for o in dir_at]
        gY = [at(arena, o + 4 * G1, (GH, P)) for o in dir_at]
        gQK = [at(arena, o + 5 * G1, (GH, P)) for o in dir_at]
        gKD = [at(arena, o + 6 * G1, (GH, P)) for o in dir_at]
        gQG = [at(arena, o + 7 * G1, (GH, P)) for o in dir_at]
        S = at(arena, 2 * GW, (2, GH, P))
        szT = at(sz, 0, (4, T))
        hrow = at(big, 0, (NT, D))
        Gl = at(big, NT * D, (CT + 2, 2, CAP_L))
        Gc = at(big, NT * D + 512, (CT, 2, CAP_C))
        GGl = at(big, NT * D + 640, (CT + 2, 2, CAP_L))
        GGc = at(big, NT * D + 1152, (CT, 2, CAP_C))
        Sl = at(big, NT * D + 1280, (SEQ,))
        Sc = at(big, NT * D + 1792, (CTX,))
        affT = at(sz, 0, (T,))
        tkw = at(sz, T, (T,))
        sel = at(sz, 2 * T, (T,))
        csum = at(sz, 3 * T, (T,))
        xs = at(arena, 0, (KD, 2, CAP))
        hid = at(arena, 1536, (FK, CAP))
        sg = at(arena, 1920, (2, 2, CAP))
        ylat = at(arena, 2304, (D,))
        yctx = at(arena, 2304 + D, (D,))
        gb = small[:, 0:96].rearrange("p (w i c) -> p w i c", w=2, i=NT)
        gc = small[:, 96:144].rearrange("p (d i h) -> p d i h", d=2, i=NT)
        bg = small[:, 144:192].rearrange("p (d i h) -> p d i h", d=2, i=NT)
        krp = small[:, 436:628].rearrange("p (i c) -> p i c", i=NT)
        rs12 = small[:, 384:396].rearrange("p (i w) -> p i w", w=2)
        ss4 = small[:, 396:404].rearrange("p (n h) -> p n h", n=2)
        mx = small[:, 404:408].rearrange("p (n w) -> p n w", n=2)
        nm = small[:, 408:410]
        sm = small[:, 352:368].rearrange("p (n h w) -> p n h w", n=2, w=2)
        rden = small[:, 416:420]
        gt4 = small[:, 420:436].rearrange("p (d w h) -> p d w h", d=2, w=2)
        aff = small[:, 436:532].rearrange("p (i e) -> p i e", i=NT)
        slotc = small[:, 532:628].rearrange("p (i e) -> p i e", i=NT)
        rt6 = small[:, 628:634]
        abw = small[:, 192:288].rearrange("p (w i c) -> p w i c", w=2, i=NT)
        ealog = small[:, 288:296]
        abe = small[:, 296:344].rearrange("p (i c) -> p i c", i=NT)
        top8 = sb("top8", [16, 8])
        tkn = sb("tkn", [16, 4])

        slot_full = [sem("slot_full%d" % i) for i in range(SLOTS)]
        slot_used = sem("slot_used")
        bank_full = [sem("bank_full%d" % i) for i in range(BANKS)]
        bank_free = [sem("bank_free%d" % i) for i in range(BANKS)]
        s_const = sem("s_const")
        s_ones = sem("s_ones")
        s_xin = sem("s_xin")
        s_out = sem("s_out")
        s_outrow = sem("s_outrow")
        NAMES = ["zero", "par", "mods", "sq1", "sqd1", "hx1", "h1", "sq2", "sqd2", "hx2", "h2", "upad", "pool", "sqm",
                 "abraw", "abexp", "abln", "gbd", "row1", "rowr", "rowa", "row2", "nm", "pv", "cv1", "qkv", "lsq",
                 "lmul", "egc", "bg", "tg", "xg", "dcl", "dex", "dm", "x1", "ml", "qg", "osq", "mixd", "rmax",
                 "rexp", "aff", "sel", "G", "dve", "pool_e"]
        sems = [dict((n, sem("%s_%d" % (n, l))) for n in NAMES) for l in range(DEPTH)]

        freed_by = []
        freed = [0]
        where = {}
        uses = [0] * BANKS
        turn = [0]
        loads = []

        def plus(base, per, i):
            return base if i is None else i * per + base

        def product_ready(eng, key, i=None):
            b, n, per = where[key]
            eng.wait_ge(bank_full[b], plus(n + 1, per, i))
            return psum[:, b, :]

        def read_out(ins, key):
            ins.then_inc(bank_free[where[key][0]], 1)

        def evacuated(eng, key, i=None):
            b, n, per = where[key]
            eng.wait_ge(bank_free[b], plus(n + 1, per, i))

        def attended(eng, l, calls, n):
            i, h = calls[n]
            if h == H - 1:
                product_ready(eng, ("o", l, i))
            else:
                eng.wait_ge(sems[l]["pv"], n - n // H)

        def tile_of(d, j):
            return j if d == 0 else (CT - 1 - j if j < CT else NT + CT - 1 - j)

        block = ctx.enter_context(nc.Block())

        @block.tensor
        def _(pe):
            held = []

            def claim(key):
                while turn[0] % BANKS in held:
                    turn[0] += 1
                b = turn[0] % BANKS
                turn[0] += 1
                if uses[b]:
                    pe.wait_ge(bank_free[b], uses[b])
                where[key] = (b, uses[b], 0)
                uses[b] += 1
                return psum[:, b, :]

            def done(ins, key):
                ins.then_inc(bank_full[where[key][0]], 1)

            def last_use(ins, key=None):
                if key is None:
                    freed[0] += 1
                    ins.then_inc(slot_used, 1)
                    freed_by.append(freed[0])
                else:
                    freed_by.append((key, None))

            def weights(name):
                n = len(loads)
                loads.append(name)
                pe.wait_ge(slot_full[n % SLOTS], 16 * (n // SLOTS + 1))
                return ring[:, n % SLOTS, :].rearrange("p (k c) -> p k c", k=KD)

            def sum_over_partitions(l, which, sqs, sqd):
                s = sems[l]
                lat = claim(("ss", l, which, 1))
                need = which == 1 or l == 0
                con = claim(("ss", l, which, 0)) if need else None
                for k in range(KD):
                    pe.wait_ge(s[sqs], k + 1)
                    m = pe.matmul(lat, lhsT=ones[:, :], rhs=sqb[:, k % 2, CTX:T], start=k == 0, stop=k == KD - 1)
                    if k == KD - 1:
                        done(m, ("ss", l, which, 1))
                    if need:
                        m = pe.matmul(con[:, 0:CTX], lhsT=ones[:, :], rhs=sqb[:, k % 2, 0:CTX], start=k == 0,
                                      stop=k == KD - 1)
                        if k == KD - 1:
                            done(m, ("ss", l, which, 0))
                    if k < KD - 1:
                        m.then_inc(s[sqd], 1)

            pe.wait_ge(s_const, 16 * CONST_DMAS)
            pe.wait_ge(s_ones, 1)
            pe.wait_ge(s_xin, 16 * 2)
            xin = at(big, 0, (NT, D))
            for k in range(KD):
                for half, tiles in enumerate((range(0, 4), range(4, 6))):
                    key = ("x", k, half)
                    b = claim(key)
                    for j, i in enumerate(tiles):
                        m = pe.transpose(b[:, j * P:(j + 1) * P], xin[:, i, k * P:(k + 1) * P], ident[:, :])
                    done(m, key)

            for l in range(DEPTH):
                s = sems[l]
                need_ctx = l < DEPTH - 1
                tiles = range(NT) if need_ctx else range(CT, NT)
                segs = (0, 1) if need_ctx else (1,)

                pe.wait_ge(s["par"], 16 * PAR_DMAS)
                b = claim(("cols", l))
                done(pe.transpose(b[:, 0:N_COLS], pstage[0:N_COLS, :], ident[0:N_COLS, 0:N_COLS]), ("cols", l))
                if l == 0:
                    b = claim("c")
                    done(pe.transpose(b[:, 0:16], cstage, ident[0:16, 0:16]), "c")
                    evacuated(pe, "c")
                b = claim(("ada", l))
                for g in range(6 * D // SLOT_COLS):
                    w = weights(("ada", l, g))
                    for j in range(2):
                        m2 = 2 * (2 * g + j)
                        for k in range(KD):
                            m = pe.matmul(b[:, m2:m2 + 2], lhsT=w[:, k, j * P:(j + 1) * P], rhs=scol[:, :, k],
                                          start=k == 0, stop=k == KD - 1)
                    if g < 6 * D // SLOT_COLS - 1:
                        last_use(m)
                    else:
                        done(m, ("ada", l))
                        last_use(m, ("ada", l))

                sum_over_partitions(l, 1, "sq1", "sqd1")

                def chunk(key, w, c0, c1, which):
                    bs = [(g, claim(key + (g,))) for g in which]
                    for k in range(KD):
                        if key[2] == "pool0":
                            pe.wait_ge(s["h1"], k + 1)
                        for g, b in bs:
                            t0, n = SEGS[g]
                            m = pe.matmul(b[0:c1 - c0, 0:n], lhsT=w[:, k, c0:c1], rhs=hT[:, k, t0:t0 + n],
                                          start=k == 0, stop=k == KD - 1)
                            if k == KD - 1:
                                done(m, key + (g,))

                def token_rows(key, w, c0, c1):
                    b = claim(key)
                    n = c1 - c0
                    for i in range(NT):
                        for k in range(KD):
                            m = pe.matmul(b[:, i * n:(i + 1) * n], lhsT=hT[:, k, i * P:(i + 1) * P],
                                          rhs=w[:, k, c0:c1], start=k == 0, stop=k == KD - 1)
                    done(m, key)

                w = weights(("in", l, 0))
                chunk(("in", l, "pool0"), w, 0, P, segs)
                chunk(("in", l, "pool1"), w, P, 2 * P, segs)
                last_use(None, ("in", l, "pool1", 1))
                w = weights(("in", l, 1))
                token_rows(("ab", l), w, 0, 16)
                last_use(None, ("ab", l))
                w = weights(("in", l, 2))
                chunk(("in", l, "ql0"), w, 0, P, segs)
                chunk(("in", l, "ql1"), w, P, Q_LORA, segs)
                last_use(None, ("in", l, "ql1", 1))
                w = weights(("in", l, 3))
                chunk(("in", l, "kv"), w, 0, KV_LORA, (0, 1))
                token_rows(("krp", l), w, KV_LORA, KV_LORA + ROPE)
                last_use(None, ("krp", l))

                b = claim(("rs", l))
                for g in (0, 1):
                    evacuated(pe, ("in", l, "kv", g))
                for g in segs:
                    evacuated(pe, ("in", l, "ql1", g))
                    evacuated(pe, ("in", l, "ql0", g))
                for i in range(NT):
                    t = slice(i * P, (i + 1) * P)
                    if i in tiles:
                        pe.matmul(b[:, 2 * i:2 * i + 1], lhsT=SQ0[:, t], rhs=ones[:, 0:1], start=True, stop=False)
                        pe.matmul(b[:, 2 * i:2 * i + 1], lhsT=SQ1[0:64, t], rhs=ones[0:64, 0:1], start=False,
                                  stop=True)
                    m = pe.matmul(b[:, 2 * i + 1:2 * i + 2], lhsT=SQK[:, t], rhs=ones[:, 0:1], start=True, stop=True)
                done(m, ("rs", l))
                jobs = [("k", i) for i in range(NT)] + [("q", i) for i in tiles]

                def project(n):
                    kind, i = jobs[n]
                    t = slice(i * P, (i + 1) * P)
                    key = (kind, l, i)
                    b = claim(key)
                    if kind == "k":
                        m = pe.matmul(b[:, 0:512], lhsT=KVG[:, t], rhs=wukv[:, :], start=True, stop=True)
                    else:
                        pe.matmul(b[:, 0:H * QK], lhsT=QG0[:, t], rhs=wuq[:, 0, :], start=True, stop=False)
                        m = pe.matmul(b[:, 0:H * QK], lhsT=QG1[0:64, t], rhs=wuq[0:64, 1, :], start=False, stop=True)
                    done(m, key)

                def turn_rows(n):
                    kind, i = jobs[n]
                    key = (kind + "t", l, i)
                    b = claim(key)
                    pe.wait_ge(s["row2"], n + 1)
                    for h in range(H):
                        m = pe.transpose(b[0:QK, h * P:(h + 1) * P], rows[:, n % 2, h, :], ident[:, :])
                    done(m, key)

                project(0)
                project(1)
                for n in range(len(jobs)):
                    if n + 2 < len(jobs):
                        project(n + 2)
                    turn_rows(n)

                for j in range(6):
                    w = weights(("in", l, 4 + j))
                    for c in range(2):
                        chunk(("in", l, "qkv%d" % (2 * j + c)), w, c * P, (c + 1) * P, (0, 1))
                    last_use(None, ("in", l, "qkv%d" % (2 * j + 1), 1))
                for j in range(2):
                    w = weights(("in", l, 10 + j))
                    for c in range(2):
                        chunk(("in", l, "z%d" % (2 * j + c)), w, c * P, (c + 1) * P, segs)
                    last_use(None, ("in", l, "z%d" % (2 * j + 1), 1))

                for c in range(2):
                    for g in segs:
                        key = ("pm", l, c, g)
                        b = claim(key)
                        pe.wait_ge(s["pool"], c + 1)
                        t0, n = SEGS[g]
                        done(pe.matmul(b[:, 0:n], lhsT=poolw[:, c, :], rhs=dT[:, c, t0:t0 + n], start=True,
                                       stop=True), key)

                calls = [(i, h) for i in tiles for h in range(H)]

                def keys_of(i):
                    return (CT,) if i < CT else (4, 2)

                def scores(i, h):
                    k0 = 0
                    for part, nk in enumerate(keys_of(i)):
                        key = ("s", l, i, h, part)
                        b = claim(key)
                        done(pe.matmul(b[:, 0:nk * P], lhsT=QT[0:QK, h, i * P:(i + 1) * P],
                                       rhs=KT[0:QK, h, k0:k0 + nk * P], start=True, stop=True), key)
                        k0 += nk * P

                evacuated(pe, (jobs[-1][0] + "t", l, jobs[-1][1]))
                evacuated(pe, (jobs[-2][0] + "t", l, jobs[-2][1]))
                scores(*calls[0])
                obank = None
                for n, (i, h) in enumerate(calls):
                    if h == 0:
                        obank = claim(("o", l, i))
                        held.append(where[("o", l, i)][0])
                    if n + 1 < len(calls):
                        scores(*calls[n + 1])
                    for part in range(len(keys_of(i))):
                        evacuated(pe, ("s", l, i, h, part))
                    k0 = 0
                    for part, nk in enumerate(keys_of(i)):
                        key = ("pt", l, i, h, part)
                        b = claim(key)
                        for j in range(nk):
                            m = pe.transpose(b[:, j * P:(j + 1) * P], PR[:, (k0 + j) * P:(k0 + j + 1) * P],
                                             ident[:, :])
                        done(m, key)
                        k0 += nk
                    for part in range(len(keys_of(i))):
                        evacuated(pe, ("pt", l, i, h, part))
                    for j in range(k0):
                        m = pe.matmul(obank[:, h * DV:(h + 1) * DV], lhsT=PT[:, j, :],
                                      rhs=V[:, j, h * DV:(h + 1) * DV], start=j == 0, stop=j == k0 - 1)
                    if h < H - 1:
                        m.then_inc(s["pv"], 1)
                    else:
                        done(m, ("o", l, i))
                        held.pop()
                        key = ("at", l, i)
                        b = claim(key)
                        evacuated(pe, ("o", l, i))
                        for c in range(2):
                            m = pe.transpose(b[:, c * P:(c + 1) * P], att[:, c * P:(c + 1) * P], ident[:, :])
                        done(m, key)

                for c in range(2 * GH):
                    pe.wait_ge(s["lsq"], c + 1)
                    for g in (0, 1):
                        t0, n = SEGS[g]
                        key = ("ln", l, c, g)
                        b = claim(key)
                        done(pe.matmul(b[:, 0:n], lhsT=ones[:, :], rhs=sqb[:, c % 2, t0:t0 + n], start=True,
                                       stop=True), key)

                b = claim(("gc", l))
                pe.wait_ge(s["gbd"], 1)
                for d in range(2):
                    for i in range(NT):
                        c0 = (d * NT + i) * GH
                        m = pe.matmul(b[:, c0:c0 + GH], lhsT=tri[:, d, :], rhs=gb[:, 0, i, d * GH:(d + 1) * GH],
                                      start=True, stop=True)
                done(m, ("gc", l))
                pe.wait_ge(s["lmul"], 2 * GH)
                pe.wait_ge(s["qkv"], 24)

                def heads(key, f, wait=None):
                    b = claim(key)
                    for h in range(GH):
                        m = f(b[:, h * P:(h + 1) * P], h)
                    done(m, key)

                for j in range(NT):
                    ti = [tile_of(d, j) for d in range(2)]
                    tt = [slice(i * P, (i + 1) * P) for i in ti]
                    use_o = [need_ctx or i >= CT for i in ti]
                    for d in range(2):
                        key = ("g", l, j, d)
                        b = claim(key)
                        pe.wait_ge(s["tg"], 2 * j + d + 1)
                        done(pe.matmul(b, lhsT=ones[:, :], rhs=gML[d].rearrange("p h c -> p (h c)"), start=True,
                                       stop=True), key)
                    for d in range(2):
                        heads(("kk", l, j, d), lambda o, h: pe.matmul(
                            o, lhsT=qkvT[:, GH + h, tt[d]], rhs=qkvT[:, GH + h, tt[d]], start=True, stop=True))
                        if use_o[d]:
                            heads(("qk", l, j, d), lambda o, h: pe.matmul(
                                o, lhsT=qkvT[:, GH + h, tt[d]], rhs=qkvT[:, h, tt[d]], start=True, stop=True))
                    for d in range(2):
                        evacuated(pe, ("kk", l, j, d))
                        heads(("at2", l, j, d), lambda o, h: pe.transpose(o, gY[d][:, h, :], ident[:, :]))
                    for n in range(1, LEVELS):
                        for d in range(2):
                            if n == 1:
                                pe.wait_ge(s["x1"], 2 * j + d + 1)
                            else:
                                for q in range(2):
                                    evacuated(pe, ("xx", l, j, d, n - 1, q))
                            pe.wait_ge(s["ml"], 2 * (j * (LEVELS - 1) + n - 1) + d + 1)
                            heads(("y", l, j, d, n), lambda o, h: pe.matmul(
                                o, lhsT=gML[d][:, h, :], rhs=gX[d][:, h, 0, :], start=True, stop=True))
                        for d in range(2):
                            evacuated(pe, ("y", l, j, d, n))
                            for q in range(2):
                                key = ("xx", l, j, d, n, q)
                                b = claim(key)
                                for e in range(2):
                                    h = 2 * q + e
                                    if n < LEVELS - 1:
                                        pe.matmul(b[:, 2 * e * P:(2 * e + 1) * P], lhsT=gX[d][:, h, 1, :],
                                                  rhs=gY[d][:, h, :], start=True, stop=True)
                                    m = pe.matmul(b[:, (2 * e + 1) * P:(2 * e + 2) * P], lhsT=gY[d][:, h, :],
                                                  rhs=gX[d][:, h, 1, :], start=True, stop=True)
                                done(m, key)
                    for d in range(2):
                        heads(("kr", l, j, d), lambda o, h: pe.transpose(o, qkvT[:, GH + h, tt[d]], ident[:, :]))
                        heads(("vr", l, j, d), lambda o, h: pe.transpose(o, qkvT[:, 2 * GH + h, tt[d]], ident[:, :]))
                    for d in range(2):
                        evacuated(pe, ("kr", l, j, d))
                        for q in range(2):
                            evacuated(pe, ("xx", l, j, d, LEVELS - 1, q))
                        heads(("wt", l, j, d), lambda o, h: pe.matmul(
                            o, lhsT=gAT[d][:, h, :], rhs=gX[d][:, h, 1, :], start=True, stop=True))
                    for d in range(2):
                        evacuated(pe, ("wt", l, j, d))
                        evacuated(pe, ("vr", l, j, d))
                        if j:
                            evacuated(pe, ("st", l, j - 1, d))
                        key = ("v", l, j, d)
                        b = claim(key)
                        for h in range(GH):
                            o = b[:, h * P:(h + 1) * P]
                            m = pe.matmul(o, lhsT=gX[d][:, h, 1, :], rhs=gY[d][:, h, :], start=True, stop=j == 0)
                            if j:
                                m = pe.matmul(o, lhsT=gML[d][:, h, :], rhs=S[:, d, h, :], start=False, stop=True)
                        done(m, key)
                    for d in range(2):
                        evacuated(pe, ("v", l, j, d))
                        if use_o[d]:
                            key = ("go", l, j, d)
                            b = claim(key)
                            if j:
                                pe.wait_ge(s["qg"], 2 * j + d + 1)
                            evacuated(pe, ("qk", l, j, d))
                            for h in range(GH):
                                o = b[:, h * P:(h + 1) * P]
                                if j:
                                    pe.matmul(o, lhsT=S[:, d, h, :], rhs=gQG[d][:, h, :], start=True, stop=False)
                                m = pe.matmul(o, lhsT=gY[d][:, h, :], rhs=gQK[d][:, h, :], start=j == 0, stop=True)
                            done(m, key)
                        if j < NT - 1:
                            heads(("st", l, j, d), lambda o, h: pe.matmul(
                                o, lhsT=gKD[d][:, h, :], rhs=gY[d][:, h, :], start=True, stop=True))

                for h in range(GH):
                    pe.wait_ge(s["osq"], h + 1)
                    for g in segs:
                        t0, n = SEGS[g]
                        key = ("on", l, h, g)
                        b = claim(key)
                        done(pe.matmul(b[:, 0:n], lhsT=ones[:, :], rhs=sqb[:, h % 2, t0:t0 + n], start=True,
                                       stop=True), key)

                for c in range(2):
                    for g in segs:
                        evacuated(pe, ("pm", l, c, g))
                evacuated(pe, ("at", l, NT - 1))
                pe.wait_ge(s["mixd"], GH)
                for j in range(4):
                    w = weights(("out", l, j))
                    for c in range(2):
                        for g in segs:
                            t0, n = SEGS[g]
                            key = ("y", l, 2 * j + c, g)
                            b = claim(key)
                            for k in range(KD):
                                m = pe.matmul(b[:, 0:n], lhsT=w[:, k, c * P:(c + 1) * P], rhs=mixT[:, k, t0:t0 + n],
                                              start=k == 0, stop=k == KD - 1)
                            done(m, key)
                    last_use(None, ("y", l, 2 * j + 1, 1))

                sum_over_partitions(l, 2, "sq2", "sqd2")

                b = claim(("rt", l))
                pe.wait_ge(s["h2"], KD)
                for i in tiles:
                    for k in range(KD):
                        m = pe.matmul(b[:, i * N_EXP:(i + 1) * N_EXP], lhsT=hT[:, k, i * P:(i + 1) * P],
                                      rhs=router[:, k, :], start=k == 0, stop=k == KD - 1)
                done(m, ("rt", l))
                for i in tiles:
                    for q in range(2):
                        key = ("hr", l, i, q)
                        b = claim(key)
                        for j in range(4):
                            m = pe.transpose(b[:, j * P:(j + 1) * P], hT[:, 4 * q + j, i * P:(i + 1) * P],
                                             ident[:, :])
                        done(m, key)
                pe.wait_ge(s["aff"], 1)
                for g in segs:
                    key = ("aT", l, g)
                    b = claim(key)
                    t0, n = SEGS[g]
                    for i in range(n // P):
                        m = pe.transpose(b[0:N_EXP, i * P:(i + 1) * P], aff[:, t0 // P + i, :], ident[:, :])
                    done(m, key)
                pe.wait_ge(s["sel"], len(segs))
                key = ("slot", l)
                b = claim(key)
                for i in tiles:
                    m = pe.transpose(b[:, i * N_EXP:(i + 1) * N_EXP], sel[0:N_EXP, i * P:(i + 1) * P],
                                     ident[0:N_EXP, 0:N_EXP])
                done(m, key)

                names, per = [], []
                seq = ["x%d" % q for q in range(4)] + ["sl"] + (["sc"] if need_ctx else [])
                for e in range(2):
                    seq += ["%s%d%d" % (t, e, q) for q in range(2) for t in ("g", "u")] + ["y%d0" % e, "y%d1" % e]
                seq += ["c%d%d" % (k, g) for k in range(KD) for g in reversed(segs)]
                per = [0] * BANKS
                for n in range(len(seq)):
                    per[(turn[0] + n) % BANKS] += 1
                t_at = turn[0]
                seen = [0] * BANKS
                for n, name in enumerate(seq):
                    b = (t_at + n) % BANKS
                    where[("moe", l, name)] = (b, uses[b] + seen[b], per[b])
                    seen[b] += 1
                r0 = len(loads)
                for q in range(2):
                    evacuated(pe, ("hr", l, NT - 1, q))
                evacuated(pe, ("slot", l))

                with pe.Fori(0, PAIRS) as i:
                    def claim2(name):
                        b, n, per = where[("moe", l, name)]
                        pe.wait_ge(bank_free[b], i * per + n)
                        return psum[:, b, :]

                    def done2(ins, name):
                        ins.then_inc(bank_full[where[("moe", l, name)][0]], 1)

                    def weights2(n, k):
                        m = r0 + n
                        pe.wait_ge(slot_full[m % SLOTS], i * (16 * 12 // SLOTS) + 16 * (m // SLOTS + 1))
                        return ring[:, m % SLOTS, :].rearrange("p (k c) -> p k c", k=k)

                    for q in range(4):
                        b = claim2("x%d" % q)
                        if q == 0:
                            pe.wait_ge(s["G"], 2 * i + 1)
                        for e in range(2):
                            k = 2 * q + e
                            o = b[:, e * 2 * CAP:(e + 1) * 2 * CAP]
                            for t in range(SEQ // P):
                                m = pe.matmul(o[:, 0:2 * CAP_L], lhsT=hrow[:, CT + t, k * P:(k + 1) * P],
                                              rhs=Gl[:, t, :, :].rearrange("p e c -> p (e c)"), start=t == 0,
                                              stop=t == SEQ // P - 1)
                            if need_ctx:
                                for t in range(CT):
                                    m = pe.matmul(o[:, 2 * CAP_L:2 * CAP], lhsT=hrow[:, t, k * P:(k + 1) * P],
                                                  rhs=Gc[:, t, :, :].rearrange("p e c -> p (e c)"), start=t == 0,
                                                  stop=t == CT - 1)
                        done2(m, "x%d" % q)
                    b = claim2("sl")
                    bc = claim2("sc") if need_ctx else None
                    pe.wait_ge(s["G"], 2 * i + 2)
                    for t in range(SEQ // P):
                        m = pe.transpose(b[:, t * P:(t + 1) * P], GGl[:, t, :, :].rearrange("p e c -> p (e c)"),
                                         ident[:, :])
                    done2(m, "sl")
                    if need_ctx:
                        for t in range(CT):
                            m = pe.transpose(bc[0:2 * CAP_C, t * P:(t + 1) * P],
                                             GGc[:, t, :, :].rearrange("p e c -> p (e c)"), ident[:, :])
                        done2(m, "sc")
                    n_cap = CAP if need_ctx else CAP_L
                    for e in range(2):
                        for q in range(2):
                            for t, name in enumerate("gu"):
                                w = weights2(6 * e + 2 * q + t, KD)
                                b = claim2("%s%d%d" % (name, e, q))
                                if e == 0 and q == 0 and t == 0:
                                    for x in range(4):
                                        evacuated(pe, ("moe", l, "x%d" % x), i)
                                for f in range(2):
                                    for k in range(KD):
                                        m = pe.matmul(b[:, f * CAP:f * CAP + n_cap], lhsT=w[:, k, f * P:(f + 1) * P],
                                                      rhs=xs[:, k, e, 0:n_cap], start=k == 0, stop=k == KD - 1)
                                done2(m, "%s%d%d" % (name, e, q))
                        ys = [claim2("y%d%d" % (e, c)) for c in range(2)]
                        for q in range(2):
                            w = weights2(6 * e + 4 + q, 2)
                            evacuated(pe, ("moe", l, "u%d%d" % (e, q)), i)
                            for f in range(2):
                                for c in range(2):
                                    m = pe.matmul(ys[c][0:n_cap, :], lhsT=hid[:, 2 * q + f, 0:n_cap],
                                                  rhs=w[:, f, c * 512:(c + 1) * 512], start=q == 0 and f == 0,
                                                  stop=q == 1 and f == 1)
                                    if q == 1 and f == 1:
                                        done2(m, "y%d%d" % (e, c))
                            if q == 0:
                                m.then_inc(slot_used, 1)
                    evacuated(pe, ("moe", l, "sl"), i)
                    if need_ctx:
                        evacuated(pe, ("moe", l, "sc"), i)
                    for e in range(2):
                        for c in range(2):
                            evacuated(pe, ("moe", l, "y%d%d" % (e, c)), i)
                    for k in range(KD):
                        for g in reversed(segs):
                            name = "c%d%d" % (k, g)
                            b = claim2(name)
                            if g:
                                m = pe.matmul(b[:, 0:SEQ], lhsT=ylat[:, k * P:(k + 1) * P], rhs=Sl[:, :], start=True,
                                              stop=True)
                            else:
                                m = pe.matmul(b[:, 0:CTX], lhsT=yctx[0:2 * CAP_C, k * P:(k + 1) * P],
                                              rhs=Sc[0:2 * CAP_C, :], start=True, stop=True)
                            done2(m, name)
                for b in range(BANKS):
                    uses[b] += PAIRS * per[b]
                for i in range(PAIRS):
                    for e in range(2):
                        for q in range(2):
                            for t, name in enumerate("gu"):
                                loads.append((("gate", "up")[t], l, 2 * i + e, q))
                                freed_by.append((("moe", l, "%s%d%d" % (name, e, q)), i))
                        loads.append(("down", l, 2 * i + e, 0))
                        freed[0] += 1
                        freed_by.append(freed[0])
                        loads.append(("down", l, 2 * i + e, 1))
                        freed_by.append((("moe", l, "y%d1" % e), i))

            evacuated(pe, ("moe", DEPTH - 1, "c%d1" % (KD - 1)), PAIRS - 1)
            for i in range(CT, NT):
                for q in range(2):
                    key = ("out", i, q)
                    b = claim(key)
                    for j in range(4):
                        m = pe.transpose(b[:, j * P:(j + 1) * P], xT[:, 4 * q + j, i * P:(i + 1) * P], ident[:, :])
                    done(m, key)

        @block.sync
        def _(sp):
            sp.dma_start(big[:, 0:CT * D].rearrange("p (i d) -> p i d", i=CT),
                         A["ctx"][0].rearrange("(i p) d -> p i d", p=P)).then_inc(s_xin, 16)
            sp.dma_start(big[:, CT * D:NT * D].rearrange("p (i d) -> p i d", i=NT - CT),
                         A["x"][0].rearrange("(i p) d -> p i d", p=P)).then_inc(s_xin, 16)

            def slot(n, k, c):
                return ring[:, n % SLOTS, :].rearrange("p (k c) -> p k c", k=k)[:, :, 0:c]

            def slot_free(n):
                if n >= SLOTS:
                    how = freed_by[n - SLOTS]
                    if isinstance(how, int):
                        sp.wait_ge(slot_used, how)
                    else:
                        product_ready(sp, how[0], how[1])

            def columns(n, src, c0, c1):
                slot_free(n)
                sp.dma_start(slot(n, KD, c1 - c0), src.rearrange("(k p) c -> p k c", p=P)[:, :, c0:c1]
                             ).then_inc(slot_full[n % SLOTS], 16)

            def expert(n, l, e, m):
                if m < 4:
                    w = A["moe_w_gate"] if m % 2 == 0 else A["moe_w_up"]
                    c0 = (m // 2) * SLOT_COLS
                    src = w[l, e].rearrange("(k p) f -> p k f", p=P)[:, :, c0:c0 + SLOT_COLS]
                    dst = slot(n, KD, SLOT_COLS)
                else:
                    src = A["moe_w_down"][l, e].rearrange("(k p) d -> p k d", p=P)[:, 2 * (m - 4):2 * (m - 4) + 2, :]
                    dst = slot(n, 2, D)
                sp.dma_start(dst, src).then_inc(slot_full[n % SLOTS], 16)

            n = 0
            for l in range(DEPTH):
                for g in range(6 * D // SLOT_COLS):
                    columns(n, A["ada_w"][l], g * SLOT_COLS, (g + 1) * SLOT_COLS)
                    n += 1
                for _, c0, c1 in IN_LOADS:
                    columns(n, A["w_in"][l], c0, c1)
                    n += 1
                for g in range(4):
                    columns(n, A["w_out"][l], g * SLOT_COLS, (g + 1) * SLOT_COLS)
                    n += 1
                for m in range(6):
                    slot_free(n + m)
                    expert(n + m, l, 0, m)
                f0 = freed_by[n + 4]
                with sp.Fori(0, PAIRS - 1) as i:
                    for m in range(12):
                        how = freed_by[n + m]
                        if isinstance(how, int):
                            sp.wait_ge(slot_used, i * 2 + how)
                        else:
                            product_ready(sp, how[0], i)
                        expert(n + m, l, 2 * i + 1 + m // 6, m % 6)
                n += 12 * (PAIRS - 1)
                for m in range(6, 12):
                    slot_free(n + m)
                    expert(n + m, l, N_EXP - 1, m - 6)
                n += 12
            assert n == len(loads)
            orow = big[:, 0:(NT - CT) * D].rearrange("p (i d) -> p i d", i=NT - CT)
            for i in range(NT - CT):
                for q in range(2):
                    evacuated(sp, ("out", CT + i, q))
                sp.dma_start(out[0, i * P:(i + 1) * P, :], orow[:, i, :]).then_inc(s_out, 16)
            sp.wait_ge(s_out, 16 * (NT - CT))

        @block.scalar
        def _(act):
            for dst, name in ((ident[:, :], "k_ident"), (tri[:, :, :], "k_tri"), (lev[:, :, :, :], "k_lev"),
                              (iota[:, :], "k_iota"), (rope[:, :, :, :], "k_rope"), (poolc[:, :, :], "k_pool")):
                act.dma_start(dst, A[name]).then_inc(s_const, 16)
            act.dma_start(arena[0:8, 11 * T:11 * T + P], A["c"].rearrange("b (k p) -> (b k) p", p=P)).then_inc(s_const, 16)
            act.dma_start(arena[8:16, 11 * T:11 * T + P], A["c_ctx"].rearrange("(k p) -> k p", p=P)).then_inc(s_const, 16)

            def squares(l, which, k):
                s = sems[l]
                t0 = 0 if which == 1 or l == 0 else CTX
                if k >= 2:
                    act.wait_ge(s["sqd%d" % which], k - 1)
                act.activation(sqb[:, k % 2, t0:T], xT[:, k, t0:T], ACT.Square).then_inc(s["sq%d" % which], 1)

            def norm(l, which):
                s = sems[l]
                segs = (1, 0) if which == 1 or l == 0 else (1,)
                for g in segs:
                    t0, n = SEGS[g]
                    b = product_ready(act, ("ss", l, which, g))
                    read_out(act.activation(rstd[:, t0:t0 + n], b[:, 0:n], ACT.Sqrt, bias=eps[:, 0:1], scale=1.0 / D),
                             ("ss", l, which, g))
                if which == 1:
                    act.wait_ge(s["mods"], 1)
                for k in range(KD):
                    act.wait_ge(s["hx%d" % which], k + 1)
                    for g in segs:
                        t0, n = SEGS[g]
                        c = 1 - g
                        m = act.activation(hT[:, k, t0:t0 + n], hT[:, k, t0:t0 + n], ACT.Identity,
                                           bias=mods[:, (0 if which == 1 else 3) * KD + k, c:c + 1],
                                           scale=amod[:, which - 1, k, c:c + 1])
                    m.then_inc(s["h%d" % which], 1)

            act.wait_ge(s_ones, 1)
            for k in range(KD):
                b = product_ready(act, ("x", k, 1))
                read_out(act.copy(xT[:, k, 512:T], b[:, 0:256]), ("x", k, 1))
            b = product_ready(act, "c")
            read_out(act.activation(scol[:, :, :].rearrange("p a b -> p (a b)"), b[:, 0:16], ACT.Silu), "c")

            for l in range(DEPTH):
                s = sems[l]
                need_ctx = l < DEPTH - 1
                tiles = range(NT) if need_ctx else range(CT, NT)
                segs = (0, 1) if need_ctx else (1,)
                t_first = tiles[0] * P

                if l == 0:
                    for k in range(KD):
                        evacuated(act, ("x", k, 0))
                        evacuated(act, ("x", k, 1))
                        squares(l, 1, k)
                else:
                    for k in range(KD):
                        for g in (0, 1):
                            evacuated(act, ("moe", l - 1, "c%d%d" % (k, g)), PAIRS - 1)
                        squares(l, 1, k)
                norm(l, 1)

                act.wait_ge(s["upad"], 1)
                for c in range(2):
                    for g in segs:
                        key = ("in", l, "pool%d" % c, g)
                        b = product_ready(act, key)
                        n = SEGS[g][1]
                        read_out(act.copy(U[:, c, UO[g]:UO[g] + n], b[:, 0:n]), key)
                for name, dst, m, gs in (("ql0", SQ0, P, segs), ("ql1", SQ1, 64, segs), ("kv", SQK, P, (0, 1))):
                    for g in gs:
                        t0, n = SEGS[g]
                        b = product_ready(act, ("in", l, name, g))
                        act.activation(dst[0:m, t0:t0 + n], b[0:m, 0:n], ACT.Square).then_inc(s["sqm"], 1)
                b = product_ready(act, ("krp", l))
                read_out(act.copy(krp.rearrange("p i c -> p (i c)"), b[:, 0:NT * ROPE]), ("krp", l))
                b = product_ready(act, ("rs", l))[:, 0:2 * NT].rearrange("p (i w) -> p i w", w=2)
                act.activation(rs12[:, tiles[0]:NT, 0:1], b[:, tiles[0]:NT, 0:1], ACT.Sqrt, bias=eps[:, 0:1],
                               scale=1.0 / Q_LORA)
                read_out(act.activation(rs12[:, :, 1:2], b[:, :, 1:2], ACT.Sqrt, bias=eps[:, 0:1],
                                        scale=1.0 / KV_LORA), ("rs", l))

                jobs = [("k", i) for i in range(NT)] + [("q", i) for i in tiles]

                def turned(n):
                    kind, i = jobs[n]
                    key = (kind + "t", l, i)
                    b = product_ready(act, key)
                    dst = (KT if kind == "k" else QT)[0:QK, :, i * P:(i + 1) * P]
                    read_out(act.copy(dst, b[0:QK, :].rearrange("p (h c) -> p h c", h=H)), key)

                for n in range(len(jobs)):
                    act.wait_ge(s["row1"], n + 1)
                    act.activation(ss4[:, n % 2, :], ss4[:, n % 2, :], ACT.Sqrt, bias=eps[:, 0:1],
                                   scale=1.0 / QK).then_inc(s["rowr"], 1)
                    if n:
                        turned(n - 1)
                turned(len(jobs) - 1)

                act.wait_ge(s["abraw"], 1)
                act.activation(abe[:, :, :], abe[:, :, :], ACT.Exp, scale=-1.0).then_inc(s["abexp"], 1)
                act.activation(abw[:, 1, :, :], abw[:, 1, :, :], ACT.Exp, scale=-1.0)
                act.activation(ealog, gpar[:, 0, :], ACT.Exp)
                act.wait_ge(s["abexp"], 1)
                act.activation(abe[:, :, :], abe[:, :, :], ACT.Ln, bias=ones[:, 0:1]).then_inc(s["abln"], 1)

                act.wait_ge(s["pool"], 2)
                units = [(m, g) for m in range(12) for g in (0, 1)]

                def silu(n):
                    m, g = units[n]
                    t0, w = SEGS[g]
                    evacuated(act, ("in", l, "qkv%d" % m, g))
                    act.activation(qkvT[:, m, t0:t0 + w], qkvT[:, m, t0:t0 + w], ACT.Silu).then_inc(s["qkv"], 1)

                for n, (m, g) in enumerate(units):
                    t0, w = SEGS[g]
                    b = product_ready(act, ("in", l, "qkv%d" % m, g))
                    cc = COL_CONV + 12 + m
                    act.activation(qkvT[:, m, t0:t0 + w], b[:, 0:w], ACT.Copy, scale=cols[:, cc:cc + 1]
                                   ).then_inc(s["cv1"], 1)
                    if n:
                        silu(n - 1)
                silu(len(units) - 1)
                for m in range(4):
                    for g in segs:
                        t0, n = SEGS[g]
                        b = product_ready(act, ("in", l, "z%d" % m, g))
                        read_out(act.activation(szT[:, m, t0:t0 + n], b[:, 0:n], ACT.Silu), ("in", l, "z%d" % m, g))

                calls = [(i, h) for i in tiles for h in range(H)]

                def turned_att(i):
                    b = product_ready(act, ("at", l, i))
                    read_out(act.copy(mixT[:, 0:2, i * P:(i + 1) * P],
                                      b[:, 0:2 * P].rearrange("p (c t) -> p c t", c=2)), ("at", l, i))

                for n, (i, h) in enumerate(calls):
                    parts = (CT,) if i < CT else (4, 2)
                    act.wait_ge(s["nm"], n + 1)
                    if n:
                        pi, ph = calls[n - 1]
                        product_ready(act, ("pt", l, pi, ph, 0 if pi < CT else 1))
                    if h == 0 and i - tiles[0] >= 2:
                        evacuated(act, ("o", l, i - 2))
                    k0 = 0
                    for part, nk in enumerate(parts):
                        key = ("s", l, i, h, part)
                        b = product_ready(act, key)
                        read_out(act.activation(PR[:, k0 * P:(k0 + nk) * P], b[:, 0:nk * P], ACT.Exp,
                                                bias=nm[:, n % 2:n % 2 + 1], scale=QK ** -0.5,
                                                accum_out=sm[:, i % 2, h, part:part + 1]), key)
                        k0 += nk
                    if h == 0 and n:
                        turned_att(i - 1)
                    if len(parts) == 2:
                        key = ("pt", l, i, h, 1)
                        b = product_ready(act, key)
                        if n:
                            attended(act, l, calls, n - 1)
                        read_out(act.copy(PT[:, 4:6, :].rearrange("p j c -> p (j c)"), b[:, 0:2 * P]), key)
                turned_att(NT - 1)

                product_ready(act, ("o", l, NT - 1))

                def lsquare(c):
                    if c >= 2:
                        product_ready(act, ("ln", l, c - 2, 1))
                    act.activation(sqb[:, c % 2, :], qkvT[:, c, :], ACT.Square).then_inc(s["lsq"], 1)

                act.wait_ge(s["qkv"], 24)
                lsquare(0)
                lsquare(1)
                for c in range(2 * GH):
                    if c >= 2:
                        act.wait_ge(s["lmul"], c - 1)
                    for g in (0, 1):
                        t0, n = SEGS[g]
                        b = product_ready(act, ("ln", l, c, g))
                        q = c < GH
                        read_out(act.activation(rs_gdn[:, c % 2, t0:t0 + n], b[:, 0:n], ACT.Sqrt,
                                                bias=eps[:, 1:2] if q else eps[:, 0:1], scale=128.0 if q else 1.0),
                                 ("ln", l, c, g))
                    if c + 2 < 2 * GH:
                        lsquare(c + 2)

                evacuated(act, ("gc", l))
                act.activation(bg[:, :, :, :], gc[:, :, :, :], ACT.Exp).then_inc(s["egc"], 1)

                for j in range(NT):
                    ti = [tile_of(d, j) for d in range(2)]
                    use_o = [need_ctx or i >= CT for i in ti]
                    for d in range(2):
                        b = product_ready(act, ("g", l, j, d))
                        if j and (need_ctx or tile_of(d, j - 1) >= CT):
                            product_ready(act, ("go", l, j - 1, d))
                        act.wait_ge(s["xg"], 2 * j + d + 1)
                        read_out(act.activation(gQG[d].rearrange("p h c -> p (h c)"), b, ACT.Exp), ("g", l, j, d))
                        act.wait_ge(s["dcl"], 2 * j + d + 1)
                        act.activation(gD[d], gD[d], ACT.Exp, scale=-1.0)
                        act.activation(gQK[d], gQK[d], ACT.Exp)
                        act.activation(gt4[:, d, :, :], gt4[:, d, :, :], ACT.Exp).then_inc(s["dex"], 1)
                    for d in range(2):
                        b = product_ready(act, ("at2", l, j, d))
                        read_out(act.copy(gAT[d].rearrange("p h c -> p (h c)"), b), ("at2", l, j, d))
                    for n in range(1, LEVELS):
                        for d in range(2):
                            key = ("xx", l, j, d, n, 0)
                            b = product_ready(act, key).rearrange("p (e x c) -> p e x c", e=2, x=2)
                            x0 = 0 if n < LEVELS - 1 else 1
                            read_out(act.copy(gX[d][:, 0:2, x0:2, :], b[:, :, x0:2, :]), key)
                    for d in range(2):
                        b = product_ready(act, ("wt", l, j, d))
                        read_out(act.mul(gML[d].rearrange("p h c -> p (h c)"), b, -1.0), ("wt", l, j, d))

                for d in range(2):
                    evacuated(act, ("go", l, NT - 1, d))

                def osquare(h):
                    if h >= 2:
                        product_ready(act, ("on", l, h - 2, 1))
                    act.activation(sqb[:, h % 2, t_first:T], mixT[:, 2 + h, t_first:T], ACT.Square
                                   ).then_inc(s["osq"], 1)

                osquare(0)
                osquare(1)
                for h in range(GH):
                    if h >= 2:
                        act.wait_ge(s["mixd"], h - 1)
                    for g in segs:
                        t0, n = SEGS[g]
                        b = product_ready(act, ("on", l, h, g))
                        read_out(act.activation(rs_gdn[:, h % 2, t0:t0 + n], b[:, 0:n], ACT.Sqrt, bias=eps[:, 0:1],
                                                scale=1.0 / P), ("on", l, h, g))
                    if h + 2 < GH:
                        osquare(h + 2)

                for k in range(KD):
                    for g in segs:
                        evacuated(act, ("y", l, k, g))
                    squares(l, 2, k)
                norm(l, 2)

                act.wait_ge(s["rmax"], 1)
                act.activation(aff[:, tiles[0]:NT, :], aff[:, tiles[0]:NT, :], ACT.Exp).then_inc(s["rexp"], 1)
                for i in tiles:
                    b = product_ready(act, ("hr", l, i, 0))
                    read_out(act.copy(hrow[:, i, 0:512], b), ("hr", l, i, 0))

                n_cap = CAP if need_ctx else CAP_L
                with act.Fori(0, PAIRS) as i:
                    for q in (0, 2):
                        name = "x%d" % q
                        b = product_ready(act, ("moe", l, name), i)[:, 0:4 * CAP].rearrange("p (k c) -> p k c", k=2)
                        copy_slots(act.copy, b, xs, q, need_ctx, lambda m: read_out(m, ("moe", l, name)))
                    b = product_ready(act, ("moe", l, "sl"), i)
                    read_out(act.copy(Sl[:, :], b), ("moe", l, "sl"))
                    if need_ctx:
                        b = product_ready(act, ("moe", l, "sc"), i)
                        read_out(act.copy(Sc[0:2 * CAP_C, :], b[0:2 * CAP_C, 0:CTX]), ("moe", l, "sc"))
                    for e in range(2):
                        for q in range(2):
                            name = "g%d%d" % (e, q)
                            b = product_ready(act, ("moe", l, name), i)[:, 0:2 * CAP].rearrange("p (f c) -> p f c", f=2)
                            if e:
                                evacuated(act, ("moe", l, "u0%d" % q), i)
                            read_out(act.activation(sg[:, q, :, 0:n_cap], b[:, :, 0:n_cap], ACT.Silu),
                                     ("moe", l, name))
                        name = "y%d0" % e
                        b = product_ready(act, ("moe", l, name), i)
                        m = act.copy(ylat[e * CAP_L:(e + 1) * CAP_L, 0:512], b[0:CAP_L, :])
                        if need_ctx:
                            m = act.copy(yctx[e * CAP_C:(e + 1) * CAP_C, 0:512], b[CAP_L:CAP, :])
                        read_out(m, ("moe", l, name))

            orow = big[:, 0:(NT - CT) * D].rearrange("p (i d) -> p i d", i=NT - CT)
            for i in range(CT, NT):
                b = product_ready(act, ("out", i, 0))
                read_out(act.copy(orow[:, i - CT, 0:512], b), ("out", i, 0))

        @block.vector
        def _(dve):
            chain = [0, 0]

            def link(ins, l):
                chain[l] += 1
                ins.then_inc(sems[l]["dve"], 1)
                dve.wait_ge(sems[l]["dve"], chain[l])

            def norm(l, which):
                s = sems[l]
                segs = (1, 0) if which == 1 or l == 0 else (1,)
                t0 = 0 if len(segs) == 2 else CTX
                for g in segs:
                    evacuated(dve, ("ss", l, which, g))
                link(dve.reciprocal(rstd[:, t0:T], rstd[:, t0:T]), l)
                for k in range(KD):
                    dve.tensor_tensor(hT[:, k, t0:T], xT[:, k, t0:T], rstd[:, t0:T], ALU.mult
                                      ).then_inc(s["hx%d" % which], 1)

            for k in range(KD):
                b = product_ready(dve, ("x", k, 0))
                read_out(dve.tensor_copy(xT[:, k, 0:512], b), ("x", k, 0))

            for l in range(DEPTH):
                s = sems[l]
                need_ctx = l < DEPTH - 1
                tiles = range(NT) if need_ctx else range(CT, NT)
                segs = (0, 1) if need_ctx else (1,)
                i0 = tiles[0]
                t_first = i0 * P

                b = product_ready(dve, ("cols", l))
                read_out(dve.tensor_copy(cols[:, :], b[:, 0:N_COLS]), ("cols", l))
                evacuated(dve, ("cols", l))
                b = product_ready(dve, ("ada", l))[:, 0:12 * KD].rearrange("p (m c) -> p m c", c=2)
                read_out(dve.tensor_tensor(mods[:, :, :], b, cols[:, 0:6 * KD].unsqueeze(2).to_broadcast(
                    [P, 6 * KD, 2]), ALU.add), ("ada", l))
                evacuated(dve, ("ada", l))
                for w, (m0, c0) in enumerate(((KD, COL_N1), (4 * KD, COL_N2))):
                    m = dve.scalar_tensor_tensor(
                        out=amod[:, w, :, :], in0=mods[:, m0:m0 + KD, :], scalar=1.0,
                        in1=cols[:, c0:c0 + KD].unsqueeze(2).to_broadcast([P, KD, 2]), op0=ALU.add, op1=ALU.mult)
                m.then_inc(s["mods"], 1)
                norm(l, 1)

                b = product_ready(dve, ("ab", l))[:, 0:NT * 16].rearrange("p (i c) -> p i c", i=NT)
                dve.wait_ge(s["par"], 16 * PAR_DMAS)
                link(dve.tensor_tensor(abw[:, 0, :, :], b[:, :, 0:8], gpar[:, 1, :].unsqueeze(1).to_broadcast(
                    [P, NT, 8]), ALU.add), l)
                read_out(dve.tensor_copy(abw[:, 1, :, :], b[:, :, 8:16]), ("ab", l))
                evacuated(dve, ("ab", l))
                dve.scalar_tensor_tensor(out=abe[:, :, :], in0=abw[:, 0, :, :], scalar=-1.0, in1=abw[:, 0, :, :],
                                         op0=ALU.mult, op1=ALU.max).then_inc(s["abraw"], 1)

                n = 0
                for name, dst, m, c, gs in (("ql0", QG0, P, COL_Q, segs), ("ql1", QG1, 64, COL_Q + 1, segs),
                                            ("kv", KVG, P, COL_KV, (0, 1))):
                    for g in gs:
                        t0, w = SEGS[g]
                        n += 1
                        b = product_ready(dve, ("in", l, name, g))
                        dve.wait_ge(s["sqm"], n)
                        read_out(dve.tensor_scalar(dst[0:m, t0:t0 + w], b[0:m, 0:w], cols[0:m, c:c + 1], None,
                                                   ALU.mult), ("in", l, name, g))
                evacuated(dve, ("rs", l))
                link(dve.reciprocal(rs12[:, :, 1:2], rs12[:, :, 1:2]), l)
                link(dve.reciprocal(rs12[:, i0:NT, 0:1], rs12[:, i0:NT, 0:1]), l)
                evacuated(dve, ("krp", l))

                jobs = [("k", i) for i in range(NT)] + [("q", i) for i in tiles]

                def scale_rows(n):
                    kind, i = jobs[n]
                    key = (kind, l, i)
                    r = rows[:, n % 2, :, :]
                    b = product_ready(dve, key)
                    if n >= 2:
                        pk, pi = jobs[n - 2]
                        product_ready(dve, (pk + "t", l, pi))
                    if kind == "q":
                        read_out(dve.tensor_scalar(r, b[:, 0:H * QK].rearrange("p (h c) -> p h c", h=H),
                                                   rs12[:, i, 0:1], None, ALU.mult), key)
                    else:
                        v = b.rearrange("p (h c) -> p h c", h=H)
                        dve.tensor_scalar(V[:, i, :].rearrange("p (h c) -> p h c", h=H), v[:, :, NOPE:NOPE + DV],
                                          rs12[:, i, 1:2], None, ALU.mult)
                        link(dve.tensor_copy(r[:, :, NOPE:QK], krp[:, i, :].unsqueeze(1).to_broadcast([P, H, ROPE])),
                             l)
                        read_out(dve.tensor_scalar(r[:, :, 0:NOPE], v[:, :, 0:NOPE], rs12[:, i, 1:2], None, ALU.mult),
                                 key)
                    evacuated(dve, key)
                    link(dve.tensor_tensor(rtmp, r, r, ALU.mult), l)
                    dve.tensor_reduce(ss4[:, n % 2, :], rtmp, AX.X, ALU.add).then_inc(s["row1"], 1)

                def norm_rows(n):
                    dve.wait_ge(s["rowr"], n + 1)
                    link(dve.reciprocal(ss4[:, n % 2, :], ss4[:, n % 2, :]), l)
                    r = rows[:, n % 2, :, :]
                    dve.tensor_tensor(r, r, ss4[:, n % 2, :].unsqueeze(2).to_broadcast([P, H, QK]), ALU.mult
                                      ).then_inc(s["rowa"], 1)

                scale_rows(0)
                for n in range(len(jobs)):
                    if n + 1 < len(jobs):
                        scale_rows(n + 1)
                    norm_rows(n)

                dve.wait_ge(s["abln"], 1)
                link(dve.scalar_tensor_tensor(out=abe[:, :, :], in0=abw[:, 0, :, :], scalar=0.0, in1=abe[:, :, :],
                                              op0=ALU.max, op1=ALU.add), l)
                dve.scalar_tensor_tensor(out=gb[:, 0, :, :], in0=abe[:, :, :], scalar=-1.0,
                                         in1=ealog.unsqueeze(1).to_broadcast([P, NT, 8]), op0=ALU.mult, op1=ALU.mult)
                link(dve.tensor_scalar(abw[:, 1, :, :], abw[:, 1, :, :], 1.0, None, ALU.add), l)
                dve.reciprocal(gb[:, 1, :, :], abw[:, 1, :, :]).then_inc(s["gbd"], 1)

                for m in range(12):
                    for g in (0, 1):
                        t0, n = SEGS[g]
                        key = ("in", l, "qkv%d" % m, g)
                        b = product_ready(dve, key)
                        dve.wait_ge(s["cv1"], 2 * m + g + 1)
                        a = qkvT[:, m, t0 + 1:t0 + n]
                        link(dve.scalar_tensor_tensor(out=a, in0=b[:, 0:n - 1], scalar=cols[:, COL_CONV + m:
                                                      COL_CONV + m + 1], in1=a, op0=ALU.mult, op1=ALU.add), l)
                        a = qkvT[:, m, t0:t0 + n - 1]
                        cc = COL_CONV + 24 + m
                        read_out(dve.scalar_tensor_tensor(out=a, in0=b[:, 1:n], scalar=cols[:, cc:cc + 1], in1=a,
                                                          op0=ALU.mult, op1=ALU.add), key)

                for c in range(2):
                    for g in segs:
                        t0, n = SEGS[g]
                        b = product_ready(dve, ("pm", l, c, g))
                        read_out(dve.tensor_scalar(mixT[:, 6 + c, t0:t0 + n], b[:, 0:n],
                                                   cols[:, COL_PS + c:COL_PS + c + 1], None, ALU.mult),
                                 ("pm", l, c, g))

                calls = [(i, h) for i in tiles for h in range(H)]

                def row_max(n):
                    i, h = calls[n]
                    parts = (CT,) if i < CT else (4, 2)
                    if n >= 2:
                        pi, ph = calls[n - 2]
                        for part in range(1 if pi < CT else 2):
                            evacuated(dve, ("s", l, pi, ph, part))
                    for part, nk in enumerate(parts):
                        b = product_ready(dve, ("s", l, i, h, part))
                        link(dve.reduce_max(mx[:, n % 2, part:part + 1], b[:, 0:nk * P], AX.X), l)
                    w = len(parts) - 1
                    dve.tensor_scalar(nm[:, n % 2:n % 2 + 1], mx[:, n % 2, 0:1], mx[:, n % 2, w:w + 1],
                                      -(QK ** -0.5), ALU.max, ALU.mult).then_inc(s["nm"], 1)

                row_max(0)
                for n, (i, h) in enumerate(calls):
                    if n + 1 < len(calls):
                        row_max(n + 1)
                    nk = CT if i < CT else 4
                    key = ("pt", l, i, h, 0)
                    b = product_ready(dve, key)
                    if n:
                        attended(dve, l, calls, n - 1)
                    read_out(dve.tensor_copy(PT[:, 0:nk, :].rearrange("p j c -> p (j c)"), b[:, 0:nk * P]), key)
                    if h == H - 1:
                        if i >= CT:
                            link(dve.tensor_tensor(rden, sm[:, i % 2, :, 0], sm[:, i % 2, :, 1], ALU.add), l)
                        else:
                            link(dve.tensor_copy(rden, sm[:, i % 2, :, 0]), l)
                        link(dve.reciprocal(rden, rden), l)
                        if i > i0:
                            product_ready(dve, ("at", l, i - 1))
                        b = product_ready(dve, ("o", l, i))
                        read_out(dve.tensor_tensor(att.rearrange("p (h c) -> p h c", h=H), b[:, 0:H * DV].rearrange(
                            "p (h c) -> p h c", h=H), rden.unsqueeze(2).to_broadcast([P, H, DV]), ALU.mult),
                            ("o", l, i))

                for c in range(2 * GH):
                    for g in (0, 1):
                        evacuated(dve, ("ln", l, c, g))
                    link(dve.reciprocal(rs_gdn[:, c % 2, :], rs_gdn[:, c % 2, :]), l)
                    dve.tensor_tensor(qkvT[:, c, :], qkvT[:, c, :], rs_gdn[:, c % 2, :], ALU.mult
                                      ).then_inc(s["lmul"], 1)

                b = product_ready(dve, ("gc", l))
                read_out(dve.tensor_copy(gc.rearrange("p d i h -> p (d i h)"), b[:, 0:2 * NT * GH]), ("gc", l))
                dve.wait_ge(s["egc"], 1)
                for d in range(2):
                    link(dve.tensor_tensor(bg[:, d, :, :], bg[:, d, :, :], gb[:, 1, :, d * GH:(d + 1) * GH],
                                           ALU.mult), l)

                for j in range(NT):
                    ti = [tile_of(d, j) for d in range(2)]
                    tt = [slice(i * P, (i + 1) * P) for i in ti]
                    use_o = [need_ctx or i >= CT for i in ti]
                    for d in range(2):
                        b = product_ready(dve, ("g", l, j, d)).rearrange("p (h c) -> p h c", h=GH)
                        g1 = gc[:, d, ti[d], :]
                        if j:
                            evacuated(dve, ("st", l, j - 1, d))
                        dve.tensor_tensor(gAT[d], b, g1.unsqueeze(2).to_broadcast([P, GH, P]), ALU.subtract)
                        last = P - 1 if d == 0 else 0
                        dve.tensor_tensor(gt4[:, d, 0, :], b[:, :, last], g1, ALU.subtract)
                        dve.tensor_copy(gt4[:, d, 1, :], b[:, :, last]).then_inc(s["xg"], 1)
                    for d in range(2):
                        key = ("kk", l, j, d)
                        b = product_ready(dve, key)
                        dve.wait_ge(s["dm"], 2 * j + d + 1)
                        if j:
                            product_ready(dve, ("st", l, j - 1, d))
                        read_out(dve.tensor_tensor(gY[d].rearrange("p h c -> p (h c)"), b,
                                                   gD[d].rearrange("p h c -> p (h c)"), ALU.mult), key)
                        if use_o[d]:
                            key = ("qk", l, j, d)
                            b = product_ready(dve, key)
                            x = gQK[d].rearrange("p h c -> p (h c)")
                            read_out(dve.tensor_tensor(x, b, x, ALU.mult), key)
                    for n in range(1, LEVELS):
                        for d in range(2):
                            key = ("y", l, j, d, n)
                            b = product_ready(dve, key).rearrange("p (h c) -> p h c", h=GH)
                            read_out(dve.tensor_tensor(gY[d], ident[:, :].unsqueeze(1).to_broadcast([P, GH, P]), b,
                                                       ALU.subtract), key)
                        for d in range(2):
                            key = ("xx", l, j, d, n, 1)
                            b = product_ready(dve, key).rearrange("p (e x c) -> p e x c", e=2, x=2)
                            x0 = 0 if n < LEVELS - 1 else 1
                            read_out(dve.tensor_copy(gX[d][:, 2:4, x0:2, :], b[:, :, x0:2, :]), key)
                    for d in range(2):
                        key = ("kr", l, j, d)
                        b = product_ready(dve, key).rearrange("p (h c) -> p h c", h=GH)
                        dve.tensor_tensor(gAT[d], b, bg[:, d, ti[d], :].unsqueeze(2).to_broadcast([P, GH, P]),
                                          ALU.mult)
                        read_out(dve.tensor_tensor(gKD[d], b, gt4[:, d, 0, :].unsqueeze(2).to_broadcast([P, GH, P]),
                                                   ALU.mult), key)
                        key = ("vr", l, j, d)
                        b = product_ready(dve, key).rearrange("p (h c) -> p h c", h=GH)
                        be = gb[:, 1, ti[d], d * GH:(d + 1) * GH]
                        read_out(dve.tensor_tensor(gY[d], b, be.unsqueeze(2).to_broadcast([P, GH, P]), ALU.mult), key)
                    for d in range(2):
                        key = ("v", l, j, d)
                        b = product_ready(dve, key)
                        read_out(dve.tensor_copy(gY[d].rearrange("p h c -> p (h c)"), b), key)
                    for d in range(2):
                        if use_o[d]:
                            key = ("go", l, j, d)
                            b = product_ready(dve, key).rearrange("p (h c) -> p h c", h=GH)
                            o = mixT[:, 2:2 + GH, tt[d]]
                            first = [tile_of(1 - d, x) for x in range(NT)].index(ti[d]) > j
                            if first:
                                read_out(dve.tensor_copy(o, b), key)
                            else:
                                read_out(dve.tensor_tensor(o, b, o, ALU.add), key)
                        if j < NT - 1:
                            key = ("st", l, j, d)
                            b = product_ready(dve, key)
                            if j == 0:
                                read_out(dve.tensor_copy(S[:, d, :, :].rearrange("p h c -> p (h c)"), b), key)
                            else:
                                for h in range(GH):
                                    m = dve.scalar_tensor_tensor(out=S[:, d, h, :], in0=S[:, d, h, :],
                                                                 scalar=gt4[:, d, 1, h:h + 1],
                                                                 in1=b[:, h * P:(h + 1) * P], op0=ALU.mult,
                                                                 op1=ALU.add)
                                read_out(m, key)

                for h in range(GH):
                    for g in segs:
                        evacuated(dve, ("on", l, h, g))
                    r = rs_gdn[:, h % 2, t_first:T]
                    link(dve.reciprocal(r, r), l)
                    o = mixT[:, 2 + h, t_first:T]
                    link(dve.tensor_tensor(o, o, r, ALU.mult), l)
                    dve.scalar_tensor_tensor(out=o, in0=o, scalar=cols[:, COL_GN:COL_GN + 1],
                                             in1=szT[:, h, t_first:T], op0=ALU.mult, op1=ALU.mult
                                             ).then_inc(s["mixd"], 1)

                for k in range(KD):
                    for g in segs:
                        t0, n = SEGS[g]
                        key = ("y", l, k, g)
                        b = product_ready(dve, key)
                        x = xT[:, k, t0:t0 + n]
                        read_out(dve.scalar_tensor_tensor(out=x, in0=b[:, 0:n], scalar=mods[:, 2 * KD + k, 1 - g:2 - g],
                                                          in1=x, op0=ALU.mult, op1=ALU.add), key)
                norm(l, 2)

                b = product_ready(dve, ("rt", l))[:, 0:NT * N_EXP].rearrange("p (i e) -> p i e", i=NT)[:, i0:NT, :]
                nt = NT - i0
                link(dve.tensor_reduce(rt6[:, i0:NT], b, AX.X, ALU.max), l)
                a = aff[:, i0:NT, :]
                r = rt6[:, i0:NT].unsqueeze(2).to_broadcast([P, nt, N_EXP])
                link(dve.tensor_tensor(a, b, r, ALU.subtract), l)
                read_out(dve.tensor_copy(rt6[:, i0:NT], b[:, :, 0]), ("rt", l))
                evacuated(dve, ("rt", l))
                dve.tensor_copy(rt6[:, i0:NT], rt6[:, i0:NT]).then_inc(s["rmax"], 1)
                for i in tiles:
                    b = product_ready(dve, ("hr", l, i, 1))
                    read_out(dve.tensor_copy(hrow[:, i, 512:1024], b), ("hr", l, i, 1))
                dve.wait_ge(s["rexp"], 1)
                link(dve.tensor_reduce(rt6[:, i0:NT], a, AX.X, ALU.add), l)
                link(dve.reciprocal(rt6[:, i0:NT], rt6[:, i0:NT]), l)
                dve.tensor_tensor(a, a, r, ALU.mult).then_inc(s["aff"], 1)

                for g in segs:
                    t0, n = SEGS[g]
                    cap = CAP_L if g else CAP_C
                    b = product_ready(dve, ("aT", l, g))
                    E = slice(0, N_EXP)
                    w, av, se, cs = (x[E, t0:t0 + n] for x in (tkw, affT, sel, csum))
                    link(dve.tensor_copy(av, b[E, 0:n]), l)
                    read_out(dve.tensor_copy(w, b[E, 0:n]), ("aT", l, g))
                    evacuated(dve, ("aT", l, g))
                    for r8 in range(cap // 8):
                        link(dve.max(top8[:, :], w), l)
                        if r8 < cap // 8 - 1:
                            link(dve.match_replace(w, top8[:, :], w, -1.0), l)
                    thr = top8[:, 7:8]
                    link(dve.tensor_scalar(se, av, thr, None, ALU.is_gt), l)
                    link(dve.tensor_scalar(w, av, thr, None, ALU.is_equal), l)
                    link(dve.tensor_reduce(tkn[:, 0:1], se, AX.X, ALU.add), l)
                    link(dve.tensor_scalar(tkn[:, 1:2], tkn[:, 0:1], -1.0, float(cap), ALU.mult, ALU.add), l)
                    link(dve.tensor_tensor_scan(cs, w, w, 0.0, ALU.add, ALU.max), l)
                    link(dve.scalar_tensor_tensor(out=w, in0=cs, scalar=tkn[:, 1:2], in1=w, op0=ALU.is_le,
                                                  op1=ALU.mult), l)
                    link(dve.tensor_tensor(se, se, w, ALU.add), l)
                    link(dve.tensor_tensor_scan(cs, se, se, 0.0, ALU.add, ALU.max), l)
                    link(dve.tensor_tensor(se, cs, se, ALU.mult), l)
                    dve.tensor_scalar(se, se, -1.0, None, ALU.add).then_inc(s["sel"], 1)
                b = product_ready(dve, ("slot", l))
                read_out(dve.tensor_copy(slotc[:, i0:NT, :].rearrange("p i e -> p (i e)"),
                                         b[:, i0 * N_EXP:NT * N_EXP]), ("slot", l))
                evacuated(dve, ("slot", l))

                n_cap = CAP if need_ctx else CAP_L
                NL = SEQ // P
                with dve.Fori(0, PAIRS) as i:
                    m = dve.tensor_tensor(Gl, iota[:, :].unsqueeze(1).unsqueeze(1).to_broadcast([P, NL, 2, CAP_L]),
                                          slotc[:, CT:NT, bass.ds(2 * i, 2)].unsqueeze(3).to_broadcast(
                                              [P, NL, 2, CAP_L]), ALU.is_equal)
                    if need_ctx:
                        m = dve.tensor_tensor(Gc, iota[:, 0:CAP_C].unsqueeze(1).unsqueeze(1).to_broadcast(
                            [P, CT, 2, CAP_C]), slotc[:, 0:CT, bass.ds(2 * i, 2)].unsqueeze(3).to_broadcast(
                                [P, CT, 2, CAP_C]), ALU.is_equal)
                    m.then_inc(s["G"], 1)
                    dve.wait_ge(s["G"], 2 * i + 1)
                    m = dve.tensor_tensor(GGl, Gl, aff[:, CT:NT, bass.ds(2 * i, 2)].unsqueeze(3).to_broadcast(
                        [P, NL, 2, CAP_L]), ALU.mult)
                    if need_ctx:
                        m = dve.tensor_tensor(GGc, Gc, aff[:, 0:CT, bass.ds(2 * i, 2)].unsqueeze(3).to_broadcast(
                            [P, CT, 2, CAP_C]), ALU.mult)
                    m.then_inc(s["G"], 1)
                    for q in (1, 3):
                        name = "x%d" % q
                        b = product_ready(dve, ("moe", l, name), i)[:, 0:4 * CAP].rearrange("p (k c) -> p k c", k=2)
                        copy_slots(dve.tensor_copy, b, xs, q, need_ctx, lambda m: read_out(m, ("moe", l, name)))
                    for e in range(2):
                        for q in range(2):
                            name = "u%d%d" % (e, q)
                            b = product_ready(dve, ("moe", l, name), i)[:, 0:2 * CAP].rearrange("p (f c) -> p f c", f=2)
                            evacuated(dve, ("moe", l, "g%d%d" % (e, q)), i)
                            if e:
                                product_ready(dve, ("moe", l, "y01"), i)
                            read_out(dve.tensor_tensor(hid[:, 2 * q:2 * q + 2, 0:n_cap], sg[:, q, :, 0:n_cap],
                                                       b[:, :, 0:n_cap], ALU.mult), ("moe", l, name))
                        name = "y%d1" % e
                        b = product_ready(dve, ("moe", l, name), i)
                        m = dve.tensor_copy(ylat[e * CAP_L:(e + 1) * CAP_L, 512:1024], b[0:CAP_L, :])
                        if need_ctx:
                            m = dve.tensor_copy(yctx[e * CAP_C:(e + 1) * CAP_C, 512:1024], b[CAP_L:CAP, :])
                        read_out(m, ("moe", l, name))
                    for k in range(KD):
                        for g in reversed(segs):
                            t0, n = SEGS[g]
                            name = "c%d%d" % (k, g)
                            b = product_ready(dve, ("moe", l, name), i)
                            x = xT[:, k, t0:t0 + n]
                            read_out(dve.scalar_tensor_tensor(out=x, in0=b[:, 0:n],
                                                              scalar=mods[:, 5 * KD + k, 1 - g:2 - g], in1=x,
                                                              op0=ALU.mult, op1=ALU.add), ("moe", l, name))

            orow = big[:, 0:(NT - CT) * D].rearrange("p (i d) -> p i d", i=NT - CT)
            for i in range(CT, NT):
                b = product_ready(dve, ("out", i, 1))
                read_out(dve.tensor_copy(orow[:, i - CT, 512:1024], b), ("out", i, 1))

        @block.gpsimd
        def _(pool):
            chain = [0, 0]

            def link(ins, l):
                chain[l] += 1
                ins.then_inc(sems[l]["pool_e"], 1)
                pool.wait_ge(sems[l]["pool_e"], chain[l])

            pool.memset(ones[:, :], 1.0)
            pool.memset(eps[:, 0:1], EPS)
            pool.memset(eps[:, 1:2], 128.0 * EPS).then_inc(s_ones, 1)
            pool.memset(poolw[:, :, :], 0.0)
            pool.memset(pstage[:, :], 0.0).then_inc(sems[0]["zero"], 1)
            pool.wait_ge(sems[0]["zero"], 1)
            pool.wait_ge(s_const, 16 * CONST_DMAS)

            def parameters(l):
                s = sems[l]
                for dst, src in (
                        (pstage[COL_ADA:COL_N1, :], A["ada_b"][l].rearrange("(r p) -> r p", p=P)),
                        (pstage[COL_N1:COL_N2, :], A["norm1_g"][l].rearrange("(r p) -> r p", p=P)),
                        (pstage[COL_N2:COL_CONV, :], A["norm2_g"][l].rearrange("(r p) -> r p", p=P)),
                        (pstage[COL_CONV:COL_KV, :], A["gdn_conv_w"][l].rearrange("t (r p) -> (t r) p", p=P)),
                        (pstage[COL_KV:COL_KV + 1, :], A["mla_kv_a_norm"][l:l + 1, :]),
                        (pstage[COL_GN:COL_GN + 1, :], A["gdn_norm_g"][l:l + 1, :]),
                        (pstage[COL_Q:COL_Q + 1, :], A["mla_q_a_norm"][l:l + 1, 0:P]),
                        (pstage[COL_Q + 1:COL_Q + 2, 0:64], A["mla_q_a_norm"][l:l + 1, P:Q_LORA]),
                        (pstage[COL_PS:COL_PS + 2, :], A["pool_scale"][l].rearrange("(r p) -> r p", p=P)),
                        (wuq[:, 0, :], A["mla_w_uq"][l, 0:P, :]),
                        (wuq[0:64, 1, :], A["mla_w_uq"][l, P:Q_LORA, :]),
                        (wukv[:, :], A["mla_w_ukv"][l]),
                        (poolw[0:64, 0, 0:64], A["pool_w"][l, 0]),
                        (poolw[64:128, 0, 64:128], A["pool_w"][l, 1]),
                        (poolw[0:64, 1, 0:64], A["pool_w"][l, 2]),
                        (poolw[64:128, 1, 64:128], A["pool_w"][l, 3]),
                        (router[:, :, :], A["moe_router"][l].rearrange("(k p) e -> p k e", p=P)),
                        (rown[:, 0, :], A["mla_k_norm"][l].partition_broadcast(P)),
                        (rown[:, 1, :], A["mla_q_norm"][l].partition_broadcast(P)),
                        (gpar[:, 0, :], A["gdn_a_log"][l].rearrange("d h -> (d h)").partition_broadcast(P)),
                        (gpar[:, 1, :], A["gdn_dt_bias"][l].rearrange("d h -> (d h)").partition_broadcast(P))):
                    pool.dma_start(dst, src).then_inc(s["par"], 16)

            parameters(0)
            for l in range(DEPTH):
                s = sems[l]
                need_ctx = l < DEPTH - 1
                tiles = range(NT) if need_ctx else range(CT, NT)
                segs = (0, 1) if need_ctx else (1,)

                if l == 0:
                    product_ready(pool, ("x", KD - 1, 1))
                else:
                    product_ready(pool, ("moe", l - 1, "c%d0" % (KD - 1)), PAIRS - 1)
                pool.memset(at(big, 0, (2 * UW,)), 0.0).then_inc(s["upad"], 1)

                def add_shift(dst, src, a, n):
                    return pool.tensor_tensor(dst[:, a:UW - n], src[:, 0:UW - n - a], src[:, a + n:UW], ALU.add)

                for c in range(2):
                    for g in segs:
                        evacuated(pool, ("in", l, "pool%d" % c, g))
                    u = U[:, c, :]
                    link(pool.tensor_tensor(BA[:, 1:UW], u[:, 1:UW], u[:, 0:UW - 1], ALU.add), l)
                    link(pool.tensor_tensor(BB[:, 2:UW - 1], BA[:, 1:UW - 2], BA[:, 3:UW], ALU.add), l)
                    if c == 1:
                        link(pool.tensor_tensor(BA[:, 4:UW - 3], BB[:, 2:UW - 5], BB[:, 6:UW - 1], ALU.add), l)
                        link(pool.tensor_tensor(BB[:, 8:UW - 7], BA[:, 4:UW - 11], BA[:, 12:UW - 3], ALU.add), l)
                    for half, src in ((0, BA), (1, BB)):
                        r = slice(64 * half, 64 * half + 64)
                        for g in segs:
                            t0, n = SEGS[g]
                            link(pool.tensor_scalar(dT[r, c, t0:t0 + n], src[r, UO[g]:UO[g] + n], poolc[r, c, 16:17],
                                                    None, ALU.mult), l)
                    for g in segs:
                        t0, n = SEGS[g]
                        x = dT[:, c, t0:t0 + 8]
                        link(pool.tensor_tensor(x, x, poolc[:, c, 0:8], ALU.mult), l)
                        x = dT[:, c, t0 + n - 8:t0 + n]
                        link(pool.tensor_tensor(x, x, poolc[:, c, 8:16], ALU.mult), l)
                        x = dT[:, c, t0:t0 + n]
                        m = pool.tensor_tensor(x, x, u[:, UO[g]:UO[g] + n], ALU.subtract)
                        if g == 1:
                            m.then_inc(s["pool"], 1)
                        else:
                            link(m, l)

                pool.wait_ge(s["par"], 16 * PAR_DMAS)
                jobs = [("k", i) for i in range(NT)] + [("q", i) for i in tiles]
                for n, (kind, i) in enumerate(jobs):
                    pool.wait_ge(s["rowa"], n + 1)
                    r = rows[:, n % 2, :, :]
                    w = rown[:, 0 if kind == "k" else 1, :].unsqueeze(1).to_broadcast([P, H, QK])
                    m = pool.tensor_tensor(r, r, w, ALU.mult)
                    if i >= CT:
                        link(m, l)
                        x = r[:, :, NOPE:QK]
                        link(pool.tensor_tensor(rot1, x, rope[:, i - CT, 0, :].unsqueeze(1).to_broadcast(
                            [P, H, ROPE]), ALU.mult), l)
                        x4 = x.rearrange("p h (g a e) -> p h g a e", g=2, a=2)
                        s4 = rope[:, i - CT, 1, :].rearrange("p (g a e) -> p g a e", g=2, a=2)
                        for a in range(2):
                            link(pool.tensor_tensor(rot2[:, :, :, a, :], x4[:, :, :, 1 - a, :],
                                                    s4[:, :, a, :].unsqueeze(1).to_broadcast([P, H, 2, ROPE // 4]),
                                                    ALU.mult), l)
                        m = pool.tensor_tensor(x, rot1, rot2.rearrange("p h g a e -> p h (g a e)"), ALU.add)
                    m.then_inc(s["row2"], 1)

                pool.wait_ge(s["gbd"], 1)
                pool.wait_ge(s["lmul"], 2 * GH)
                product_ready(pool, ("gc", l))
                for j in range(NT):
                    ti = [tile_of(d, j) for d in range(2)]
                    tt = [slice(i * P, (i + 1) * P) for i in ti]
                    for d in range(2):
                        if j:
                            product_ready(pool, ("v", l, j - 1, d))
                        pool.tensor_tensor(gML[d], tri[:, d, :].unsqueeze(1).to_broadcast([P, GH, P]),
                                           gb[:, 0, ti[d], d * GH:(d + 1) * GH].unsqueeze(2).to_broadcast(
                                               [P, GH, P]), ALU.mult).then_inc(s["tg"], 1)
                    for d in range(2):
                        pool.wait_ge(s["xg"], 2 * j + d + 1)
                        if j and (need_ctx or tile_of(d, j - 1) >= CT):
                            product_ready(pool, ("go", l, j - 1, d))
                        pool.tensor_scalar(gD[d], gAT[d], 0.0, None, ALU.max)
                        pool.tensor_scalar(gQK[d], gAT[d], 0.0, None, ALU.min).then_inc(s["dcl"], 1)
                    for d in range(2):
                        pool.wait_ge(s["dex"], 2 * j + d + 1)
                        pool.tensor_tensor(gQK[d], gQK[d], tri[:, d, :].unsqueeze(1).to_broadcast([P, GH, P]),
                                           ALU.mult)
                        pool.tensor_tensor(gD[d], gD[d], gb[:, 1, ti[d], d * GH:(d + 1) * GH].unsqueeze(2)
                                           .to_broadcast([P, GH, P]), ALU.mult).then_inc(s["dm"], 1)
                    for d in range(2):
                        evacuated(pool, ("kk", l, j, d))
                        evacuated(pool, ("at2", l, j, d))
                        if j == 0 or True:
                            pool.tensor_tensor(gML[d], gAT[d], lev[:, d, 1, :].unsqueeze(1).to_broadcast(
                                [P, GH, P]), ALU.mult).then_inc(s["ml"], 1)
                        for x, src in ((0, gY[d]), (1, gAT[d])):
                            link(pool.tensor_tensor(gX[d][:, :, x, :], src, lev[:, d if x else 1 - d, 0, :]
                                                    .unsqueeze(1).to_broadcast([P, GH, P]), ALU.mult), l)
                            m = pool.tensor_tensor(gX[d][:, :, x, :], ident[:, :].unsqueeze(1).to_broadcast(
                                [P, GH, P]), gX[d][:, :, x, :], ALU.subtract)
                        m.then_inc(s["x1"], 1)
                    for n in range(2, LEVELS):
                        for d in range(2):
                            product_ready(pool, ("y", l, j, d, n - 1))
                            pool.tensor_tensor(gML[d], gAT[d], lev[:, d, n, :].unsqueeze(1).to_broadcast(
                                [P, GH, P]), ALU.mult).then_inc(s["ml"], 1)
                    for d in range(2):
                        evacuated(pool, ("g", l, j, d))
                        pool.tensor_tensor(gQG[d], gQG[d], qkvT[:, 0:GH, tt[d]], ALU.mult).then_inc(s["qg"], 1)

                if l + 1 < DEPTH:
                    product_ready(pool, ("rt", l))
                    evacuated(pool, ("cols", l))
                    parameters(l + 1)
    return where


def copy_slots(copy, b, xs, q, need_ctx, finish):
    lat = b[:, :, 0:2 * CAP_L].rearrange("p k (e c) -> p k e c", e=2)
    m = copy(xs[:, 2 * q:2 * q + 2, :, 0:CAP_L], lat)
    if need_ctx:
        con = b[:, :, 2 * CAP_L:2 * CAP].rearrange("p k (e c) -> p k e c", e=2)
        m = copy(xs[:, 2 * q:2 * q + 2, :, CAP_L:CAP], con)
    finish(m)


_INS = ["x", "c", "ctx", "c_ctx", "ada_w", "ada_b", "norm1_g", "norm2_g", "w_in", "mla_q_a_norm", "mla_w_uq",
        "mla_kv_a_norm", "mla_w_ukv", "mla_q_norm", "mla_k_norm", "gdn_conv_w", "gdn_a_log", "gdn_dt_bias",
        "gdn_norm_g", "pool_w", "pool_scale", "w_out", "moe_router", "moe_w_gate", "moe_w_up", "moe_w_down"]


def kernel(**inputs):
    import concourse.bacc as _bacc
    from concourse.bass_utils import run_bass_kernel_spmd as _run

    nc = _bacc.Bacc("TRN2", target_bir_lowering=False, num_devices=1)
    arrays, args = {}, {}
    for name, a in [(n, inputs[n]) for n in _INS] + list(shape_constants().items()):
        a = np.ascontiguousarray(a)
        arrays["in_" + name] = a
        args[name] = nc.dram_tensor("in_" + name, a.shape, mybir.dt.from_np(a.dtype), kind="ExternalInput").ap()
    out = nc.dram_tensor("out", (1, SEQ, D), F32, kind="ExternalOutput").ap()
    build_program(nc, args, out)
    r = _run(nc, [arrays], core_ids=[0])
    return r.results[0]["out"]
```

```python
from contextlib import ExitStack

import numpy as np

import concourse.bass as bass
from concourse import mybir

F32 = mybir.dt.float32
ALU = mybir.AluOpType
ACT = mybir.ActivationFunctionType
AX = mybir.AxisListType

P = 128
D = 1024
KD = D // P
CTX = 256
SEQ = 512
T = CTX + SEQ
NT = T // P
CT = CTX // P
DEPTH = 2
EPS = 1e-6
GRID_W = 64
ROPE_THETA = 10000.0

H = 4
NOPE, ROPE, DV = 64, 32, 64
QK = NOPE + ROPE
Q_LORA, KV_LORA = 192, 128
GH = 4
WINDOWS = (2, 4, 8, 16)
PG = 64
PAD = 8
N_EXP = 16
F_EXP = 512
FK = F_EXP // P
CAP_L = 2 * SEQ // N_EXP
CAP_C = 2 * CTX // N_EXP
CAP = CAP_L + CAP_C
PAIRS = N_EXP // 2
LEVELS = 7

ADA_LOADS = 6 * D // 256
ADA_FIRST = 2 * D // 256
ADA_LATER = [(0, g) for g in range(ADA_FIRST, ADA_LOADS)] + [(1, g) for g in range(ADA_LOADS)]
ADA_GROUP = LEVELS - 1
ADA_GROUPS = -(-len(ADA_LATER) // ADA_GROUP)

SPLITS = (Q_LORA, KV_LORA, ROPE, 512, 512, 512, 512, 8, 8, 256)
OFF = [int(x) for x in np.cumsum((0,) + SPLITS)]
SLOTS = 6
COL_DMAS = 9
PAR_DMAS = 12
CONST_DMAS = 8
SLOT_COLS = 256
BANKS = 8

SEGS = ((0, CTX), (CTX, SEQ))
COL_ADA, COL_N1, COL_N2, COL_CONV, COL_KV, COL_GN, COL_Q, COL_PS = 0, 48, 56, 64, 100, 101, 102, 104
N_COLS = 106
IN_LOADS = [("pool", OFF[9], OFF[10]), ("ab", OFF[7], OFF[9]), ("ql", OFF[0], OFF[1]), ("kvr", OFF[1], OFF[3])]
IN_LOADS += [("qkv%d" % j, OFF[3] + 256 * j, OFF[3] + 256 * (j + 1)) for j in range(6)]
IN_LOADS += [("z%d" % j, OFF[6] + 256 * j, OFF[6] + 256 * (j + 1)) for j in range(2)]


def shape_constants():
    s = np.arange(P)
    out = {"k_ident": np.eye(P, dtype=np.float32)}
    out["k_tri"] = np.stack([s[:, None] <= s[None, :], s[:, None] >= s[None, :]], 1).astype(np.float32)
    lev = np.zeros((P, 2, LEVELS, P), np.float32)
    for n in range(LEVELS):
        b = 1 << n
        same = (s[:, None] // (2 * b)) == (s[None, :] // (2 * b))
        low = (s // b) % 2 == 0
        lev[:, 0, n] = same & low[:, None] & ~low[None, :]
        lev[:, 1, n] = same & ~low[:, None] & low[None, :]
    out["k_lev"] = lev
    slots = np.tile(np.arange(CAP_L, dtype=np.float32), (P, 1))
    tokens = s[:, None] + P * np.arange(SEQ // P)[None, :]
    out["k_iota"] = np.concatenate([slots, tokens.astype(np.float32)], 1)
    n = ROPE // 4
    inv = np.float32(ROPE_THETA) ** (-np.arange(n, dtype=np.float32) / np.float32(n))
    t = np.arange(SEQ)
    ar = (t // GRID_W).astype(np.float32)[:, None] * inv
    ac = (t % GRID_W).astype(np.float32)[:, None] * inv
    cos = np.concatenate([np.cos(ar), np.cos(ar), np.cos(ac), np.cos(ac)], 1)
    sin = np.concatenate([-np.sin(ar), np.sin(ar), -np.sin(ac), np.sin(ac)], 1)
    tab = np.stack([cos, sin], 1).astype(np.float32)
    out["k_rope"] = np.ascontiguousarray(tab.reshape(SEQ // P, P, 2, ROPE).transpose(1, 0, 2, 3))
    pool = np.zeros((P, 2, 17), np.float32)
    for g, w in enumerate(WINDOWS):
        rows, c = slice(64 * (g % 2), 64 * (g % 2) + 64), g // 2
        for j in range(8):
            pool[rows, c, j] = w / (w - max(0, w // 2 - j))
            pool[rows, c, 8 + j] = w / (w - max(0, w // 2 - (8 - j)))
        pool[rows, c, 16] = 1.0 / w
    out["k_pool"] = pool
    return out


def build_program(nc, A, out):
    ctx = ExitStack()
    with ctx:
        def sb(name, shape):
            return ctx.enter_context(nc.sbuf_tensor(name, shape, F32))

        def sem(name):
            return ctx.enter_context(nc.semaphore(name))

        xT = sb("xT", [P, KD, T])
        hT = sb("hT", [P, KD, T])
        ring = sb("ring", [P, SLOTS, KD * SLOT_COLS])
        big = sb("big", [P, 12 * T])
        sz = sb("sz", [P, 4 * T])
        dT = sb("dT", [P, 2, T])
        arena = sb("arena", [P, 12 * T])
        ident = sb("ident", [P, P])
        ones = sb("ones", [P, P])
        tri = sb("tri", [P, 2, P])
        lev = sb("lev", [P, 2, LEVELS, P])
        iota = sb("iota", [P, CAP_L + SEQ // P])
        rope = sb("rope", [P, SEQ // P, 2, ROPE])
        poolc = sb("poolc", [P, 2, 17])
        pstage = hT[:, 0, 0:P]
        cstage = arena[0:16, 11 * T:11 * T + P]
        cols = sb("cols", [P, N_COLS])
        scol = sb("scol", [P, 2, KD])
        modraw = sb("modraw", [P, DEPTH * 6 * KD, 2])
        amods = sb("amods", [P, DEPTH, 2, KD, 2])
        wuq = sb("wuq", [P, 2, H * QK])
        wukv = sb("wukv", [P, H * (NOPE + DV)])
        poolw = sb("poolw", [P, 2, P])
        router = sb("router", [P, KD, N_EXP])
        rown = sb("rown", [P, 2, QK])
        gpar = sb("gpar", [P, 2, 8])
        eps = sb("eps", [P, 2])
        small = sb("small", [P, 640])
        psum = ctx.enter_context(nc.psum_tensor("psum", [P, BANKS, 512], F32))

        mixT = hT
        mods_of = [modraw[:, l * 6 * KD:(l + 1) * 6 * KD, :] for l in range(DEPTH)]
        amod_of = [amods[:, l, :, :, :] for l in range(DEPTH)]

        def at(t, first, shape):
            n = int(np.prod(shape))
            v = t[:, first:first + n]
            if len(shape) == 2:
                return v.rearrange("p (a b) -> p a b", a=shape[0])
            if len(shape) == 3:
                return v.rearrange("p (a b c) -> p a b c", a=shape[0], b=shape[1])
            if len(shape) == 4:
                return v.rearrange("p (a b c d) -> p a b c d", a=shape[0], b=shape[1], c=shape[2])
            return v

        sqb = at(arena, 0, (2, T))
        rstd = at(arena, 2 * T, (T,))
        rs_gdn = at(arena, 2 * T, (2, T))
        UW = T + 4 * PAD
        U = at(big, 0, (2, UW))
        BA = at(big, 2 * UW, (UW,))
        BB = at(big, 3 * UW, (UW,))
        rows = at(arena, 10 * T, (2, H, QK))
        rtmp = at(arena, 10 * T + 2 * H * QK, (H, QK))
        rot1 = at(arena, 10 * T + 3 * H * QK, (H, ROPE))
        rot2 = at(arena, 10 * T + 3 * H * QK + H * ROPE, (H, 2, 2, ROPE // 4))
        assert 3 * H * QK + 2 * H * ROPE <= 2 * T
        abrow = arena[0:16, 0:T]
        krow = arena[0:ROPE, 4 * T:5 * T]
        rtrow = sz[0:N_EXP, T:2 * T]
        UO = (PAD, CTX + 3 * PAD)
        QG0 = at(big, 6 * T, (T,))
        QG1 = at(big, 7 * T, (T,))
        KVG = at(big, 8 * T, (T,))
        SQ0 = at(big, 9 * T, (T,))
        SQ1 = at(big, 10 * T, (T,))
        SQK = at(big, 11 * T, (T,))
        qkvT = at(big, 0, (12, T))
        KT = at(arena, 0, (H, T))
        QT = at(arena, 4 * T, (H, T))
        V = at(arena, 8 * T, (NT, H * DV))
        PR = at(arena, 10 * T, (T,))
        PT = at(arena, 11 * T, (NT, P))
        att = dT[:, 0, 0:H * DV]
        G1 = GH * P
        GW = 8 * G1
        dir_at = [d * GW for d in range(2)]
        gAT = [at(arena, o, (GH, P)) for o in dir_at]
        gML = [at(arena, o + G1, (GH, P)) for o in dir_at]
        gX = [at(arena, o + 2 * G1, (GH, 2, P)) for o in dir_at]
        gD = [at(arena, o + 2 * G1, (GH, P)) for o in dir_at]
        gY = [at(arena, o + 4 * G1, (GH, P)) for o in dir_at]
        gQK = [at(arena, o + 5 * G1, (GH, P)) for o in dir_at]
        gKD = [at(arena, o + 6 * G1, (GH, P)) for o in dir_at]
        gQG = [at(arena, o + 7 * G1, (GH, P)) for o in dir_at]
        S = at(arena, 2 * GW, (2, GH, P))
        szT = at(sz, 0, (4, T))
        szrow = sz[0:2, 0:ADA_FIRST * SLOT_COLS]
        dTrow = dT[0:2, :, :].rearrange("p c t -> p (c t)")
        assert ADA_GROUP * SLOT_COLS <= 2 * T
        hrow = at(big, 0, (NT, D))
        Sl = at(big, NT * D, (SEQ,))
        Sc = at(big, NT * D + SEQ, (CTX,))
        tokrow = at(big, NT * D + SEQ + CTX, (SEQ,))
        xlat = at(big, 0, (D,))
        xctx = at(big, D, (D,))
        G = [at(arena, t * N_EXP * CAP_L, (N_EXP, CAP_L)) for t in range(SEQ // P)]
        G += [at(arena, (SEQ // P) * N_EXP * CAP_L + t * N_EXP * CAP_C, (N_EXP, CAP_C)) for t in range(CT)]
        at_m = N_EXP * (SEQ // P * CAP_L + CT * CAP_C)
        NW = 1 + N_EXP
        mrow = arena[0:NW, at_m:at_m + N_EXP * CAP]
        tokaff = at(arena, at_m + N_EXP * CAP, (NT, NW))
        affT = at(sz, 0, (T,))
        tkw = at(sz, T, (T,))
        sel = at(sz, 2 * T, (T,))
        csum = at(sz, 3 * T, (T,))
        xs = at(arena, 0, (KD, 2, CAP))
        hid = at(arena, 1536, (2, FK, CAP))
        sg = at(arena, 2304, (2, 2, CAP))
        ylat = at(arena, 2688, (D,))
        yctx = at(arena, 2688 + D, (D,))
        gcol = small[:, 0:32].rearrange("p (i w) -> p i w", w=4)
        gnow = small[:, 32:36]
        gb = small[:, 0:96].rearrange("p (w i c) -> p w i c", w=2, i=NT)
        gc = small[:, 96:144].rearrange("p (d i h) -> p d i h", d=2, i=NT)
        bg = small[:, 144:192].rearrange("p (d i h) -> p d i h", d=2, i=NT)
        krp = small[:, 436:628].rearrange("p (i c) -> p i c", i=NT)
        rs12 = small[:, 384:396].rearrange("p (i w) -> p i w", w=2)
        ss4 = small[:, 396:404].rearrange("p (n h) -> p n h", n=2)
        mx = small[:, 404:408].rearrange("p (n w) -> p n w", n=2)
        nm = small[:, 408:410]
        sm = small[:, 352:368].rearrange("p (n h w) -> p n h w", n=2, w=2)
        rden = small[:, 416:420]
        gt4 = small[:, 420:436].rearrange("p (d w h) -> p d w h", d=2, w=2)
        aff = small[:, 436:532].rearrange("p (i e) -> p i e", i=NT)
        slotc = small[:, 532:628].rearrange("p (i e) -> p i e", i=NT)
        rt6 = small[:, 628:634]
        abw = small[:, 192:288].rearrange("p (w i c) -> p w i c", w=2, i=NT)
        ealog = small[:, 288:296]
        abe = small[:, 296:344].rearrange("p (i c) -> p i c", i=NT)
        top8 = small[0:16, 36:44]
        tkn = small[0:16, 44:48]
        idx = ctx.enter_context(nc.sbuf_tensor("idx", [P, 2, PAIRS], mybir.dt.uint32))

        hD = [nc.dram_tensor("h_rows_%s" % n, (SEGS[g][1], D), F32).ap() for g, n in enumerate(("ctx", "lat"))]

        slot_full = [sem("slot_full%d" % i) for i in range(SLOTS)]
        slot_used = sem("slot_used")
        bank_full = [sem("bank_full%d" % i) for i in range(BANKS)]
        bank_free = [sem("bank_free%d" % i) for i in range(BANKS)]
        s_const = sem("s_const")
        s_ones = sem("s_ones")
        s_xin = sem("s_xin")
        s_out = sem("s_out")
        s_outrow = sem("s_outrow")
        NAMES = ["zero", "pcol", "par", "mods1", "mods2", "rinv", "sq1", "sqd1", "hx1", "h1", "sq2", "sqd2", "hx2", "h2", "upad", "pool", "sqm",
                 "abraw", "abexp", "abln", "gbd", "row1", "rowr", "rowa", "row2", "nm", "pv", "cv1", "qkv", "lsq",
                 "lmul", "egc", "bg", "tg", "xg", "dcl", "dex", "dm", "x1", "ml", "qg", "osq", "mixd", "rmax",
                 "rexp", "aff", "sel", "G", "hrow", "tok", "idx", "gath", "cur", "S", "dve", "pool_e"]
        sems = [dict((n, sem("%s_%d" % (n, l))) for n in NAMES) for l in range(DEPTH)]

        freed_by = []
        freed = [0]
        where = {}
        uses = [0] * BANKS
        turn = [0]
        loads = []

        def plus(base, per, i):
            return base if i is None else i * per + base

        def product_ready(eng, key, i=None):
            b, n, per = where[key]
            eng.wait_ge(bank_full[b], plus(n + 1, per, i))
            return psum[:, b, :]

        def read_out(ins, key):
            ins.then_inc(bank_free[where[key][0]], 1)

        def evacuated(eng, key, i=None):
            b, n, per = where[key]
            eng.wait_ge(bank_free[b], plus(n + 1, per, i))

        def attended(eng, l, calls, n):
            i, h = calls[n]
            if h == H - 1:
                product_ready(eng, ("o", l, i))
            else:
                eng.wait_ge(sems[l]["pv"], n - n // H)

        def tile_of(d, j):
            return j if d == 0 else (CT - 1 - j if j < CT else NT + CT - 1 - j)

        def expert_part(n):
            return (n // 4, n % 4) if n < 8 else ((n - 8) // 2, 4 + n % 2)

        def ada_keys(group):
            return [("ar",) + x for x in ADA_LATER[group * ADA_GROUP:(group + 1) * ADA_GROUP]]

        assert ADA_GROUPS == NT + 1
        def channel_parameters(eng, l):
            for dst, src in (
                    (pstage[COL_ADA:COL_N1, :], A["ada_b"][l].rearrange("(r p) -> r p", p=P)),
                    (pstage[COL_N1:COL_N2, :], A["norm1_g"][l].rearrange("(r p) -> r p", p=P)),
                    (pstage[COL_N2:COL_CONV, :], A["norm2_g"][l].rearrange("(r p) -> r p", p=P)),
                    (pstage[COL_CONV:COL_KV, :], A["gdn_conv_w"][l].rearrange("t (r p) -> (t r) p", p=P)),
                    (pstage[COL_KV:COL_KV + 1, :], A["mla_kv_a_norm"][l:l + 1, :]),
                    (pstage[COL_GN:COL_GN + 1, :], A["gdn_norm_g"][l:l + 1, :]),
                    (pstage[COL_Q:COL_Q + 1, :], A["mla_q_a_norm"][l:l + 1, 0:P]),
                    (pstage[COL_Q + 1:COL_Q + 2, 0:64], A["mla_q_a_norm"][l:l + 1, P:Q_LORA]),
                    (pstage[COL_PS:COL_PS + 2, :], A["pool_scale"][l].rearrange("(r p) -> r p", p=P))):
                eng.dma_start(dst, src).then_inc(sems[l]["pcol"], 16)

        block = ctx.enter_context(nc.Block())

        @block.tensor
        def _(pe):
            held = []

            def claim(key):
                while turn[0] % BANKS in held:
                    turn[0] += 1
                b = turn[0] % BANKS
                turn[0] += 1
                if uses[b]:
                    pe.wait_ge(bank_free[b], uses[b])
                where[key] = (b, uses[b], 0)
                uses[b] += 1
                return psum[:, b, :]

            def done(ins, key):
                ins.then_inc(bank_full[where[key][0]], 1)

            def last_use(ins, key=None):
                if key is None:
                    freed[0] += 1
                    ins.then_inc(slot_used, 1)
                    freed_by.append(freed[0])
                else:
                    freed_by.append((key, None))

            def weights(name):
                n = len(loads)
                loads.append(name)
                pe.wait_ge(slot_full[n % SLOTS], 16 * (n // SLOTS + 1))
                return ring[:, n % SLOTS, :].rearrange("p (k c) -> p k c", k=KD)

            def sum_over_partitions(l, which, sqs, sqd):
                s = sems[l]
                lat = claim(("ss", l, which, 1))
                need = which == 1 or l == 0
                con = claim(("ss", l, which, 0)) if need else None
                for k in range(KD):
                    pe.wait_ge(s[sqs], k + 1)
                    m = pe.matmul(lat, lhsT=ones[:, :], rhs=sqb[:, k % 2, CTX:T], start=k == 0, stop=k == KD - 1)
                    if k == KD - 1:
                        done(m, ("ss", l, which, 1))
                    if need:
                        m = pe.matmul(con[:, 0:CTX], lhsT=ones[:, :], rhs=sqb[:, k % 2, 0:CTX], start=k == 0,
                                      stop=k == KD - 1)
                        if k == KD - 1:
                            done(m, ("ss", l, which, 0))
                    if k < KD - 1:
                        m.then_inc(s[sqd], 1)

            def ada_row(b, w, key, ks):
                for k in ks:
                    m = pe.matmul(b[0:2, 0:SLOT_COLS], lhsT=scol[:, :, k], rhs=w[:, k, :], start=k == 0,
                                  stop=k == KD - 1)
                if ks[-1] == KD - 1:
                    done(m, key)
                    last_use(None, key)

            def ada_columns(key, row, keys):
                for x in keys:
                    evacuated(pe, x)
                b = claim(key)
                for j in range(len(keys) * SLOT_COLS // P):
                    m = pe.transpose(b[:, 2 * j:2 * j + 2], row[0:2, j * P:(j + 1) * P], ident[0:2, 0:2])
                done(m, key)

            later = [0, None, None]

            def ada_later(half):
                if later[0] == len(ADA_LATER):
                    return
                key = ("ar",) + ADA_LATER[later[0]]
                if half == 0:
                    later[1] = claim(key)
                    held.append(where[key][0])
                    later[2] = weights(("ada",) + ADA_LATER[later[0]])
                ada_row(later[1], later[2], key, range(half * KD // 2, (half + 1) * KD // 2))
                if half == 1:
                    held.remove(where[key][0])
                    later[0] += 1

            pe.wait_ge(s_const, 16 * CONST_DMAS)
            pe.wait_ge(s_ones, 1)
            pe.wait_ge(s_xin, 16 * 2)
            xin = at(big, 0, (NT, D))
            for k in range(KD):
                for half, tiles in enumerate((range(0, 4), range(4, 6))):
                    key = ("x", k, half)
                    b = claim(key)
                    for j, i in enumerate(tiles):
                        m = pe.transpose(b[:, j * P:(j + 1) * P], xin[:, i, k * P:(k + 1) * P], ident[:, :])
                    done(m, key)

            for l in range(DEPTH):
                s = sems[l]
                need_ctx = l < DEPTH - 1
                tiles = range(NT) if need_ctx else range(CT, NT)
                segs = (0, 1) if need_ctx else (1,)

                pe.wait_ge(s["pcol"], 16 * COL_DMAS)
                b = claim(("cols", l))
                done(pe.transpose(b[:, 0:N_COLS], pstage[0:N_COLS, :], ident[0:N_COLS, 0:N_COLS]), ("cols", l))
                if l == 0:
                    b = claim("c")
                    done(pe.transpose(b[:, 0:16], cstage, ident[0:16, 0:16]), "c")
                sum_over_partitions(l, 1, "sq1", "sqd1")
                if l == 0:
                    evacuated(pe, "c")
                    for g in range(ADA_FIRST):
                        key = ("ar", 0, g)
                        ada_row(claim(key), weights(("ada", 0, g)), key, range(KD))
                    ada_columns(("am", 0), szrow, [("ar", 0, g) for g in range(ADA_FIRST)])

                def chunk(key, w, c0, c1, which):
                    bs = [(g, claim(key + (g,))) for g in which]
                    for k in range(KD):
                        if key[2] == "pool0":
                            pe.wait_ge(s["h1"], k + 1)
                        for g, b in bs:
                            t0, n = SEGS[g]
                            m = pe.matmul(b[0:c1 - c0, 0:n], lhsT=w[:, k, c0:c1], rhs=hT[:, k, t0:t0 + n],
                                          start=k == 0, stop=k == KD - 1)
                            if k == KD - 1:
                                done(m, key + (g,))

                def token_rows(key, src, ts):
                    n = src.shape[0]
                    b = claim(key)
                    for i in ts:
                        m = pe.transpose(b[:, i * n:(i + 1) * n], src[:, i * P:(i + 1) * P], ident[0:n, 0:n])
                    done(m, key)

                w = weights(("in", l, 0))
                chunk(("in", l, "pool0"), w, 0, P, segs)
                chunk(("in", l, "pool1"), w, P, 2 * P, segs)
                last_use(None, ("in", l, "pool1", 1))
                w = weights(("in", l, 1))
                chunk(("in", l, "ab"), w, 0, 16, (0, 1))
                last_use(None, ("in", l, "ab", 1))
                w = weights(("in", l, 2))
                chunk(("in", l, "ql0"), w, 0, P, segs)
                chunk(("in", l, "ql1"), w, P, Q_LORA, segs)
                last_use(None, ("in", l, "ql1", 1))
                for g in (0, 1):
                    evacuated(pe, ("in", l, "ab", g))
                token_rows(("ab", l), abrow, range(NT))
                w = weights(("in", l, 3))
                chunk(("in", l, "kv"), w, 0, KV_LORA, (0, 1))
                chunk(("in", l, "krp"), w, KV_LORA, KV_LORA + ROPE, (0, 1))
                last_use(None, ("in", l, "krp", 1))

                b = claim(("rs", l))
                for g in (0, 1):
                    evacuated(pe, ("in", l, "kv", g))
                for g in segs:
                    evacuated(pe, ("in", l, "ql1", g))
                    evacuated(pe, ("in", l, "ql0", g))
                for i in range(NT):
                    t = slice(i * P, (i + 1) * P)
                    if i in tiles:
                        pe.matmul(b[:, 2 * i:2 * i + 1], lhsT=SQ0[:, t], rhs=ones[:, 0:1], start=True, stop=False)
                        pe.matmul(b[:, 2 * i:2 * i + 1], lhsT=SQ1[0:64, t], rhs=ones[0:64, 0:1], start=False,
                                  stop=True)
                    m = pe.matmul(b[:, 2 * i + 1:2 * i + 2], lhsT=SQK[:, t], rhs=ones[:, 0:1], start=True, stop=True)
                done(m, ("rs", l))
                for g in (0, 1):
                    evacuated(pe, ("in", l, "krp", g))
                token_rows(("krp", l), krow, range(NT))
                jobs = [("k", i) for i in range(NT)] + [("q", i) for i in tiles]
                pe.wait_ge(s["par"], 16 * PAR_DMAS)

                def project(n):
                    kind, i = jobs[n]
                    t = slice(i * P, (i + 1) * P)
                    key = (kind, l, i)
                    b = claim(key)
                    if kind == "k":
                        m = pe.matmul(b[:, 0:512], lhsT=KVG[:, t], rhs=wukv[:, :], start=True, stop=True)
                    else:
                        pe.matmul(b[:, 0:H * QK], lhsT=QG0[:, t], rhs=wuq[:, 0, :], start=True, stop=False)
                        m = pe.matmul(b[:, 0:H * QK], lhsT=QG1[0:64, t], rhs=wuq[0:64, 1, :], start=False, stop=True)
                    done(m, key)

                def turn_rows(n):
                    kind, i = jobs[n]
                    key = (kind + "t", l, i)
                    b = claim(key)
                    pe.wait_ge(s["row2"], n + 1)
                    for h in range(H):
                        m = pe.transpose(b[0:QK, h * P:(h + 1) * P], rows[:, n % 2, h, :], ident[:, :])
                    done(m, key)

                def qkv(m):
                    if m % 2 == 0:
                        qkv_w[0] = weights(("in", l, 4 + m // 2))
                    chunk(("in", l, "qkv%d" % m), qkv_w[0], m % 2 * P, (m % 2 + 1) * P, (0, 1))
                    if m % 2:
                        last_use(None, ("in", l, "qkv%d" % m, 1))

                qkv_w = [None]
                project(0)
                project(1)
                for n in range(len(jobs)):
                    if n + 2 < len(jobs):
                        project(n + 2)
                    turn_rows(n)
                    if n % 2:
                        qkv(n // 2)
                for m in range(len(jobs) // 2, 12):
                    qkv(m)
                for j in range(2):
                    w = weights(("in", l, 10 + j))
                    for c in range(2):
                        chunk(("in", l, "z%d" % (2 * j + c)), w, c * P, (c + 1) * P, segs)
                    last_use(None, ("in", l, "z%d" % (2 * j + 1), 1))

                for c in range(2):
                    for g in segs:
                        key = ("pm", l, c, g)
                        b = claim(key)
                        pe.wait_ge(s["pool"], c + 1)
                        t0, n = SEGS[g]
                        done(pe.matmul(b[:, 0:n], lhsT=poolw[:, c, :], rhs=dT[:, c, t0:t0 + n], start=True,
                                       stop=True), key)

                calls = [(i, h) for i in tiles for h in range(H)]

                def keys_of(i):
                    return (CT,) if i < CT else (4, 2)

                def scores(i, h):
                    k0 = 0
                    for part, nk in enumerate(keys_of(i)):
                        key = ("s", l, i, h, part)
                        b = claim(key)
                        done(pe.matmul(b[:, 0:nk * P], lhsT=QT[0:QK, h, i * P:(i + 1) * P],
                                       rhs=KT[0:QK, h, k0:k0 + nk * P], start=True, stop=True), key)
                        k0 += nk * P

                evacuated(pe, (jobs[-1][0] + "t", l, jobs[-1][1]))
                evacuated(pe, (jobs[-2][0] + "t", l, jobs[-2][1]))
                scores(*calls[0])
                obank = None
                for n, (i, h) in enumerate(calls):
                    if h == 0:
                        obank = claim(("o", l, i))
                        held.append(where[("o", l, i)][0])
                    if n + 1 < len(calls):
                        scores(*calls[n + 1])
                    for part in range(len(keys_of(i))):
                        evacuated(pe, ("s", l, i, h, part))
                    k0 = 0
                    for part, nk in enumerate(keys_of(i)):
                        key = ("pt", l, i, h, part)
                        b = claim(key)
                        for j in range(nk):
                            m = pe.transpose(b[:, j * P:(j + 1) * P], PR[:, (k0 + j) * P:(k0 + j + 1) * P],
                                             ident[:, :])
                        done(m, key)
                        k0 += nk
                    for part in range(len(keys_of(i))):
                        evacuated(pe, ("pt", l, i, h, part))
                    for j in range(k0):
                        m = pe.matmul(obank[:, h * DV:(h + 1) * DV], lhsT=PT[:, j, :],
                                      rhs=V[:, j, h * DV:(h + 1) * DV], start=j == 0, stop=j == k0 - 1)
                    if h < H - 1:
                        m.then_inc(s["pv"], 1)
                    else:
                        done(m, ("o", l, i))
                        held.remove(where[("o", l, i)][0])
                        key = ("at", l, i)
                        b = claim(key)
                        evacuated(pe, ("o", l, i))
                        for c in range(2):
                            m = pe.transpose(b[:, c * P:(c + 1) * P], att[:, c * P:(c + 1) * P], ident[:, :])
                        done(m, key)

                for c in range(2 * GH):
                    pe.wait_ge(s["lsq"], c + 1)
                    for g in (0, 1):
                        t0, n = SEGS[g]
                        key = ("ln", l, c, g)
                        b = claim(key)
                        done(pe.matmul(b[:, 0:n], lhsT=ones[:, :], rhs=sqb[:, c % 2, t0:t0 + n], start=True,
                                       stop=True), key)

                b = claim(("gc", l))
                pe.wait_ge(s["gbd"], 1)
                for d in range(2):
                    for i in range(NT):
                        c0 = (d * NT + i) * GH
                        m = pe.matmul(b[:, c0:c0 + GH], lhsT=tri[:, d, :], rhs=gb[:, 0, i, d * GH:(d + 1) * GH],
                                      start=True, stop=True)
                done(m, ("gc", l))
                pe.wait_ge(s["lmul"], 2 * GH)
                pe.wait_ge(s["qkv"], 24)

                def heads(key, f, wait=None):
                    b = claim(key)
                    for h in range(GH):
                        m = f(b[:, h * P:(h + 1) * P], h)
                    done(m, key)

                for j in range(NT):
                    ti = [tile_of(d, j) for d in range(2)]
                    tt = [slice(i * P, (i + 1) * P) for i in ti]
                    use_o = [need_ctx or i >= CT for i in ti]
                    for d in range(2):
                        key = ("g", l, j, d)
                        b = claim(key)
                        pe.wait_ge(s["tg"], 2 * j + d + 1)
                        done(pe.matmul(b, lhsT=ones[:, :], rhs=gML[d].rearrange("p h c -> p (h c)"), start=True,
                                       stop=True), key)
                    for d in range(2):
                        heads(("kk", l, j, d), lambda o, h: pe.matmul(
                            o, lhsT=qkvT[:, GH + h, tt[d]], rhs=qkvT[:, GH + h, tt[d]], start=True, stop=True))
                        if use_o[d]:
                            heads(("qk", l, j, d), lambda o, h: pe.matmul(
                                o, lhsT=qkvT[:, GH + h, tt[d]], rhs=qkvT[:, h, tt[d]], start=True, stop=True))
                    if l == 0 and j:
                        ada_columns(("am", j), dTrow, ada_keys(j - 1))
                    for d in range(2):
                        evacuated(pe, ("kk", l, j, d))
                        heads(("at2", l, j, d), lambda o, h: pe.transpose(o, gY[d][:, h, :], ident[:, :]))
                    for n in range(1, LEVELS):
                        for d in range(2):
                            if n == 1:
                                pe.wait_ge(s["x1"], 2 * j + d + 1)
                            else:
                                for q in range(2):
                                    evacuated(pe, ("xx", l, j, d, n - 1, q))
                            pe.wait_ge(s["ml"], 2 * (j * (LEVELS - 1) + n - 1) + d + 1)
                            heads(("y", l, j, d, n), lambda o, h: pe.matmul(
                                o, lhsT=gML[d][:, h, :], rhs=gX[d][:, h, 0, :], start=True, stop=True))
                        if l == 0:
                            ada_later(0)
                        for d in range(2):
                            evacuated(pe, ("y", l, j, d, n))
                            for q in range(2):
                                key = ("xx", l, j, d, n, q)
                                b = claim(key)
                                for e in range(2):
                                    h = 2 * q + e
                                    if n < LEVELS - 1:
                                        pe.matmul(b[:, 2 * e * P:(2 * e + 1) * P], lhsT=gX[d][:, h, 1, :],
                                                  rhs=gY[d][:, h, :], start=True, stop=True)
                                    m = pe.matmul(b[:, (2 * e + 1) * P:(2 * e + 2) * P], lhsT=gY[d][:, h, :],
                                                  rhs=gX[d][:, h, 1, :], start=True, stop=True)
                                done(m, key)
                        if l == 0:
                            ada_later(1)
                    for d in range(2):
                        heads(("kr", l, j, d), lambda o, h: pe.transpose(o, qkvT[:, GH + h, tt[d]], ident[:, :]))
                        heads(("vr", l, j, d), lambda o, h: pe.transpose(o, qkvT[:, 2 * GH + h, tt[d]], ident[:, :]))
                    for d in range(2):
                        evacuated(pe, ("kr", l, j, d))
                        for q in range(2):
                            evacuated(pe, ("xx", l, j, d, LEVELS - 1, q))
                        heads(("wt", l, j, d), lambda o, h: pe.matmul(
                            o, lhsT=gAT[d][:, h, :], rhs=gX[d][:, h, 1, :], start=True, stop=True))
                    for d in range(2):
                        evacuated(pe, ("wt", l, j, d))
                        evacuated(pe, ("vr", l, j, d))
                        if j:
                            evacuated(pe, ("st", l, j - 1, d))
                        key = ("v", l, j, d)
                        b = claim(key)
                        for h in range(GH):
                            o = b[:, h * P:(h + 1) * P]
                            m = pe.matmul(o, lhsT=gX[d][:, h, 1, :], rhs=gY[d][:, h, :], start=True, stop=j == 0)
                            if j:
                                m = pe.matmul(o, lhsT=gML[d][:, h, :], rhs=S[:, d, h, :], start=False, stop=True)
                        done(m, key)
                    for d in range(2):
                        evacuated(pe, ("v", l, j, d))
                        if use_o[d]:
                            key = ("go", l, j, d)
                            b = claim(key)
                            if j:
                                pe.wait_ge(s["qg"], 2 * j + d + 1)
                            evacuated(pe, ("qk", l, j, d))
                            for h in range(GH):
                                o = b[:, h * P:(h + 1) * P]
                                if j:
                                    pe.matmul(o, lhsT=S[:, d, h, :], rhs=gQG[d][:, h, :], start=True, stop=False)
                                m = pe.matmul(o, lhsT=gY[d][:, h, :], rhs=gQK[d][:, h, :], start=j == 0, stop=True)
                            done(m, key)
                        if j < NT - 1:
                            heads(("st", l, j, d), lambda o, h: pe.matmul(
                                o, lhsT=gKD[d][:, h, :], rhs=gY[d][:, h, :], start=True, stop=True))

                if l == 0:
                    ada_columns(("am", NT), dTrow, ada_keys(NT - 1))
                    for n in range(ADA_GROUP * NT, len(ADA_LATER)):
                        ada_later(0)
                        ada_later(1)
                    ada_columns(("am", NT + 1), dTrow, ada_keys(NT))

                for h in range(GH):
                    pe.wait_ge(s["osq"], h + 1)
                    for g in segs:
                        t0, n = SEGS[g]
                        key = ("on", l, h, g)
                        b = claim(key)
                        done(pe.matmul(b[:, 0:n], lhsT=ones[:, :], rhs=sqb[:, h % 2, t0:t0 + n], start=True,
                                       stop=True), key)

                for c in range(2):
                    for g in segs:
                        evacuated(pe, ("pm", l, c, g))
                evacuated(pe, ("at", l, NT - 1))
                pe.wait_ge(s["mixd"], GH)
                for j in range(4):
                    w = weights(("out", l, j))
                    for c in range(2):
                        for g in segs:
                            t0, n = SEGS[g]
                            key = ("y", l, 2 * j + c, g)
                            b = claim(key)
                            for k in range(KD):
                                m = pe.matmul(b[:, 0:n], lhsT=w[:, k, c * P:(c + 1) * P], rhs=mixT[:, k, t0:t0 + n],
                                              start=k == 0, stop=k == KD - 1)
                            done(m, key)
                    last_use(None, ("y", l, 2 * j + 1, 1))

                sum_over_partitions(l, 2, "sq2", "sqd2")

                bs = [(g, claim(("rtT", l, g))) for g in segs]
                for k in range(KD):
                    pe.wait_ge(s["h2"], k + 1)
                    for g, b in bs:
                        t0, n = SEGS[g]
                        m = pe.matmul(b[0:N_EXP, 0:n], lhsT=router[:, k, :], rhs=hT[:, k, t0:t0 + n], start=k == 0,
                                      stop=k == KD - 1)
                        if k == KD - 1:
                            done(m, ("rtT", l, g))
                for g in segs:
                    evacuated(pe, ("rtT", l, g))
                token_rows(("rt", l), rtrow, tiles)
                for i in tiles:
                    for q in range(2):
                        key = ("hr", l, i, q)
                        b = claim(key)
                        for j in range(4):
                            m = pe.transpose(b[:, j * P:(j + 1) * P], hT[:, 4 * q + j, i * P:(i + 1) * P],
                                             ident[:, :])
                        done(m, key)
                pe.wait_ge(s["aff"], 1)
                for g in segs:
                    key = ("aT", l, g)
                    b = claim(key)
                    t0, n = SEGS[g]
                    for i in range(n // P):
                        m = pe.transpose(b[0:N_EXP, i * P:(i + 1) * P], aff[:, t0 // P + i, :], ident[:, :])
                    done(m, key)
                pe.wait_ge(s["sel"], len(segs))
                key = ("slot", l)
                b = claim(key)
                for i in tiles:
                    m = pe.transpose(b[:, i * N_EXP:(i + 1) * N_EXP], sel[0:N_EXP, i * P:(i + 1) * P],
                                     ident[0:N_EXP, 0:N_EXP])
                done(m, key)

                parts = [(0, range(CT, NT), 0, 8), (1, range(CT, NT), 8, 16)]
                if need_ctx:
                    parts.append((2, range(CT), 0, 16))
                bs = {x: claim(("mr", l, x)) for x, _, _, _ in parts}
                order = list(range(CT, NT)) + (list(range(CT)) if need_ctx else [])
                for x, ts, e0, e1 in parts:
                    for t in ts:
                        pe.wait_ge(s["G"], order.index(t) + 1)
                        g = G[t - CT] if t >= CT else G[SEQ // P + t]
                        m = pe.matmul(bs[x][0:NW, :], lhsT=tokaff[:, t, :],
                                      rhs=g[:, e0:e1, :].rearrange("p e c -> p (e c)"), start=t == ts[0],
                                      stop=t == ts[-1])
                    done(m, ("mr", l, x))
                for g in reversed(segs):
                    for x, _, _, _ in parts:
                        if (x < 2) == (g == 1):
                            evacuated(pe, ("mr", l, x))
                    key = ("mc", l, g)
                    b = claim(key)
                    n, c0 = (2 * CAP_L, 0) if g else (2 * CAP_C, N_EXP * CAP_L)
                    for p in range(PAIRS):
                        m = pe.transpose(b[0:n, p * NW:(p + 1) * NW], mrow[:, c0 + p * n:c0 + (p + 1) * n],
                                         ident[0:NW, 0:NW])
                    done(m, key)

                seq = ["%s%d%d" % (t, e, q) for e in range(2) for q in range(2) for t in ("g", "u")]
                seq += ["y00", "y01", "y10", "y11"] + ["x%d" % q for q in range(4)]
                seq += ["c%d%d" % (k, g) for k in range(KD) for g in reversed(segs)]
                n_cap = CAP if need_ctx else CAP_L

                def pair(claim_, done_, weights_, free_, here, i, nxt):
                    for e in range(2):
                        for q in range(2):
                            for t, name in enumerate("gu"):
                                w = weights_(4 * e + 2 * q + t, KD)
                                b = claim_("%s%d%d" % (name, e, q))
                                for f in range(2):
                                    for k in range(KD):
                                        m = pe.matmul(b[:, f * CAP:f * CAP + n_cap], lhsT=w[:, k, f * P:(f + 1) * P],
                                                      rhs=xs[:, k, e, 0:n_cap], start=k == 0, stop=k == KD - 1)
                                done_(m, "%s%d%d" % (name, e, q))
                                free_(None, "%s%d%d" % (name, e, q))
                    for e in range(2):
                        ys = [claim_("y%d%d" % (e, c)) for c in range(2)]
                        for q in range(2):
                            w = weights_(8 + 2 * e + q, 2)
                            evacuated(pe, here("u%d%d" % (e, q)), i)
                            for f in range(2):
                                for c in range(2):
                                    m = pe.matmul(ys[c][0:n_cap, :], lhsT=hid[:, e, 2 * q + f, 0:n_cap],
                                                  rhs=w[:, f, c * 512:(c + 1) * 512], start=q == 0 and f == 0,
                                                  stop=q == 1 and f == 1)
                                    if q == 1 and f == 1:
                                        done_(m, "y%d%d" % (e, c))
                            free_(m if q == 0 else None, None if q == 0 else "y%d1" % e)
                    if nxt is not None:
                        pe.wait_ge(s["gath"], nxt)
                        turn_tokens(claim_, done_)
                    for e in range(2):
                        for c in range(2):
                            evacuated(pe, here("y%d%d" % (e, c)), i)
                    pe.wait_ge(s["S"], plus(1, 1, i) if i is not None else PAIRS)
                    for k in range(KD):
                        for g in reversed(segs):
                            name = "c%d%d" % (k, g)
                            b = claim_(name)
                            if g:
                                m = pe.matmul(b[:, 0:SEQ], lhsT=ylat[:, k * P:(k + 1) * P], rhs=Sl[:, :], start=True,
                                              stop=True)
                            else:
                                m = pe.matmul(b[:, 0:CTX], lhsT=yctx[0:2 * CAP_C, k * P:(k + 1) * P],
                                              rhs=Sc[0:2 * CAP_C, :], start=True, stop=True)
                            done_(m, name)
                    if nxt is not None:
                        for q in range(4):
                            evacuated(pe, here("x%d" % q), i)

                def turn_tokens(claim_, done_):
                    for q in range(4):
                        b = claim_("x%d" % q)
                        for e in range(2):
                            k = 2 * q + e
                            o = b[:, e * 2 * CAP:(e + 1) * 2 * CAP]
                            m = pe.transpose(o[:, 0:2 * CAP_L], xlat[:, k * P:(k + 1) * P], ident[:, :])
                            if need_ctx:
                                m = pe.transpose(o[:, 2 * CAP_L:2 * CAP], xctx[0:2 * CAP_C, k * P:(k + 1) * P],
                                                 ident[0:2 * CAP_C, 0:2 * CAP_C])
                        done_(m, "x%d" % q)

                per_pair = 16 * len(segs)
                pe.wait_ge(s["gath"], per_pair)
                turn_tokens(lambda name: claim(("first", l, name)), lambda m, name: done(m, ("first", l, name)))
                for q in range(4):
                    evacuated(pe, ("first", l, "x%d" % q))

                per = [0] * BANKS
                for n in range(len(seq)):
                    per[(turn[0] + n) % BANKS] += 1
                seen = [0] * BANKS
                for n, name in enumerate(seq):
                    b = (turn[0] + n) % BANKS
                    where[("moe", l, name)] = (b, uses[b] + seen[b], per[b])
                    seen[b] += 1
                r0 = len(loads)

                with pe.Fori(0, PAIRS - 1) as i:
                    def claim2(name):
                        b, n, per = where[("moe", l, name)]
                        pe.wait_ge(bank_free[b], i * per + n)
                        return psum[:, b, :]

                    def done2(ins, name):
                        ins.then_inc(bank_full[where[("moe", l, name)][0]], 1)

                    def weights2(n, k):
                        m = r0 + n
                        pe.wait_ge(slot_full[m % SLOTS], i * (16 * 12 // SLOTS) + 16 * (m // SLOTS + 1))
                        return ring[:, m % SLOTS, :].rearrange("p (k c) -> p k c", k=k)

                    def free2(ins, name):
                        if ins is not None:
                            ins.then_inc(slot_used, 1)

                    pair(claim2, done2, weights2, free2, lambda name: ("moe", l, name), i,
                         i * per_pair + 2 * per_pair)
                for b in range(BANKS):
                    uses[b] += (PAIRS - 1) * per[b]
                for i in range(PAIRS - 1):
                    for n in range(12):
                        e, m = expert_part(n)
                        loads.append(("moe", l, 2 * i + e, m))
                        if m == 4:
                            freed[0] += 1
                            freed_by.append(freed[0])
                        else:
                            name = "y%d1" % e if m == 5 else "%s%d%d" % ("gu"[m % 2], e, m // 2)
                            freed_by.append((("moe", l, name), i))

                def weights1(n, k):
                    e, m = expert_part(n)
                    w = weights(("moe", l, N_EXP - 2 + e, m))
                    return w.rearrange("p k c -> p (k c)").rearrange("p (k c) -> p k c", k=k)

                def last(name):
                    return ("last", l, name)

                pair(lambda name: claim(last(name)), lambda m, name: done(m, last(name)), weights1,
                     lambda m, name: last_use(m, last(name) if name else None), last, None, None)

            evacuated(pe, ("last", DEPTH - 1, "c%d1" % (KD - 1)))
            for i in range(CT, NT):
                for q in range(2):
                    key = ("out", i, q)
                    b = claim(key)
                    for j in range(4):
                        m = pe.transpose(b[:, j * P:(j + 1) * P], xT[:, 4 * q + j, i * P:(i + 1) * P], ident[:, :])
                    done(m, key)

        @block.sync
        def _(sp):
            sp.dma_start(big[:, 0:CT * D].rearrange("p (i d) -> p i d", i=CT),
                         A["ctx"][0].rearrange("(i p) d -> p i d", p=P)).then_inc(s_xin, 16)
            sp.dma_start(big[:, CT * D:NT * D].rearrange("p (i d) -> p i d", i=NT - CT),
                         A["x"][0].rearrange("(i p) d -> p i d", p=P)).then_inc(s_xin, 16)

            def slot(n, k, c):
                return ring[:, n % SLOTS, :].rearrange("p (k c) -> p k c", k=k)[:, :, 0:c]

            def slot_free(n):
                if n >= SLOTS:
                    how = freed_by[n - SLOTS]
                    if isinstance(how, int):
                        sp.wait_ge(slot_used, how)
                    else:
                        product_ready(sp, how[0], how[1])

            def columns(n, src, c0, c1):
                slot_free(n)
                sp.dma_start(slot(n, KD, c1 - c0), src.rearrange("(k p) c -> p k c", p=P)[:, :, c0:c1]
                             ).then_inc(slot_full[n % SLOTS], 16)

            def expert(n, l, e, m):
                if m < 4:
                    w = A["moe_w_gate"] if m % 2 == 0 else A["moe_w_up"]
                    c0 = (m // 2) * SLOT_COLS
                    src = w[l, e].rearrange("(k p) f -> p k f", p=P)[:, :, c0:c0 + SLOT_COLS]
                    dst = slot(n, KD, SLOT_COLS)
                else:
                    src = A["moe_w_down"][l, e].rearrange("(k p) d -> p k d", p=P)[:, 2 * (m - 4):2 * (m - 4) + 2, :]
                    dst = slot(n, 2, D)
                sp.dma_start(dst, src).then_inc(slot_full[n % SLOTS], 16)

            n = 0
            for l in range(DEPTH):
                while loads[n][0] in ("ada", "in", "out"):
                    kind, m, g = loads[n]
                    if kind == "in":
                        columns(n, A["w_in"][m], *IN_LOADS[g][1:])
                    else:
                        columns(n, A["ada_w" if kind == "ada" else "w_out"][m], g * SLOT_COLS, (g + 1) * SLOT_COLS)
                    n += 1
                for m in range(6):
                    slot_free(n + m)
                    expert(n + m, l, *expert_part(m))
                with sp.Fori(0, PAIRS - 1) as i:
                    for m in range(12):
                        if m != 4:
                            how = freed_by[n + (4 if m == 3 else m)]
                            if isinstance(how, int):
                                sp.wait_ge(slot_used, i * 2 + how)
                            else:
                                product_ready(sp, how[0], i)
                        e, part = expert_part((m + 6) % 12)
                        expert(n + 6 + m, l, 2 * i + (e + 2 if m >= 6 else e), part)
                n += 12 * (PAIRS - 1)
                for m in range(6, 12):
                    slot_free(n + m)
                    e, part = expert_part(m)
                    expert(n + m, l, N_EXP - 2 + e, part)
                n += 12
            assert n == len(loads)
            orow = big[:, 0:(NT - CT) * D].rearrange("p (i d) -> p i d", i=NT - CT)
            for i in range(NT - CT):
                for q in range(2):
                    evacuated(sp, ("out", CT + i, q))
                sp.dma_start(out[0, i * P:(i + 1) * P, :], orow[:, i, :]).then_inc(s_out, 16)
            sp.wait_ge(s_out, 16 * (NT - CT))

        @block.scalar
        def _(act):
            for dst, name in ((ident[:, :], "k_ident"), (tri[:, :, :], "k_tri"), (lev[:, :, :, :], "k_lev"),
                              (iota[:, :], "k_iota"), (rope[:, :, :, :], "k_rope"), (poolc[:, :, :], "k_pool")):
                act.dma_start(dst, A[name]).then_inc(s_const, 16)
            act.dma_start(arena[0:8, 11 * T:11 * T + P], A["c"].rearrange("b (k p) -> (b k) p", p=P)).then_inc(s_const, 16)
            act.dma_start(arena[8:16, 11 * T:11 * T + P], A["c_ctx"].rearrange("(k p) -> k p", p=P)).then_inc(s_const, 16)

            act.wait_ge(sems[0]["zero"], 1)
            channel_parameters(act, 0)

            def squares(l, which, k):
                s = sems[l]
                t0 = 0 if which == 1 or l == 0 else CTX
                if k >= 2:
                    act.wait_ge(s["sqd%d" % which], k - 1)
                act.activation(sqb[:, k % 2, t0:T], xT[:, k, t0:T], ACT.Square).then_inc(s["sq%d" % which], 1)

            def inverse_roots(l, dst, keys, bias, scale):
                for key in keys:
                    t0, n = SEGS[key[-1]]
                    b = product_ready(act, key)
                    read_out(act.activation(dst[:, t0:t0 + n], b[:, 0:n], ACT.Ln, bias=bias, scale=scale), key)
                for key in keys:
                    evacuated(act, key)
                t0 = min(SEGS[key[-1]][0] for key in keys)
                act.activation(dst[:, t0:T], dst[:, t0:T], ACT.Exp, scale=-0.5).then_inc(sems[l]["rinv"], 1)

            def ada_rows(row, keys):
                for n, key in enumerate(keys):
                    b = product_ready(act, key)
                    read_out(act.copy(row[0:2, n * SLOT_COLS:(n + 1) * SLOT_COLS], b[0:2, 0:SLOT_COLS]), key)

            def ada_group(group):
                key = ("am", group + 1)
                m0 = 2 * (ADA_FIRST + group * ADA_GROUP)
                n = 2 * len(ada_keys(group))
                b = product_ready(act, key)
                read_out(act.copy(modraw[:, m0:m0 + n, :].rearrange("p m c -> p (m c)"), b[:, 0:2 * n]), key)

            def norm(l, which):
                s = sems[l]
                segs = (1, 0) if which == 1 or l == 0 else (1,)
                inverse_roots(l, rstd, [("ss", l, which, g) for g in segs], eps[:, 0:1], 1.0 / D)
                if l == 0 and which == 1:
                    ada_rows(szrow, [("ar", 0, g) for g in range(ADA_FIRST)])
                act.wait_ge(s["mods%d" % which], 1)
                for k in range(KD):
                    act.wait_ge(s["hx%d" % which], k + 1)
                    for g in segs:
                        t0, n = SEGS[g]
                        c = 1 - g
                        m = act.activation(hT[:, k, t0:t0 + n], hT[:, k, t0:t0 + n], ACT.Identity,
                                           bias=mods_of[l][:, (0 if which == 1 else 3) * KD + k, c:c + 1],
                                           scale=amod_of[l][:, which - 1, k, c:c + 1])
                    m.then_inc(s["h%d" % which], 1)

            def narrow(l, name, dst, gs):
                for g in gs:
                    t0, n = SEGS[g]
                    key = ("in", l, name, g) if name != "rtT" else ("rtT", l, g)
                    b = product_ready(act, key)
                    read_out(act.copy(dst[:, t0:t0 + n], b[0:dst.shape[0], 0:n]), key)

            act.wait_ge(s_ones, 1)
            for k in range(KD):
                b = product_ready(act, ("x", k, 1))
                read_out(act.copy(xT[:, k, 512:T], b[:, 0:256]), ("x", k, 1))
            b = product_ready(act, "c")
            read_out(act.activation(scol[:, :, :].rearrange("p a b -> p (a b)"), b[:, 0:16], ACT.Silu), "c")

            for l in range(DEPTH):
                s = sems[l]
                need_ctx = l < DEPTH - 1
                tiles = range(NT) if need_ctx else range(CT, NT)
                segs = (0, 1) if need_ctx else (1,)
                t_first = tiles[0] * P

                if l == 0:
                    for k in range(KD):
                        evacuated(act, ("x", k, 0))
                        evacuated(act, ("x", k, 1))
                        squares(l, 1, k)
                else:
                    for k in range(KD):
                        for g in (0, 1):
                            evacuated(act, ("last", l - 1, "c%d%d" % (k, g)))
                        squares(l, 1, k)
                norm(l, 1)

                act.wait_ge(s["upad"], 1)
                for c in range(2):
                    for g in segs:
                        key = ("in", l, "pool%d" % c, g)
                        b = product_ready(act, key)
                        n = SEGS[g][1]
                        read_out(act.copy(U[:, c, UO[g]:UO[g] + n], b[:, 0:n]), key)
                narrow(l, "ab", abrow, (0, 1))
                for name, dst, m, gs in (("ql0", SQ0, P, segs), ("ql1", SQ1, 64, segs), ("kv", SQK, P, (0, 1))):
                    for g in gs:
                        t0, n = SEGS[g]
                        b = product_ready(act, ("in", l, name, g))
                        act.activation(dst[0:m, t0:t0 + n], b[0:m, 0:n], ACT.Square).then_inc(s["sqm"], 1)
                narrow(l, "krp", krow, (0, 1))
                b = product_ready(act, ("rs", l))[:, 0:2 * NT].rearrange("p (i w) -> p i w", w=2)
                act.activation(rs12[:, tiles[0]:NT, 0:1], b[:, tiles[0]:NT, 0:1], ACT.Sqrt, bias=eps[:, 0:1],
                               scale=1.0 / Q_LORA)
                read_out(act.activation(rs12[:, :, 1:2], b[:, :, 1:2], ACT.Sqrt, bias=eps[:, 0:1],
                                        scale=1.0 / KV_LORA), ("rs", l))
                b = product_ready(act, ("krp", l))
                read_out(act.copy(krp.rearrange("p i c -> p (i c)"), b[:, 0:NT * ROPE]), ("krp", l))

                jobs = [("k", i) for i in range(NT)] + [("q", i) for i in tiles]

                def turned(n):
                    kind, i = jobs[n]
                    key = (kind + "t", l, i)
                    b = product_ready(act, key)
                    dst = (KT if kind == "k" else QT)[0:QK, :, i * P:(i + 1) * P]
                    read_out(act.copy(dst, b[0:QK, :].rearrange("p (h c) -> p h c", h=H)), key)

                def middle_tap(m):
                    for g in (0, 1):
                        t0, w = SEGS[g]
                        b = product_ready(act, ("in", l, "qkv%d" % m, g))
                        cc = COL_CONV + 12 + m
                        act.activation(qkvT[:, m, t0:t0 + w], b[:, 0:w], ACT.Copy, scale=cols[:, cc:cc + 1]
                                       ).then_inc(s["cv1"], 1)

                def silu(m):
                    for g in (0, 1):
                        t0, w = SEGS[g]
                        evacuated(act, ("in", l, "qkv%d" % m, g))
                        act.activation(qkvT[:, m, t0:t0 + w], qkvT[:, m, t0:t0 + w], ACT.Silu).then_inc(s["qkv"], 1)

                for n in range(len(jobs)):
                    act.wait_ge(s["row1"], n + 1)
                    act.activation(ss4[:, n % 2, :], ss4[:, n % 2, :], ACT.Sqrt, bias=eps[:, 0:1],
                                   scale=1.0 / QK).then_inc(s["rowr"], 1)
                    if n:
                        turned(n - 1)
                    if n % 2 == 0 and n:
                        if n == 2:
                            act.wait_ge(s["pool"], 2)
                        middle_tap(n // 2 - 1)
                turned(len(jobs) - 1)
                middle_tap(len(jobs) // 2 - 1)

                act.wait_ge(s["abraw"], 1)
                act.activation(abe[:, :, :], abe[:, :, :], ACT.Exp, scale=-1.0).then_inc(s["abexp"], 1)
                act.activation(abw[:, 1, :, :], abw[:, 1, :, :], ACT.Exp, scale=-1.0)
                act.activation(ealog, gpar[:, 0, :], ACT.Exp)
                act.wait_ge(s["abexp"], 1)
                act.activation(abe[:, :, :], abe[:, :, :], ACT.Ln, bias=ones[:, 0:1]).then_inc(s["abln"], 1)

                silus = 0
                for m in range(len(jobs) // 2, 12):
                    middle_tap(m)
                    while silus < min(m, 2 * (m - len(jobs) // 2 + 1)):
                        silu(silus)
                        silus += 1
                while silus < 12:
                    silu(silus)
                    silus += 1
                for m in range(4):
                    for g in segs:
                        t0, n = SEGS[g]
                        b = product_ready(act, ("in", l, "z%d" % m, g))
                        read_out(act.activation(szT[:, m, t0:t0 + n], b[:, 0:n], ACT.Silu), ("in", l, "z%d" % m, g))

                calls = [(i, h) for i in tiles for h in range(H)]

                def turned_att(i):
                    b = product_ready(act, ("at", l, i))
                    read_out(act.copy(mixT[:, 0:2, i * P:(i + 1) * P],
                                      b[:, 0:2 * P].rearrange("p (c t) -> p c t", c=2)), ("at", l, i))

                for n, (i, h) in enumerate(calls):
                    parts = (CT,) if i < CT else (4, 2)
                    act.wait_ge(s["nm"], n + 1)
                    if n:
                        pi, ph = calls[n - 1]
                        product_ready(act, ("pt", l, pi, ph, 0 if pi < CT else 1))
                    if h == 0 and i - tiles[0] >= 2:
                        evacuated(act, ("o", l, i - 2))
                    k0 = 0
                    for part, nk in enumerate(parts):
                        key = ("s", l, i, h, part)
                        b = product_ready(act, key)
                        read_out(act.activation(PR[:, k0 * P:(k0 + nk) * P], b[:, 0:nk * P], ACT.Exp,
                                                bias=nm[:, n % 2:n % 2 + 1], scale=QK ** -0.5,
                                                accum_out=sm[:, i % 2, h, part:part + 1]), key)
                        k0 += nk
                    if h == 0 and n:
                        turned_att(i - 1)
                    if len(parts) == 2:
                        key = ("pt", l, i, h, 1)
                        b = product_ready(act, key)
                        if n:
                            attended(act, l, calls, n - 1)
                        read_out(act.copy(PT[:, 4:6, :].rearrange("p j c -> p (j c)"), b[:, 0:2 * P]), key)
                turned_att(NT - 1)

                product_ready(act, ("o", l, NT - 1))

                def lsquare(c):
                    if c >= 2:
                        product_ready(act, ("ln", l, c - 2, 1))
                    act.activation(sqb[:, c % 2, :], qkvT[:, c, :], ACT.Square).then_inc(s["lsq"], 1)

                act.wait_ge(s["qkv"], 24)
                lsquare(0)
                lsquare(1)
                for c in range(2 * GH):
                    if c >= 2:
                        act.wait_ge(s["lmul"], c - 1)
                    q = c < GH
                    inverse_roots(l, rs_gdn[:, c % 2, :], [("ln", l, c, g) for g in (0, 1)],
                                  eps[:, 1:2] if q else eps[:, 0:1], 128.0 if q else 1.0)
                    if c + 2 < 2 * GH:
                        lsquare(c + 2)

                evacuated(act, ("gc", l))
                act.activation(bg[:, :, :, :], gc[:, :, :, :], ACT.Exp).then_inc(s["egc"], 1)

                for j in range(NT):
                    ti = [tile_of(d, j) for d in range(2)]
                    use_o = [need_ctx or i >= CT for i in ti]
                    for d in range(2):
                        b = product_ready(act, ("g", l, j, d))
                        if j and (need_ctx or tile_of(d, j - 1) >= CT):
                            product_ready(act, ("go", l, j - 1, d))
                        act.wait_ge(s["xg"], 2 * j + d + 1)
                        read_out(act.activation(gQG[d].rearrange("p h c -> p (h c)"), b, ACT.Exp), ("g", l, j, d))
                        act.wait_ge(s["dcl"], 2 * j + d + 1)
                        act.activation(gD[d], gD[d], ACT.Exp, scale=-1.0)
                        act.activation(gQK[d], gQK[d], ACT.Exp)
                        act.activation(gt4[:, d, :, :], gt4[:, d, :, :], ACT.Exp).then_inc(s["dex"], 1)
                    for d in range(2):
                        b = product_ready(act, ("at2", l, j, d))
                        read_out(act.copy(gAT[d].rearrange("p h c -> p (h c)"), b), ("at2", l, j, d))
                    for n in range(1, LEVELS):
                        if l == 0 and n == 1 and j:
                            ada_group(j - 1)
                        if l == 0 and n > 1:
                            ada_rows(dTrow[:, (n - 2) * SLOT_COLS:], ada_keys(j)[n - 2:n - 1])
                        for d in range(2):
                            key = ("xx", l, j, d, n, 0)
                            b = product_ready(act, key).rearrange("p (e x c) -> p e x c", e=2, x=2)
                            x0 = 0 if n < LEVELS - 1 else 1
                            read_out(act.copy(gX[d][:, 0:2, x0:2, :], b[:, :, x0:2, :]), key)
                    if l == 0:
                        ada_rows(dTrow[:, (LEVELS - 2) * SLOT_COLS:], ada_keys(j)[LEVELS - 2:LEVELS - 1])
                    for d in range(2):
                        b = product_ready(act, ("wt", l, j, d))
                        read_out(act.mul(gML[d].rearrange("p h c -> p (h c)"), b, -1.0), ("wt", l, j, d))

                if l == 0:
                    ada_group(NT - 1)
                    ada_rows(dTrow, ada_keys(NT))
                    ada_group(NT)

                for d in range(2):
                    evacuated(act, ("go", l, NT - 1, d))

                def osquare(h):
                    if h >= 2:
                        product_ready(act, ("on", l, h - 2, 1))
                    act.activation(sqb[:, h % 2, t_first:T], mixT[:, 2 + h, t_first:T], ACT.Square
                                   ).then_inc(s["osq"], 1)

                osquare(0)
                osquare(1)
                for h in range(GH):
                    if h >= 2:
                        act.wait_ge(s["mixd"], h - 1)
                    inverse_roots(l, rs_gdn[:, h % 2, :], [("on", l, h, g) for g in segs], eps[:, 0:1], 1.0 / P)
                    if h + 2 < GH:
                        osquare(h + 2)

                for k in range(KD):
                    for g in segs:
                        evacuated(act, ("y", l, k, g))
                    squares(l, 2, k)
                norm(l, 2)

                narrow(l, "rtT", rtrow, segs)
                act.wait_ge(s["rmax"], 1)
                act.activation(aff[:, tiles[0]:NT, :], aff[:, tiles[0]:NT, :], ACT.Exp).then_inc(s["rexp"], 1)
                for i in tiles:
                    b = product_ready(act, ("hr", l, i, 0))
                    read_out(act.copy(hrow[:, i, 0:512], b), ("hr", l, i, 0))

                for g in segs:
                    t0, n = SEGS[g][0] // P, SEGS[g][1] // P
                    for i in range(t0, t0 + n):
                        evacuated(act, ("hr", l, i, 0))
                        evacuated(act, ("hr", l, i, 1))
                    act.dma_start(hD[g].rearrange("(i p) d -> p i d", p=P), hrow[:, t0:t0 + n, :]
                                  ).then_inc(s["hrow"], 16)
                for x in range(3 if need_ctx else 2):
                    b = product_ready(act, ("mr", l, x))
                    read_out(act.copy(mrow[:, x * 512:(x + 1) * 512], b[0:NW, :]), ("mr", l, x))

                n_cap = CAP if need_ctx else CAP_L

                def tokens(name_of, i):
                    for q in (0, 2):
                        key = name_of("x%d" % q)
                        b = product_ready(act, key, i)[:, 0:4 * CAP].rearrange("p (k c) -> p k c", k=2)
                        copy_slots(act.copy, b, xs, q, need_ctx, lambda m: read_out(m, key))

                def pair(here, i, nxt):
                    for e in range(2):
                        for q in range(2):
                            key = here("g%d%d" % (e, q))
                            b = product_ready(act, key, i)[:, 0:2 * CAP].rearrange("p (f c) -> p f c", f=2)
                            if e:
                                evacuated(act, here("u0%d" % q), i)
                            read_out(act.activation(sg[:, q, :, 0:n_cap], b[:, :, 0:n_cap], ACT.Silu), key)
                    for e in range(2):
                        key = here("y%d0" % e)
                        b = product_ready(act, key, i)
                        m = act.copy(ylat[e * CAP_L:(e + 1) * CAP_L, 0:512], b[0:CAP_L, :])
                        if need_ctx:
                            m = act.copy(yctx[e * CAP_C:(e + 1) * CAP_C, 0:512], b[CAP_L:CAP, :])
                        read_out(m, key)
                    if nxt:
                        tokens(here, i)

                tokens(lambda name: ("first", l, name), None)
                with act.Fori(0, PAIRS - 1) as i:
                    pair(lambda name: ("moe", l, name), i, True)
                pair(lambda name: ("last", l, name), None, False)

            orow = big[:, 0:(NT - CT) * D].rearrange("p (i d) -> p i d", i=NT - CT)
            for i in range(CT, NT):
                b = product_ready(act, ("out", i, 0))
                read_out(act.copy(orow[:, i - CT, 0:512], b), ("out", i, 0))

        @block.vector
        def _(dve):
            chain = [0, 0]

            def link(ins, l):
                chain[l] += 1
                ins.then_inc(sems[l]["dve"], 1)
                dve.wait_ge(sems[l]["dve"], chain[l])

            def norm(l, which):
                s = sems[l]
                segs = (1, 0) if which == 1 or l == 0 else (1,)
                t0 = 0 if len(segs) == 2 else CTX
                dve.wait_ge(s["rinv"], 1 if which == 1 else 2 + 3 * GH)
                for k in range(KD):
                    dve.tensor_tensor(hT[:, k, t0:T], xT[:, k, t0:T], rstd[:, t0:T], ALU.mult
                                      ).then_inc(s["hx%d" % which], 1)

            def modulation(l, part):
                m0, m1 = ((0, 2 * KD), (2 * KD, 6 * KD))[part]
                x = mods_of[l][:, m0:m1, :]
                link(dve.tensor_tensor(x, x, cols[:, m0:m1].unsqueeze(2).to_broadcast([P, m1 - m0, 2]), ALU.add), l)
                m0, c0 = ((KD, COL_N1), (4 * KD, COL_N2))[part]
                dve.scalar_tensor_tensor(
                    out=amod_of[l][:, part, :, :], in0=mods_of[l][:, m0:m0 + KD, :], scalar=1.0,
                    in1=cols[:, c0:c0 + KD].unsqueeze(2).to_broadcast([P, KD, 2]), op0=ALU.add,
                    op1=ALU.mult).then_inc(sems[l]["mods%d" % (part + 1)], 1)

            for k in range(KD):
                b = product_ready(dve, ("x", k, 0))
                read_out(dve.tensor_copy(xT[:, k, 0:512], b), ("x", k, 0))

            for l in range(DEPTH):
                s = sems[l]
                need_ctx = l < DEPTH - 1
                tiles = range(NT) if need_ctx else range(CT, NT)
                segs = (0, 1) if need_ctx else (1,)
                i0 = tiles[0]
                t_first = i0 * P

                b = product_ready(dve, ("cols", l))
                read_out(dve.tensor_copy(cols[:, :], b[:, 0:N_COLS]), ("cols", l))
                evacuated(dve, ("cols", l))
                if l == 0:
                    norm(l, 1)
                    b = product_ready(dve, ("am", 0))
                    read_out(dve.tensor_copy(modraw[:, 0:2 * ADA_FIRST, :].rearrange("p m c -> p (m c)"),
                                             b[:, 0:4 * ADA_FIRST]), ("am", 0))
                    evacuated(dve, ("am", 0))
                    modulation(0, 0)
                else:
                    evacuated(dve, ("am", ADA_GROUPS))
                    modulation(l, 0)
                    modulation(l, 1)
                    norm(l, 1)

                b = product_ready(dve, ("ab", l))[:, 0:NT * 16].rearrange("p (i c) -> p i c", i=NT)
                dve.wait_ge(s["par"], 16 * PAR_DMAS)
                link(dve.tensor_tensor(abw[:, 0, :, :], b[:, :, 0:8], gpar[:, 1, :].unsqueeze(1).to_broadcast(
                    [P, NT, 8]), ALU.add), l)
                read_out(dve.tensor_copy(abw[:, 1, :, :], b[:, :, 8:16]), ("ab", l))
                evacuated(dve, ("ab", l))
                dve.scalar_tensor_tensor(out=abe[:, :, :], in0=abw[:, 0, :, :], scalar=-1.0, in1=abw[:, 0, :, :],
                                         op0=ALU.mult, op1=ALU.max).then_inc(s["abraw"], 1)

                n = 0
                for name, dst, m, c, gs in (("ql0", QG0, P, COL_Q, segs), ("ql1", QG1, 64, COL_Q + 1, segs),
                                            ("kv", KVG, P, COL_KV, (0, 1))):
                    for g in gs:
                        t0, w = SEGS[g]
                        n += 1
                        b = product_ready(dve, ("in", l, name, g))
                        dve.wait_ge(s["sqm"], n)
                        read_out(dve.tensor_scalar(dst[0:m, t0:t0 + w], b[0:m, 0:w], cols[0:m, c:c + 1], None,
                                                   ALU.mult), ("in", l, name, g))
                evacuated(dve, ("rs", l))
                link(dve.reciprocal(rs12[:, :, 1:2], rs12[:, :, 1:2]), l)
                link(dve.reciprocal(rs12[:, i0:NT, 0:1], rs12[:, i0:NT, 0:1]), l)
                evacuated(dve, ("krp", l))

                jobs = [("k", i) for i in range(NT)] + [("q", i) for i in tiles]

                def scale_rows(n):
                    kind, i = jobs[n]
                    key = (kind, l, i)
                    r = rows[:, n % 2, :, :]
                    b = product_ready(dve, key)
                    if n >= 2:
                        pk, pi = jobs[n - 2]
                        product_ready(dve, (pk + "t", l, pi))
                    if kind == "q":
                        read_out(dve.tensor_scalar(r, b[:, 0:H * QK].rearrange("p (h c) -> p h c", h=H),
                                                   rs12[:, i, 0:1], None, ALU.mult), key)
                    else:
                        v = b.rearrange("p (h c) -> p h c", h=H)
                        dve.tensor_scalar(V[:, i, :].rearrange("p (h c) -> p h c", h=H), v[:, :, NOPE:NOPE + DV],
                                          rs12[:, i, 1:2], None, ALU.mult)
                        link(dve.tensor_copy(r[:, :, NOPE:QK], krp[:, i, :].unsqueeze(1).to_broadcast([P, H, ROPE])),
                             l)
                        read_out(dve.tensor_scalar(r[:, :, 0:NOPE], v[:, :, 0:NOPE], rs12[:, i, 1:2], None, ALU.mult),
                                 key)
                    evacuated(dve, key)
                    link(dve.tensor_tensor(rtmp, r, r, ALU.mult), l)
                    dve.tensor_reduce(ss4[:, n % 2, :], rtmp, AX.X, ALU.add).then_inc(s["row1"], 1)

                def norm_rows(n):
                    dve.wait_ge(s["rowr"], n + 1)
                    link(dve.reciprocal(ss4[:, n % 2, :], ss4[:, n % 2, :]), l)
                    r = rows[:, n % 2, :, :]
                    dve.tensor_tensor(r, r, ss4[:, n % 2, :].unsqueeze(2).to_broadcast([P, H, QK]), ALU.mult
                                      ).then_inc(s["rowa"], 1)

                def outer_taps(m):
                    for g in (0, 1):
                        t0, n = SEGS[g]
                        key = ("in", l, "qkv%d" % m, g)
                        b = product_ready(dve, key)
                        dve.wait_ge(s["cv1"], 2 * m + g + 1)
                        a = qkvT[:, m, t0 + 1:t0 + n]
                        link(dve.scalar_tensor_tensor(out=a, in0=b[:, 0:n - 1], scalar=cols[:, COL_CONV + m:
                                                      COL_CONV + m + 1], in1=a, op0=ALU.mult, op1=ALU.add), l)
                        a = qkvT[:, m, t0:t0 + n - 1]
                        cc = COL_CONV + 24 + m
                        read_out(dve.scalar_tensor_tensor(out=a, in0=b[:, 1:n], scalar=cols[:, cc:cc + 1], in1=a,
                                                          op0=ALU.mult, op1=ALU.add), key)

                scale_rows(0)
                for n in range(len(jobs)):
                    if n + 1 < len(jobs):
                        scale_rows(n + 1)
                    norm_rows(n)
                    if n % 2 == 0 and n:
                        outer_taps(n // 2 - 1)
                outer_taps(len(jobs) // 2 - 1)

                dve.wait_ge(s["abln"], 1)
                link(dve.scalar_tensor_tensor(out=abe[:, :, :], in0=abw[:, 0, :, :], scalar=0.0, in1=abe[:, :, :],
                                              op0=ALU.max, op1=ALU.add), l)
                dve.scalar_tensor_tensor(out=gb[:, 0, :, :], in0=abe[:, :, :], scalar=-1.0,
                                         in1=ealog.unsqueeze(1).to_broadcast([P, NT, 8]), op0=ALU.mult, op1=ALU.mult)
                link(dve.tensor_scalar(abw[:, 1, :, :], abw[:, 1, :, :], 1.0, None, ALU.add), l)
                dve.reciprocal(gb[:, 1, :, :], abw[:, 1, :, :]).then_inc(s["gbd"], 1)

                for m in range(len(jobs) // 2, 12):
                    outer_taps(m)

                for c in range(2):
                    for g in segs:
                        t0, n = SEGS[g]
                        b = product_ready(dve, ("pm", l, c, g))
                        read_out(dve.tensor_scalar(mixT[:, 6 + c, t0:t0 + n], b[:, 0:n],
                                                   cols[:, COL_PS + c:COL_PS + c + 1], None, ALU.mult),
                                 ("pm", l, c, g))

                calls = [(i, h) for i in tiles for h in range(H)]

                def row_max(n):
                    i, h = calls[n]
                    parts = (CT,) if i < CT else (4, 2)
                    if n >= 2:
                        pi, ph = calls[n - 2]
                        for part in range(1 if pi < CT else 2):
                            evacuated(dve, ("s", l, pi, ph, part))
                    for part, nk in enumerate(parts):
                        b = product_ready(dve, ("s", l, i, h, part))
                        link(dve.reduce_max(mx[:, n % 2, part:part + 1], b[:, 0:nk * P], AX.X), l)
                    w = len(parts) - 1
                    dve.tensor_scalar(nm[:, n % 2:n % 2 + 1], mx[:, n % 2, 0:1], mx[:, n % 2, w:w + 1],
                                      -(QK ** -0.5), ALU.max, ALU.mult).then_inc(s["nm"], 1)

                row_max(0)
                for n, (i, h) in enumerate(calls):
                    if n + 1 < len(calls):
                        row_max(n + 1)
                    nk = CT if i < CT else 4
                    key = ("pt", l, i, h, 0)
                    b = product_ready(dve, key)
                    if n:
                        attended(dve, l, calls, n - 1)
                    read_out(dve.tensor_copy(PT[:, 0:nk, :].rearrange("p j c -> p (j c)"), b[:, 0:nk * P]), key)
                    if h == H - 1:
                        if i >= CT:
                            link(dve.tensor_tensor(rden, sm[:, i % 2, :, 0], sm[:, i % 2, :, 1], ALU.add), l)
                        else:
                            link(dve.tensor_copy(rden, sm[:, i % 2, :, 0]), l)
                        link(dve.reciprocal(rden, rden), l)
                        if i > i0:
                            product_ready(dve, ("at", l, i - 1))
                        b = product_ready(dve, ("o", l, i))
                        read_out(dve.tensor_tensor(att.rearrange("p (h c) -> p h c", h=H), b[:, 0:H * DV].rearrange(
                            "p (h c) -> p h c", h=H), rden.unsqueeze(2).to_broadcast([P, H, DV]), ALU.mult),
                            ("o", l, i))

                for c in range(2 * GH):
                    dve.wait_ge(s["rinv"], 2 + c)
                    dve.tensor_tensor(qkvT[:, c, :], qkvT[:, c, :], rs_gdn[:, c % 2, :], ALU.mult
                                      ).then_inc(s["lmul"], 1)

                b = product_ready(dve, ("gc", l))
                read_out(dve.tensor_copy(gc.rearrange("p d i h -> p (d i h)"), b[:, 0:2 * NT * GH]), ("gc", l))
                dve.wait_ge(s["egc"], 1)
                for d in range(2):
                    link(dve.tensor_tensor(bg[:, d, :, :], bg[:, d, :, :], gb[:, 1, :, d * GH:(d + 1) * GH],
                                           ALU.mult), l)

                for j in range(NT):
                    ti = [tile_of(d, j) for d in range(2)]
                    tt = [slice(i * P, (i + 1) * P) for i in ti]
                    use_o = [need_ctx or i >= CT for i in ti]
                    for d in range(2):
                        b = product_ready(dve, ("g", l, j, d)).rearrange("p (h c) -> p h c", h=GH)
                        g1 = gc[:, d, ti[d], :]
                        if j:
                            evacuated(dve, ("st", l, j - 1, d))
                        dve.tensor_tensor(gAT[d], b, g1.unsqueeze(2).to_broadcast([P, GH, P]), ALU.subtract)
                        last = P - 1 if d == 0 else 0
                        dve.tensor_tensor(gt4[:, d, 0, :], b[:, :, last], g1, ALU.subtract)
                        dve.tensor_copy(gt4[:, d, 1, :], b[:, :, last]).then_inc(s["xg"], 1)
                    for d in range(2):
                        key = ("kk", l, j, d)
                        b = product_ready(dve, key)
                        dve.wait_ge(s["dm"], 2 * j + d + 1)
                        if j:
                            product_ready(dve, ("st", l, j - 1, d))
                        read_out(dve.tensor_tensor(gY[d].rearrange("p h c -> p (h c)"), b,
                                                   gD[d].rearrange("p h c -> p (h c)"), ALU.mult), key)
                        if use_o[d]:
                            key = ("qk", l, j, d)
                            b = product_ready(dve, key)
                            x = gQK[d].rearrange("p h c -> p (h c)")
                            read_out(dve.tensor_tensor(x, b, x, ALU.mult), key)
                    for n in range(1, LEVELS):
                        for d in range(2):
                            key = ("y", l, j, d, n)
                            b = product_ready(dve, key).rearrange("p (h c) -> p h c", h=GH)
                            read_out(dve.tensor_tensor(gY[d], ident[:, :].unsqueeze(1).to_broadcast([P, GH, P]), b,
                                                       ALU.subtract), key)
                        for d in range(2):
                            key = ("xx", l, j, d, n, 1)
                            b = product_ready(dve, key).rearrange("p (e x c) -> p e x c", e=2, x=2)
                            x0 = 0 if n < LEVELS - 1 else 1
                            read_out(dve.tensor_copy(gX[d][:, 2:4, x0:2, :], b[:, :, x0:2, :]), key)
                    for d in range(2):
                        key = ("kr", l, j, d)
                        b = product_ready(dve, key).rearrange("p (h c) -> p h c", h=GH)
                        dve.tensor_tensor(gAT[d], b, bg[:, d, ti[d], :].unsqueeze(2).to_broadcast([P, GH, P]),
                                          ALU.mult)
                        read_out(dve.tensor_tensor(gKD[d], b, gt4[:, d, 0, :].unsqueeze(2).to_broadcast([P, GH, P]),
                                                   ALU.mult), key)
                        key = ("vr", l, j, d)
                        b = product_ready(dve, key).rearrange("p (h c) -> p h c", h=GH)
                        be = gb[:, 1, ti[d], d * GH:(d + 1) * GH]
                        read_out(dve.tensor_tensor(gY[d], b, be.unsqueeze(2).to_broadcast([P, GH, P]), ALU.mult), key)
                    for d in range(2):
                        key = ("v", l, j, d)
                        b = product_ready(dve, key)
                        read_out(dve.tensor_copy(gY[d].rearrange("p h c -> p (h c)"), b), key)
                    for d in range(2):
                        if use_o[d]:
                            key = ("go", l, j, d)
                            b = product_ready(dve, key).rearrange("p (h c) -> p h c", h=GH)
                            o = mixT[:, 2:2 + GH, tt[d]]
                            first = [tile_of(1 - d, x) for x in range(NT)].index(ti[d]) > j
                            if first:
                                read_out(dve.tensor_copy(o, b), key)
                            else:
                                read_out(dve.tensor_tensor(o, b, o, ALU.add), key)
                        if j < NT - 1:
                            key = ("st", l, j, d)
                            b = product_ready(dve, key)
                            if j == 0:
                                read_out(dve.tensor_copy(S[:, d, :, :].rearrange("p h c -> p (h c)"), b), key)
                            else:
                                for h in range(GH):
                                    m = dve.scalar_tensor_tensor(out=S[:, d, h, :], in0=S[:, d, h, :],
                                                                 scalar=gt4[:, d, 1, h:h + 1],
                                                                 in1=b[:, h * P:(h + 1) * P], op0=ALU.mult,
                                                                 op1=ALU.add)
                                read_out(m, key)

                if l == 0:
                    evacuated(dve, ("am", ADA_GROUPS))
                    modulation(0, 1)

                for h in range(GH):
                    dve.wait_ge(s["rinv"], 2 + 2 * GH + h)
                    r = rs_gdn[:, h % 2, t_first:T]
                    o = mixT[:, 2 + h, t_first:T]
                    link(dve.tensor_tensor(o, o, r, ALU.mult), l)
                    dve.scalar_tensor_tensor(out=o, in0=o, scalar=cols[:, COL_GN:COL_GN + 1],
                                             in1=szT[:, h, t_first:T], op0=ALU.mult, op1=ALU.mult
                                             ).then_inc(s["mixd"], 1)

                for k in range(KD):
                    for g in segs:
                        t0, n = SEGS[g]
                        key = ("y", l, k, g)
                        b = product_ready(dve, key)
                        x = xT[:, k, t0:t0 + n]
                        read_out(dve.scalar_tensor_tensor(out=x, in0=b[:, 0:n], scalar=mods_of[l][:, 2 * KD + k, 1 - g:2 - g],
                                                          in1=x, op0=ALU.mult, op1=ALU.add), key)
                norm(l, 2)

                b = product_ready(dve, ("rt", l))[:, 0:NT * N_EXP].rearrange("p (i e) -> p i e", i=NT)[:, i0:NT, :]
                nt = NT - i0
                link(dve.tensor_reduce(rt6[:, i0:NT], b, AX.X, ALU.max), l)
                a = aff[:, i0:NT, :]
                r = rt6[:, i0:NT].unsqueeze(2).to_broadcast([P, nt, N_EXP])
                link(dve.tensor_tensor(a, b, r, ALU.subtract), l)
                read_out(dve.tensor_copy(rt6[:, i0:NT], b[:, :, 0]), ("rt", l))
                evacuated(dve, ("rt", l))
                dve.tensor_copy(rt6[:, i0:NT], rt6[:, i0:NT]).then_inc(s["rmax"], 1)
                for i in tiles:
                    b = product_ready(dve, ("hr", l, i, 1))
                    read_out(dve.tensor_copy(hrow[:, i, 512:1024], b), ("hr", l, i, 1))
                dve.wait_ge(s["rexp"], 1)
                link(dve.tensor_reduce(rt6[:, i0:NT], a, AX.X, ALU.add), l)
                link(dve.reciprocal(rt6[:, i0:NT], rt6[:, i0:NT]), l)
                dve.tensor_tensor(a, a, r, ALU.mult).then_inc(s["aff"], 1)

                for g in segs:
                    t0, n = SEGS[g]
                    cap = CAP_L if g else CAP_C
                    b = product_ready(dve, ("aT", l, g))
                    E = slice(0, N_EXP)
                    w, av, se, cs = (x[E, t0:t0 + n] for x in (tkw, affT, sel, csum))
                    link(dve.tensor_copy(av, b[E, 0:n]), l)
                    read_out(dve.tensor_copy(w, b[E, 0:n]), ("aT", l, g))
                    evacuated(dve, ("aT", l, g))
                    for r8 in range(cap // 8):
                        link(dve.max(top8[:, :], w), l)
                        if r8 < cap // 8 - 1:
                            link(dve.match_replace(w, top8[:, :], w, -1.0), l)
                    thr = top8[:, 7:8]
                    link(dve.tensor_scalar(se, av, thr, None, ALU.is_gt), l)
                    link(dve.tensor_scalar(w, av, thr, None, ALU.is_equal), l)
                    link(dve.tensor_reduce(tkn[:, 0:1], se, AX.X, ALU.add), l)
                    link(dve.tensor_scalar(tkn[:, 1:2], tkn[:, 0:1], -1.0, float(cap), ALU.mult, ALU.add), l)
                    link(dve.tensor_tensor_scan(cs, w, w, 0.0, ALU.add, ALU.max), l)
                    link(dve.scalar_tensor_tensor(out=w, in0=cs, scalar=tkn[:, 1:2], in1=w, op0=ALU.is_le,
                                                  op1=ALU.mult), l)
                    link(dve.tensor_tensor(se, se, w, ALU.add), l)
                    link(dve.tensor_tensor_scan(cs, se, se, 0.0, ALU.add, ALU.max), l)
                    link(dve.tensor_tensor(se, cs, se, ALU.mult), l)
                    dve.tensor_scalar(se, se, -1.0, None, ALU.add).then_inc(s["sel"], 1)
                b = product_ready(dve, ("slot", l))
                read_out(dve.tensor_copy(slotc[:, i0:NT, :].rearrange("p i e -> p (i e)"),
                                         b[:, i0 * N_EXP:NT * N_EXP]), ("slot", l))
                evacuated(dve, ("slot", l))

                dve.tensor_copy(tokaff[:, CT:NT, 0:1], iota[:, CAP_L:CAP_L + SEQ // P].unsqueeze(2))
                if need_ctx:
                    dve.tensor_copy(tokaff[:, 0:CT, 0:1], iota[:, CAP_L:CAP_L + CT].unsqueeze(2))
                dve.tensor_copy(tokaff[:, i0:NT, 1:NW], aff[:, i0:NT, :])
                for t in list(range(CT, NT)) + (list(range(CT)) if need_ctx else []):
                    g, cap = (G[t - CT], CAP_L) if t >= CT else (G[SEQ // P + t], CAP_C)
                    dve.tensor_tensor(g, iota[:, 0:cap].unsqueeze(1).to_broadcast([P, N_EXP, cap]),
                                      slotc[:, t, :].unsqueeze(2).to_broadcast([P, N_EXP, cap]), ALU.is_equal
                                      ).then_inc(s["G"], 1)
                for g in reversed(segs):
                    b = product_ready(dve, ("mc", l, g))
                    cap, w = (CAP_L, 0) if g else (CAP_C, 2)
                    n = 2 * cap
                    number = b[0:n, 0:PAIRS * NW].rearrange("p (i c) -> p i c", c=NW)[:, :, 0:1]
                    dve.tensor_copy(idx[0:n, g, :].unsqueeze(2), number).then_inc(s["idx"], 1)
                    dve.tensor_copy(gcol[0:n, :, w:w + 1], number)
                    for e in range(2):
                        r = slice(e * cap, (e + 1) * cap)
                        m = dve.tensor_copy(gcol[r, :, w + 1:w + 2], b[r, 1 + e:2 + e + (NW + 2) * (PAIRS - 1):NW + 2]
                                            .unsqueeze(2))
                    read_out(m, ("mc", l, g))
                    evacuated(dve, ("mc", l, g))

                n_cap = CAP if need_ctx else CAP_L
                dve.wait_ge(s["tok"], 1)

                def tokens(name_of, i):
                    for q in (1, 3):
                        key = name_of("x%d" % q)
                        b = product_ready(dve, key, i)[:, 0:4 * CAP].rearrange("p (k c) -> p k c", k=2)
                        copy_slots(dve.tensor_copy, b, xs, q, need_ctx, lambda m: read_out(m, key))

                def pair(here, i, nxt):
                    now = gcol[:, bass.ds(i, 1), :] if i is not None else gcol[:, PAIRS - 1:PAIRS, :]
                    dve.tensor_copy(gnow.unsqueeze(1), now).then_inc(s["cur"], 1)
                    dve.wait_ge(s["cur"], plus(1, 1, i) if i is not None else PAIRS)
                    m = dve.tensor_scalar(Sl, tokrow, gnow[:, 0:1], gnow[:, 1:2], ALU.is_equal, ALU.mult)
                    if need_ctx:
                        n = 2 * CAP_C
                        m = dve.tensor_scalar(Sc[0:n, :], tokrow[0:n, 0:CTX], gnow[0:n, 2:3], gnow[0:n, 3:4],
                                              ALU.is_equal, ALU.mult)
                    m.then_inc(s["S"], 1)
                    for e in range(2):
                        for q in range(2):
                            key = here("u%d%d" % (e, q))
                            b = product_ready(dve, key, i)[:, 0:2 * CAP].rearrange("p (f c) -> p f c", f=2)
                            evacuated(dve, here("g%d%d" % (e, q)), i)
                            read_out(dve.tensor_tensor(hid[:, e, 2 * q:2 * q + 2, 0:n_cap], sg[:, q, :, 0:n_cap],
                                                       b[:, :, 0:n_cap], ALU.mult), key)
                    for e in range(2):
                        key = here("y%d1" % e)
                        b = product_ready(dve, key, i)
                        m = dve.tensor_copy(ylat[e * CAP_L:(e + 1) * CAP_L, 512:1024], b[0:CAP_L, :])
                        if need_ctx:
                            m = dve.tensor_copy(yctx[e * CAP_C:(e + 1) * CAP_C, 512:1024], b[CAP_L:CAP, :])
                        read_out(m, key)
                    if nxt:
                        tokens(here, i)
                    for k in range(KD):
                        for g in reversed(segs):
                            t0, n = SEGS[g]
                            key = here("c%d%d" % (k, g))
                            b = product_ready(dve, key, i)
                            x = xT[:, k, t0:t0 + n]
                            read_out(dve.scalar_tensor_tensor(out=x, in0=b[:, 0:n],
                                                              scalar=mods_of[l][:, 5 * KD + k, 1 - g:2 - g], in1=x,
                                                              op0=ALU.mult, op1=ALU.add), key)

                tokens(lambda name: ("first", l, name), None)
                with dve.Fori(0, PAIRS - 1) as i:
                    pair(lambda name: ("moe", l, name), i, True)
                pair(lambda name: ("last", l, name), None, False)

            orow = big[:, 0:(NT - CT) * D].rearrange("p (i d) -> p i d", i=NT - CT)
            for i in range(CT, NT):
                b = product_ready(dve, ("out", i, 1))
                read_out(dve.tensor_copy(orow[:, i - CT, 512:1024], b), ("out", i, 1))

        @block.gpsimd
        def _(pool):
            chain = [0, 0]

            def link(ins, l):
                chain[l] += 1
                ins.then_inc(sems[l]["pool_e"], 1)
                pool.wait_ge(sems[l]["pool_e"], chain[l])

            pool.memset(pstage[:, :], 0.0)
            pool.memset(poolw[:, :, :], 0.0).then_inc(sems[0]["zero"], 1)
            pool.memset(ones[:, :], 1.0)
            pool.memset(eps[:, 0:1], EPS)
            pool.memset(eps[:, 1:2], 128.0 * EPS).then_inc(s_ones, 1)
            pool.wait_ge(sems[0]["zero"], 1)

            def parameters(l):
                s = sems[l]
                for dst, src in (
                        (wuq[:, 0, :], A["mla_w_uq"][l, 0:P, :]),
                        (wuq[0:64, 1, :], A["mla_w_uq"][l, P:Q_LORA, :]),
                        (wukv[:, :], A["mla_w_ukv"][l]),
                        (poolw[0:64, 0, 0:64], A["pool_w"][l, 0]),
                        (poolw[64:128, 0, 64:128], A["pool_w"][l, 1]),
                        (poolw[0:64, 1, 0:64], A["pool_w"][l, 2]),
                        (poolw[64:128, 1, 64:128], A["pool_w"][l, 3]),
                        (router[:, :, :], A["moe_router"][l].rearrange("(k p) e -> p k e", p=P)),
                        (rown[:, 0, :], A["mla_k_norm"][l].partition_broadcast(P)),
                        (rown[:, 1, :], A["mla_q_norm"][l].partition_broadcast(P)),
                        (gpar[:, 0, :], A["gdn_a_log"][l].rearrange("d h -> (d h)").partition_broadcast(P)),
                        (gpar[:, 1, :], A["gdn_dt_bias"][l].rearrange("d h -> (d h)").partition_broadcast(P))):
                    pool.dma_start(dst, src).then_inc(s["par"], 16)

            parameters(0)
            for l in range(DEPTH):
                s = sems[l]
                need_ctx = l < DEPTH - 1
                tiles = range(NT) if need_ctx else range(CT, NT)
                segs = (0, 1) if need_ctx else (1,)

                if l == 0:
                    product_ready(pool, ("x", KD - 1, 1))
                else:
                    product_ready(pool, ("last", l - 1, "c%d0" % (KD - 1)))
                pool.memset(at(big, 0, (2 * UW,)), 0.0).then_inc(s["upad"], 1)

                def add_shift(dst, src, a, n):
                    return pool.tensor_tensor(dst[:, a:UW - n], src[:, 0:UW - n - a], src[:, a + n:UW], ALU.add)

                for c in range(2):
                    for g in segs:
                        evacuated(pool, ("in", l, "pool%d" % c, g))
                    u = U[:, c, :]
                    link(pool.tensor_tensor(BA[:, 1:UW], u[:, 1:UW], u[:, 0:UW - 1], ALU.add), l)
                    link(pool.tensor_tensor(BB[:, 2:UW - 1], BA[:, 1:UW - 2], BA[:, 3:UW], ALU.add), l)
                    if c == 1:
                        link(pool.tensor_tensor(BA[:, 4:UW - 3], BB[:, 2:UW - 5], BB[:, 6:UW - 1], ALU.add), l)
                        link(pool.tensor_tensor(BB[:, 8:UW - 7], BA[:, 4:UW - 11], BA[:, 12:UW - 3], ALU.add), l)
                    for half, src in ((0, BA), (1, BB)):
                        r = slice(64 * half, 64 * half + 64)
                        for g in segs:
                            t0, n = SEGS[g]
                            link(pool.tensor_scalar(dT[r, c, t0:t0 + n], src[r, UO[g]:UO[g] + n], poolc[r, c, 16:17],
                                                    None, ALU.mult), l)
                    for g in segs:
                        t0, n = SEGS[g]
                        x = dT[:, c, t0:t0 + 8]
                        link(pool.tensor_tensor(x, x, poolc[:, c, 0:8], ALU.mult), l)
                        x = dT[:, c, t0 + n - 8:t0 + n]
                        link(pool.tensor_tensor(x, x, poolc[:, c, 8:16], ALU.mult), l)
                        x = dT[:, c, t0:t0 + n]
                        m = pool.tensor_tensor(x, x, u[:, UO[g]:UO[g] + n], ALU.subtract)
                        if g == 1:
                            m.then_inc(s["pool"], 1)
                        else:
                            link(m, l)

                pool.wait_ge(s["par"], 16 * PAR_DMAS)
                jobs = [("k", i) for i in range(NT)] + [("q", i) for i in tiles]
                for n, (kind, i) in enumerate(jobs):
                    pool.wait_ge(s["rowa"], n + 1)
                    r = rows[:, n % 2, :, :]
                    w = rown[:, 0 if kind == "k" else 1, :].unsqueeze(1).to_broadcast([P, H, QK])
                    m = pool.tensor_tensor(r, r, w, ALU.mult)
                    if i >= CT:
                        link(m, l)
                        x = r[:, :, NOPE:QK]
                        link(pool.tensor_tensor(rot1, x, rope[:, i - CT, 0, :].unsqueeze(1).to_broadcast(
                            [P, H, ROPE]), ALU.mult), l)
                        x4 = x.rearrange("p h (g a e) -> p h g a e", g=2, a=2)
                        s4 = rope[:, i - CT, 1, :].rearrange("p (g a e) -> p g a e", g=2, a=2)
                        for a in range(2):
                            link(pool.tensor_tensor(rot2[:, :, :, a, :], x4[:, :, :, 1 - a, :],
                                                    s4[:, :, a, :].unsqueeze(1).to_broadcast([P, H, 2, ROPE // 4]),
                                                    ALU.mult), l)
                        m = pool.tensor_tensor(x, rot1, rot2.rearrange("p h g a e -> p h (g a e)"), ALU.add)
                    m.then_inc(s["row2"], 1)

                pool.wait_ge(s["gbd"], 1)
                pool.wait_ge(s["lmul"], 2 * GH)
                product_ready(pool, ("gc", l))
                for j in range(NT):
                    ti = [tile_of(d, j) for d in range(2)]
                    tt = [slice(i * P, (i + 1) * P) for i in ti]
                    for d in range(2):
                        if j:
                            product_ready(pool, ("v", l, j - 1, d))
                        pool.tensor_tensor(gML[d], tri[:, d, :].unsqueeze(1).to_broadcast([P, GH, P]),
                                           gb[:, 0, ti[d], d * GH:(d + 1) * GH].unsqueeze(2).to_broadcast(
                                               [P, GH, P]), ALU.mult).then_inc(s["tg"], 1)
                    for d in range(2):
                        pool.wait_ge(s["xg"], 2 * j + d + 1)
                        if j and (need_ctx or tile_of(d, j - 1) >= CT):
                            product_ready(pool, ("go", l, j - 1, d))
                        pool.tensor_scalar(gD[d], gAT[d], 0.0, None, ALU.max)
                        pool.tensor_scalar(gQK[d], gAT[d], 0.0, None, ALU.min).then_inc(s["dcl"], 1)
                    for d in range(2):
                        pool.wait_ge(s["dex"], 2 * j + d + 1)
                        pool.tensor_tensor(gQK[d], gQK[d], tri[:, d, :].unsqueeze(1).to_broadcast([P, GH, P]),
                                           ALU.mult)
                        pool.tensor_tensor(gD[d], gD[d], gb[:, 1, ti[d], d * GH:(d + 1) * GH].unsqueeze(2)
                                           .to_broadcast([P, GH, P]), ALU.mult).then_inc(s["dm"], 1)
                    for d in range(2):
                        evacuated(pool, ("kk", l, j, d))
                        evacuated(pool, ("at2", l, j, d))
                        if j == 0 or True:
                            pool.tensor_tensor(gML[d], gAT[d], lev[:, d, 1, :].unsqueeze(1).to_broadcast(
                                [P, GH, P]), ALU.mult).then_inc(s["ml"], 1)
                        for x, src in ((0, gY[d]), (1, gAT[d])):
                            link(pool.tensor_tensor(gX[d][:, :, x, :], src, lev[:, d if x else 1 - d, 0, :]
                                                    .unsqueeze(1).to_broadcast([P, GH, P]), ALU.mult), l)
                            m = pool.tensor_tensor(gX[d][:, :, x, :], ident[:, :].unsqueeze(1).to_broadcast(
                                [P, GH, P]), gX[d][:, :, x, :], ALU.subtract)
                        m.then_inc(s["x1"], 1)
                    for n in range(2, LEVELS):
                        for d in range(2):
                            product_ready(pool, ("y", l, j, d, n - 1))
                            pool.tensor_tensor(gML[d], gAT[d], lev[:, d, n, :].unsqueeze(1).to_broadcast(
                                [P, GH, P]), ALU.mult).then_inc(s["ml"], 1)
                    for d in range(2):
                        evacuated(pool, ("g", l, j, d))
                        pool.tensor_tensor(gQG[d], gQG[d], qkvT[:, 0:GH, tt[d]], ALU.mult).then_inc(s["qg"], 1)

                product_ready(pool, ("rtT", l, 1))
                for j in range(SEQ // CAP_L):
                    m = pool.tensor_scalar(tokrow[:, j * CAP_L:(j + 1) * CAP_L], iota[:, 0:CAP_L], float(j * CAP_L),
                                           None, ALU.add)
                m.then_inc(s["tok"], 1)

                pool.wait_ge(s["hrow"], 16 * len(segs))
                pool.wait_ge(s["idx"], len(segs))
                for p in range(PAIRS):
                    if p == 1:
                        product_ready(pool, ("first", l, "x3"))
                    elif p:
                        product_ready(pool, ("moe", l, "x3"), p - 2)
                    for g in reversed(segs):
                        dst, n = (xlat, 2 * CAP_L) if g else (xctx, 2 * CAP_C)
                        pool.indirect_dma_start(dst[0:n, :], None, hD[g],
                                                bass.IndirectOffsetOnAxis(ap=idx[0:n, g, p:p + 1], axis=0)
                                                ).then_inc(s["gath"], 16)
                    if p == 1 and l + 1 < DEPTH:
                        evacuated(pool, ("cols", l))
                        channel_parameters(pool, l + 1)
                        parameters(l + 1)
    return where


def copy_slots(copy, b, xs, q, need_ctx, finish):
    lat = b[:, :, 0:2 * CAP_L].rearrange("p k (e c) -> p k e c", e=2)
    m = copy(xs[:, 2 * q:2 * q + 2, :, 0:CAP_L], lat)
    if need_ctx:
        con = b[:, :, 2 * CAP_L:2 * CAP].rearrange("p k (e c) -> p k e c", e=2)
        m = copy(xs[:, 2 * q:2 * q + 2, :, CAP_L:CAP], con)
    finish(m)


_INS = ["x", "c", "ctx", "c_ctx", "ada_w", "ada_b", "norm1_g", "norm2_g", "w_in", "mla_q_a_norm", "mla_w_uq",
        "mla_kv_a_norm", "mla_w_ukv", "mla_q_norm", "mla_k_norm", "gdn_conv_w", "gdn_a_log", "gdn_dt_bias",
        "gdn_norm_g", "pool_w", "pool_scale", "w_out", "moe_router", "moe_w_gate", "moe_w_up", "moe_w_down"]


def kernel(**inputs):
    import concourse.bacc as _bacc
    from concourse.bass_utils import run_bass_kernel_spmd as _run

    nc = _bacc.Bacc("TRN2", target_bir_lowering=False, num_devices=1)
    arrays, args = {}, {}
    for name, a in [(n, inputs[n]) for n in _INS] + list(shape_constants().items()):
        a = np.ascontiguousarray(a)
        arrays["in_" + name] = a
        args[name] = nc.dram_tensor("in_" + name, a.shape, mybir.dt.from_np(a.dtype), kind="ExternalInput").ap()
    out = nc.dram_tensor("out", (1, SEQ, D), F32, kind="ExternalOutput").ap()
    build_program(nc, args, out)
    r = _run(nc, [arrays], core_ids=[0])
    return r.results[0]["out"]
```

```python
from contextlib import ExitStack

import numpy as np

import concourse.bass as bass
from concourse import mybir

F32 = mybir.dt.float32
ALU = mybir.AluOpType
ACT = mybir.ActivationFunctionType
AX = mybir.AxisListType

P = 128
D = 1024
KD = D // P
CTX = 256
SEQ = 512
T = CTX + SEQ
NT = T // P
CT = CTX // P
DEPTH = 2
EPS = 1e-6
GRID_W = 64
ROPE_THETA = 10000.0

H = 4
NOPE, ROPE, DV = 64, 32, 64
QK = NOPE + ROPE
Q_LORA, KV_LORA = 192, 128
GH = 4
WINDOWS = (2, 4, 8, 16)
PG = 64
PAD = 8
N_EXP = 16
F_EXP = 512
FK = F_EXP // P
CAP_L = 2 * SEQ // N_EXP
CAP_C = 2 * CTX // N_EXP
CAP = CAP_L + CAP_C
PAIRS = N_EXP // 2
LEVELS = 7

ADA_LOADS = 6 * D // 256
ADA_FIRST = 2 * D // 256
ADA_LATER = [(0, g) for g in range(ADA_FIRST, ADA_LOADS)] + [(1, g) for g in range(ADA_LOADS)]
ADA_GROUP = LEVELS - 1
ADA_ROWS = 3 * 32 + 2
ADA_GROUPS = -(-len(ADA_LATER) // ADA_GROUP)

SPLITS = (Q_LORA, KV_LORA, ROPE, 512, 512, 512, 512, 8, 8, 256)
OFF = [int(x) for x in np.cumsum((0,) + SPLITS)]
SLOTS = 6
COL_DMAS = 9
PAR_DMAS = 12
CONST_DMAS = 4
SLOT_COLS = 256
BANKS = 8

SEGS = ((0, CTX), (CTX, SEQ))
COL_ADA, COL_N1, COL_N2, COL_CONV, COL_KV, COL_GN, COL_Q, COL_PS = 0, 48, 56, 64, 100, 101, 102, 104
N_COLS = 106
IN_LOADS = [("pool", OFF[9], OFF[10]), ("ab", OFF[7], OFF[9]), ("ql", OFF[0], OFF[1]), ("kvr", OFF[1], OFF[3])]
IN_LOADS += [("qkv%d" % j, OFF[3] + 256 * j, OFF[3] + 256 * (j + 1)) for j in range(6)]
IN_LOADS += [("z%d" % j, OFF[6] + 256 * j, OFF[6] + 256 * (j + 1)) for j in range(2)]


def shape_constants():
    s = np.arange(P)
    out = {"k_ident": np.eye(P, dtype=np.float32)}
    out["k_tri"] = np.stack([s[:, None] <= s[None, :], s[:, None] >= s[None, :]], 1).astype(np.float32)
    lev = np.zeros((P, 2, LEVELS, P), np.float32)
    for n in range(LEVELS):
        b = 1 << n
        same = (s[:, None] // (2 * b)) == (s[None, :] // (2 * b))
        low = (s // b) % 2 == 0
        lev[:, 0, n] = same & low[:, None] & ~low[None, :]
        lev[:, 1, n] = same & ~low[:, None] & low[None, :]
    out["k_lev"] = lev
    slots = np.tile(np.arange(CAP_L, dtype=np.float32), (P, 1))
    tokens = s[:, None] + P * np.arange(SEQ // P)[None, :]
    groups = (s[:, None] % 32 == np.arange(2)[None, :])
    out["k_iota"] = np.concatenate([slots, tokens.astype(np.float32), groups.astype(np.float32)], 1)
    n = ROPE // 4
    inv = np.float32(ROPE_THETA) ** (-np.arange(n, dtype=np.float32) / np.float32(n))
    t = np.arange(SEQ)
    ar = (t // GRID_W).astype(np.float32)[:, None] * inv
    ac = (t % GRID_W).astype(np.float32)[:, None] * inv
    cos = np.concatenate([np.cos(ar), np.cos(ar), np.cos(ac), np.cos(ac)], 1)
    sin = np.concatenate([-np.sin(ar), np.sin(ar), -np.sin(ac), np.sin(ac)], 1)
    tab = np.stack([cos, sin], 1).astype(np.float32)
    out["k_rope"] = np.ascontiguousarray(tab.reshape(SEQ // P, P, 2, ROPE).transpose(1, 0, 2, 3))
    pool = np.zeros((P, 2, 17), np.float32)
    for g, w in enumerate(WINDOWS):
        rows, c = slice(64 * (g % 2), 64 * (g % 2) + 64), g // 2
        for j in range(8):
            pool[rows, c, j] = w / (w - max(0, w // 2 - j))
            pool[rows, c, 8 + j] = w / (w - max(0, w // 2 - (8 - j)))
        pool[rows, c, 16] = 1.0 / w
    out["k_pool"] = pool
    return out


def build_program(nc, A, out):
    ctx = ExitStack()
    with ctx:
        def sb(name, shape):
            return ctx.enter_context(nc.sbuf_tensor(name, shape, F32))

        def sem(name):
            return ctx.enter_context(nc.semaphore(name))

        xT = sb("xT", [P, KD, T])
        hT = sb("hT", [P, KD, T])
        ring = sb("ring", [P, SLOTS, KD * SLOT_COLS])
        big = sb("big", [P, 12 * T])
        sz = sb("sz", [P, 4 * T])
        dT = sb("dT", [P, 2, T])
        arena = sb("arena", [P, 12 * T])
        ident = sb("ident", [P, P])
        ones = sb("ones", [P, P])
        tri = sb("tri", [P, 2, P])
        lev = sb("lev", [P, 2, LEVELS, P])
        iota = sb("iota", [P, CAP_L + SEQ // P + 2])
        rope = sb("rope", [P, SEQ // P, 2, ROPE])
        poolc = sb("poolc", [P, 2, 17])
        pstage = hT[:, 0, 0:P]
        cstage = arena[0:16, 11 * T:11 * T + P]
        cols = sb("cols", [P, N_COLS])
        scol = sb("scol", [P, 2, KD])
        modraw = sb("modraw", [P, DEPTH * 6 * KD, 2])
        amods = sb("amods", [P, DEPTH, 2, KD, 2])
        wuq = sb("wuq", [P, 2, H * QK])
        wukv = sb("wukv", [P, H * (NOPE + DV)])
        poolw = sb("poolw", [P, 2, P])
        router = sb("router", [P, KD, N_EXP])
        rown = sb("rown", [P, 2, QK])
        gpar = sb("gpar", [P, 2, 8])
        eps = sb("eps", [P, 2])
        small = sb("small", [P, 640])
        psum = ctx.enter_context(nc.psum_tensor("psum", [P, BANKS, 512], F32))

        mixT = hT
        mods_of = [modraw[:, l * 6 * KD:(l + 1) * 6 * KD, :] for l in range(DEPTH)]
        amod_of = [amods[:, l, :, :, :] for l in range(DEPTH)]

        def at(t, first, shape):
            n = int(np.prod(shape))
            v = t[:, first:first + n]
            if len(shape) == 2:
                return v.rearrange("p (a b) -> p a b", a=shape[0])
            if len(shape) == 3:
                return v.rearrange("p (a b c) -> p a b c", a=shape[0], b=shape[1])
            if len(shape) == 4:
                return v.rearrange("p (a b c d) -> p a b c d", a=shape[0], b=shape[1], c=shape[2])
            return v

        sqb = at(arena, 0, (2, T))
        rstd = at(arena, 2 * T, (T,))
        rs_gdn = at(arena, 2 * T, (2, T))
        l2b = at(arena, 10 * T, (2, T))
        UW = T + 4 * PAD
        U = at(big, 0, (2, UW))
        BA = at(big, 2 * UW, (UW,))
        BB = at(big, 3 * UW, (UW,))
        rows = at(arena, 10 * T, (2, H, QK))
        rtmp = at(arena, 10 * T + 2 * H * QK, (H, QK))
        rot1 = at(arena, 10 * T + 3 * H * QK, (H, ROPE))
        rot2 = at(arena, 10 * T + 3 * H * QK + H * ROPE, (H, 2, 2, ROPE // 4))
        assert 3 * H * QK + 2 * H * ROPE <= 2 * T
        abrow = arena[0:16, 0:T]
        krow = arena[0:ROPE, 4 * T:5 * T]
        rtrow = sz[0:N_EXP, T:2 * T]
        UO = (PAD, CTX + 3 * PAD)
        SQ0 = at(big, 6 * T, (T,))
        SQ1 = at(big, 7 * T, (T,))
        SQK = at(big, 8 * T, (T,))
        KVG = at(big, 9 * T, (T,))
        QG0 = at(big, 10 * T, (T,))
        QG1 = at(big, 11 * T, (T,))
        qkvT = at(big, 0, (12, T))
        KT = at(arena, 0, (H, T))
        QT = at(arena, 4 * T, (H, T))
        V = at(arena, 8 * T, (NT, H * DV))
        PR = at(arena, 10 * T, (T,))
        PT = at(arena, 11 * T, (NT, P))
        G1 = GH * P
        GW = 8 * G1
        dir_at = [d * GW for d in range(2)]
        gAT = [at(arena, o, (GH, P)) for o in dir_at]
        gML = [at(arena, o + G1, (GH, P)) for o in dir_at]
        gX = [at(arena, o + 2 * G1, (GH, 2, P)) for o in dir_at]
        gD = [at(arena, o + 2 * G1, (GH, P)) for o in dir_at]
        gY = [at(arena, o + 4 * G1, (GH, P)) for o in dir_at]
        gQK = [at(arena, o + 5 * G1, (GH, P)) for o in dir_at]
        gKD = [at(arena, o + 6 * G1, (GH, P)) for o in dir_at]
        gQG = [at(arena, o + 7 * G1, (GH, P)) for o in dir_at]
        S = at(arena, 2 * GW, (2, GH, P))
        szT = at(sz, 0, (4, T))
        szrow = sz[0:ADA_ROWS, 0:ADA_FIRST * SLOT_COLS]
        dTrow = dT[0:ADA_ROWS, :, :].rearrange("p c t -> p (c t)")
        assert ADA_GROUP * SLOT_COLS <= 2 * T
        hrow = at(big, 0, (NT, D))
        Sl = at(big, NT * D, (SEQ,))
        Sc = at(big, NT * D + SEQ, (CTX,))
        tokrow = at(big, NT * D + SEQ + CTX, (SEQ,))
        xlat = at(big, 0, (D,))
        xctx = at(big, D, (D,))
        G = [at(arena, t * N_EXP * CAP_L, (N_EXP, CAP_L)) for t in range(SEQ // P)]
        G += [at(arena, (SEQ // P) * N_EXP * CAP_L + t * N_EXP * CAP_C, (N_EXP, CAP_C)) for t in range(CT)]
        at_m = N_EXP * (SEQ // P * CAP_L + CT * CAP_C)
        NW = 1 + N_EXP
        n_m = N_EXP * (CAP_L + 2 * CAP_C)
        mrow = arena[0:NW, at_m:at_m + n_m]
        tokaff = at(arena, at_m + n_m, (NT, NW))
        affT = at(sz, 0, (T,))
        tkw = at(sz, T, (T,))
        sel = at(sz, 2 * T, (T,))
        csum = at(sz, 3 * T, (T,))
        xs = at(arena, 0, (KD, 2, CAP))
        HW = 2 * 2 * CAP
        sg = at(arena, 1536, (2, HW))
        hid = at(arena, 1536 + 2 * HW, (2, HW))
        hidT = at(arena, 1536 + 4 * HW, (2, HW))
        ylat = at(arena, 1536 + 6 * HW, (D,))
        yctx = at(arena, 1536 + 6 * HW + D, (D // 2,))
        gcol = small[:, 0:32].rearrange("p (i w) -> p i w", w=4)
        gnow = small[:, 32:36]
        gb = small[:, 0:96].rearrange("p (w i c) -> p w i c", w=2, i=NT)
        gc = small[:, 96:144].rearrange("p (d i h) -> p d i h", d=2, i=NT)
        bg = small[:, 144:192].rearrange("p (d i h) -> p d i h", d=2, i=NT)
        krp = small[:, 436:628].rearrange("p (i c) -> p i c", i=NT)
        rs12 = small[:, 384:396].rearrange("p (i w) -> p i w", w=2)
        ss4 = small[:, 396:404].rearrange("p (n h) -> p n h", n=2)
        mx = small[:, 404:408].rearrange("p (n w) -> p n w", n=2)
        nm = small[:, 408:410]
        sm = small[:, 352:368].rearrange("p (n h w) -> p n h w", n=2, w=2)
        rden = small[:, 416:420]
        gt4 = small[:, 420:436].rearrange("p (d w h) -> p d w h", d=2, w=2)
        aff = small[:, 436:532].rearrange("p (i e) -> p i e", i=NT)
        slotc = small[:, 532:628].rearrange("p (i e) -> p i e", i=NT)
        rt6 = small[:, 628:634]
        abw = small[:, 192:288].rearrange("p (w i c) -> p w i c", w=2, i=NT)
        ealog = small[:, 288:296]
        abe = small[:, 296:344].rearrange("p (i c) -> p i c", i=NT)
        top8 = small[0:16, 36:44]
        tkn = small[0:16, 44:48]
        idx = ctx.enter_context(nc.sbuf_tensor("idx", [P, 2, PAIRS], mybir.dt.uint32))

        hD = [nc.dram_tensor("h_rows_%s" % n, (SEGS[g][1], D), F32).ap() for g, n in enumerate(("ctx", "lat"))]

        slot_full = [sem("slot_full%d" % i) for i in range(SLOTS)]
        slot_used = sem("slot_used")
        bank_full = [sem("bank_full%d" % i) for i in range(BANKS)]
        bank_free = [sem("bank_free%d" % i) for i in range(BANKS)]
        s_ident = sem("s_ident")
        s_sum = sem("s_sum")
        s_const = sem("s_const")
        s_ones = sem("s_ones")
        s_xin = sem("s_xin")
        s_out = sem("s_out")
        s_outrow = sem("s_outrow")
        NAMES = ["zero", "zrow", "pcol", "par", "mods1", "mods2", "rinv", "sq1", "sqd1", "hx1", "h1", "sq2", "sqd2", "hx2", "h2", "upad", "pool", "sqm",
                 "abraw", "abexp", "abln", "gbd", "row1", "rowr", "rowa", "row2", "nm", "pv", "cv1", "qkv", "lsq",
                 "lmul", "egc", "bg", "tg", "xg", "dex", "dm", "x0", "x1", "ml", "qg", "osq", "mixd", "rmax",
                 "rexp", "aff", "sel", "G", "hrow", "att", "tok", "idx", "gath", "cur", "S", "dve", "pool_e"]
        sems = [dict((n, sem("%s_%d" % (n, l))) for n in NAMES) for l in range(DEPTH)]

        freed_by = []
        freed = [0]
        where = {}
        uses = [0] * BANKS
        turn = [0]
        loads = []

        def plus(base, per, i):
            return base if i is None else i * per + base

        def product_ready(eng, key, i=None):
            b, n, per = where[key]
            eng.wait_ge(bank_full[b], plus(n + 1, per, i))
            return psum[:, b, :]

        def read_out(ins, key):
            ins.then_inc(bank_free[where[key][0]], 1)

        def evacuated(eng, key, i=None):
            b, n, per = where[key]
            eng.wait_ge(bank_free[b], plus(n + 1, per, i))

        def attended(eng, l, calls, n):
            i, h = calls[n]
            if h == H - 1:
                product_ready(eng, ("o", l, i))
            else:
                eng.wait_ge(sems[l]["pv"], n - n // H)

        def chunks_after(n, n_jobs):
            return [m for m in range(1, 8) if max(1, (m * n_jobs - 1) // 8) == n]

        def att_of(i):
            return QT[:, 2:4, i * P:(i + 1) * P]

        def tile_of(d, j):
            return j if d == 0 else (CT - 1 - j if j < CT else NT + CT - 1 - j)

        def expert_part(n):
            return n % 2, n // 2

        def ada_keys(group):
            return [("ar",) + x for x in ADA_LATER[group * ADA_GROUP:(group + 1) * ADA_GROUP]]

        assert ADA_GROUPS == NT + 1
        def channel_parameters(eng, l):
            for dst, src in (
                    (pstage[COL_ADA:COL_N1, :], A["ada_b"][l].rearrange("(r p) -> r p", p=P)),
                    (pstage[COL_N1:COL_N2, :], A["norm1_g"][l].rearrange("(r p) -> r p", p=P)),
                    (pstage[COL_N2:COL_CONV, :], A["norm2_g"][l].rearrange("(r p) -> r p", p=P)),
                    (pstage[COL_CONV:COL_KV, :], A["gdn_conv_w"][l].rearrange("t (r p) -> (t r) p", p=P)),
                    (pstage[COL_KV:COL_KV + 1, :], A["mla_kv_a_norm"][l:l + 1, :]),
                    (pstage[COL_GN:COL_GN + 1, :], A["gdn_norm_g"][l:l + 1, :]),
                    (pstage[COL_Q:COL_Q + 1, :], A["mla_q_a_norm"][l:l + 1, 0:P]),
                    (pstage[COL_Q + 1:COL_Q + 2, 0:64], A["mla_q_a_norm"][l:l + 1, P:Q_LORA]),
                    (pstage[COL_PS:COL_PS + 2, :], A["pool_scale"][l].rearrange("(r p) -> r p", p=P))):
                eng.dma_start(dst, src).then_inc(sems[l]["pcol"], 16)

        block = ctx.enter_context(nc.Block())

        @block.tensor
        def _(pe):
            held = []

            def claim(key):
                while turn[0] % BANKS in held:
                    turn[0] += 1
                b = turn[0] % BANKS
                turn[0] += 1
                if uses[b]:
                    pe.wait_ge(bank_free[b], uses[b])
                where[key] = (b, uses[b], 0)
                uses[b] += 1
                return psum[:, b, :]

            def done(ins, key):
                ins.then_inc(bank_full[where[key][0]], 1)

            def last_use(ins, key=None):
                if key is None:
                    freed[0] += 1
                    ins.then_inc(slot_used, 1)
                    freed_by.append(freed[0])
                else:
                    freed_by.append((key, None))

            def weights(name):
                n = len(loads)
                loads.append(name)
                pe.wait_ge(slot_full[n % SLOTS], 16 * (n // SLOTS + 1))
                return ring[:, n % SLOTS, :].rearrange("p (k c) -> p k c", k=KD)

            def sum_over_partitions(l, which, sqs, sqd):
                s = sems[l]
                lat = claim(("ss", l, which, 1))
                need = which == 1 or l == 0
                con = claim(("ss", l, which, 0)) if need else None
                for k in range(KD):
                    pe.wait_ge(s[sqs], k + 1)
                    m = pe.matmul(lat, lhsT=ones[:, :], rhs=sqb[:, k % 2, CTX:T], start=k == 0, stop=k == KD - 1)
                    if k == KD - 1:
                        done(m, ("ss", l, which, 1))
                    if need:
                        m = pe.matmul(con[:, 0:CTX], lhsT=ones[:, :], rhs=sqb[:, k % 2, 0:CTX], start=k == 0,
                                      stop=k == KD - 1)
                        if k == KD - 1:
                            done(m, ("ss", l, which, 0))
                    if k < KD - 1:
                        m.then_inc(s[sqd], 1)

            def ada_row(b, w, key, ks):
                for k in ks:
                    r = 32 * (k % 4)
                    m = pe.matmul(b[r:r + 2, 0:SLOT_COLS], lhsT=scol[:, :, k], rhs=w[:, k, :], start=k < 4,
                                  stop=k >= KD - 4)
                if ks[-1] == KD - 1:
                    done(m, key)
                    last_use(None, key)

            def ada_columns(key, row, keys):
                for x in keys:
                    evacuated(pe, x)
                b = claim(key)
                for j in range(len(keys) * SLOT_COLS // P):
                    m = pe.matmul(b[:, 2 * j:2 * j + 2], lhsT=row[:, j * P:(j + 1) * P],
                                  rhs=iota[0:ADA_ROWS, CAP_L + SEQ // P:], start=True, stop=True)
                done(m, key)

            later = [0, None, None]

            def ada_later(half):
                if later[0] == len(ADA_LATER):
                    return
                key = ("ar",) + ADA_LATER[later[0]]
                if half == 0:
                    later[1] = claim(key)
                    held.append(where[key][0])
                    later[2] = weights(("ada",) + ADA_LATER[later[0]])
                ada_row(later[1], later[2], key, range(half * KD // 2, (half + 1) * KD // 2))
                if half == 1:
                    held.remove(where[key][0])
                    later[0] += 1

            pe.wait_ge(s_ident, 16 * 3)
            pe.wait_ge(s_ones, 1)
            pe.wait_ge(s_xin, 16 * 2)
            xin = at(big, 0, (NT, D))
            for k in range(KD):
                for half, tiles in enumerate((range(0, 4), range(4, 6))):
                    key = ("x", k, half)
                    b = claim(key)
                    for j, i in enumerate(tiles):
                        m = pe.transpose(b[:, j * P:(j + 1) * P], xin[:, i, k * P:(k + 1) * P], ident[:, :])
                    done(m, key)

            for l in range(DEPTH):
                s = sems[l]
                need_ctx = l < DEPTH - 1
                tiles = range(NT) if need_ctx else range(CT, NT)
                segs = (0, 1) if need_ctx else (1,)

                pe.wait_ge(s["pcol"], 16 * COL_DMAS)
                b = claim(("cols", l))
                done(pe.transpose(b[:, 0:N_COLS], pstage[0:N_COLS, :], ident[0:N_COLS, 0:N_COLS]), ("cols", l))
                if l == 0:
                    b = claim("c")
                    done(pe.transpose(b[:, 0:16], cstage, ident[0:16, 0:16]), "c")
                sum_over_partitions(l, 1, "sq1", "sqd1")
                if l == 0:
                    evacuated(pe, "c")
                    for g in range(ADA_FIRST):
                        key = ("ar", 0, g)
                        ada_row(claim(key), weights(("ada", 0, g)), key, range(KD))
                    pe.wait_ge(s_sum, 16)
                    ada_columns(("am", 0), szrow, [("ar", 0, g) for g in range(ADA_FIRST)])

                def chunk(key, w, c0, c1, which):
                    bs = [(g, claim(key + (g,))) for g in which]
                    for k in range(KD):
                        if key[2] == "pool0":
                            pe.wait_ge(s["h1"], k + 1)
                        for g, b in bs:
                            t0, n = SEGS[g]
                            m = pe.matmul(b[0:c1 - c0, 0:n], lhsT=w[:, k, c0:c1], rhs=hT[:, k, t0:t0 + n],
                                          start=k == 0, stop=k == KD - 1)
                            if k == KD - 1:
                                done(m, key + (g,))

                def token_rows(key, src, ts):
                    n = src.shape[0]
                    b = claim(key)
                    for i in ts:
                        m = pe.transpose(b[:, i * n:(i + 1) * n], src[:, i * P:(i + 1) * P], ident[0:n, 0:n])
                    done(m, key)

                w = weights(("in", l, 0))
                chunk(("in", l, "pool0"), w, 0, P, segs)
                chunk(("in", l, "pool1"), w, P, 2 * P, segs)
                last_use(None, ("in", l, "pool1", 1))
                w = weights(("in", l, 1))
                chunk(("in", l, "ab"), w, 0, 16, (0, 1))
                last_use(None, ("in", l, "ab", 1))
                w = weights(("in", l, 2))
                chunk(("in", l, "ql0"), w, 0, P, segs)
                chunk(("in", l, "ql1"), w, P, Q_LORA, segs)
                last_use(None, ("in", l, "ql1", 1))
                for g in (0, 1):
                    evacuated(pe, ("in", l, "ab", g))
                token_rows(("ab", l), abrow, range(NT))
                w = weights(("in", l, 3))
                chunk(("in", l, "kv"), w, 0, KV_LORA, (0, 1))
                chunk(("in", l, "krp"), w, KV_LORA, KV_LORA + ROPE, (0, 1))
                last_use(None, ("in", l, "krp", 1))

                def qkv(m):
                    if m % 2 == 0:
                        qkv_w[0] = weights(("in", l, 4 + m // 2))
                    chunk(("in", l, "qkv%d" % m), qkv_w[0], m % 2 * P, (m % 2 + 1) * P, (0, 1))
                    if m % 2:
                        last_use(None, ("in", l, "qkv%d" % m, 1))

                qkv_w = [None]
                qkv(0)
                first_banks = [where[("in", l, "qkv0", g)][0] for g in (0, 1)]
                held.extend(first_banks)

                b = claim(("rs", l))
                for g in (0, 1):
                    evacuated(pe, ("in", l, "kv", g))
                for g in segs:
                    evacuated(pe, ("in", l, "ql1", g))
                    evacuated(pe, ("in", l, "ql0", g))
                for i in range(NT):
                    t = slice(i * P, (i + 1) * P)
                    if i in tiles:
                        pe.matmul(b[:, 2 * i:2 * i + 1], lhsT=SQ0[:, t], rhs=ones[:, 0:1], start=True, stop=False)
                        pe.matmul(b[:, 2 * i:2 * i + 1], lhsT=SQ1[0:64, t], rhs=ones[0:64, 0:1], start=False,
                                  stop=True)
                    m = pe.matmul(b[:, 2 * i + 1:2 * i + 2], lhsT=SQK[:, t], rhs=ones[:, 0:1], start=True, stop=True)
                done(m, ("rs", l))
                for g in (0, 1):
                    evacuated(pe, ("in", l, "krp", g))
                token_rows(("krp", l), krow, range(NT))
                jobs = [("k", i) for i in range(NT)] + [("q", i) for i in tiles]
                pe.wait_ge(s["par"], 16 * PAR_DMAS)

                def project(n):
                    kind, i = jobs[n]
                    t = slice(i * P, (i + 1) * P)
                    key = (kind, l, i)
                    b = claim(key)
                    if kind == "k":
                        m = pe.matmul(b[:, 0:512], lhsT=KVG[:, t], rhs=wukv[:, :], start=True, stop=True)
                    else:
                        pe.matmul(b[:, 0:H * QK], lhsT=QG0[:, t], rhs=wuq[:, 0, :], start=True, stop=False)
                        m = pe.matmul(b[:, 0:H * QK], lhsT=QG1[0:64, t], rhs=wuq[0:64, 1, :], start=False, stop=True)
                    done(m, key)

                def turn_rows(n):
                    kind, i = jobs[n]
                    key = (kind + "t", l, i)
                    b = claim(key)
                    pe.wait_ge(s["row2"], n + 1)
                    for h in range(H):
                        m = pe.transpose(b[0:QK, h * P:(h + 1) * P], rows[:, n % 2, h, :], ident[:, :])
                    done(m, key)

                project(0)
                project(1)
                for n in range(len(jobs)):
                    if n + 2 < len(jobs):
                        project(n + 2)
                    turn_rows(n)
                    if n == 3:
                        for x in first_banks:
                            held.remove(x)
                    for m in chunks_after(n, len(jobs)):
                        qkv(m)
                for m in range(8, 12):
                    qkv(m)
                    if m >= 8:
                        for c in (2 * m - 16, 2 * m - 15):
                            pe.wait_ge(s["lsq"], c + 1)
                            for g in (0, 1):
                                t0, n = SEGS[g]
                                key = ("ln", l, c, g)
                                b = claim(key)
                                done(pe.matmul(b[:, 0:n], lhsT=ones[:, :], rhs=l2b[:, c % 2, t0:t0 + n], start=True,
                                               stop=True), key)

                def gate_steps():
                    for m in range(4):
                        if m % 2 == 0:
                            w = weights(("in", l, 10 + m // 2))
                        bs = [(g, ("in", l, "z%d" % m, g)) for g in segs]
                        bs = [(g, key, claim(key)) for g, key in bs]
                        held.extend(where[key][0] for _, key, _ in bs)
                        for k in range(KD):
                            for g, key, b in bs:
                                t0, n = SEGS[g]
                                x = pe.matmul(b[:, 0:n], lhsT=w[:, k, m % 2 * P:(m % 2 + 1) * P],
                                              rhs=hT[:, k, t0:t0 + n], start=k == 0, stop=k == KD - 1)
                                if k == KD - 1:
                                    done(x, key)
                                    held.remove(where[key][0])
                            if k == KD - 1 and m % 2:
                                last_use(None, key)
                            yield

                calls = [(i, h) for i in tiles for h in range(H)]

                def keys_of(i):
                    return (CT,) if i < CT else (4, 2)

                def scores(i, h):
                    k0 = 0
                    for part, nk in enumerate(keys_of(i)):
                        key = ("s", l, i, h, part)
                        b = claim(key)
                        done(pe.matmul(b[:, 0:nk * P], lhsT=QT[0:QK, h, i * P:(i + 1) * P],
                                       rhs=KT[0:QK, h, k0:k0 + nk * P], start=True, stop=True), key)
                        k0 += nk * P

                evacuated(pe, (jobs[-1][0] + "t", l, jobs[-1][1]))
                evacuated(pe, (jobs[-2][0] + "t", l, jobs[-2][1]))
                gate = gate_steps()
                scores(*calls[0])
                obank = None
                for n, (i, h) in enumerate(calls):
                    if h == 0:
                        obank = claim(("o", l, i))
                        held.append(where[("o", l, i)][0])
                    if n + 1 < len(calls):
                        scores(*calls[n + 1])
                    next(gate, None)
                    for part in range(len(keys_of(i))):
                        evacuated(pe, ("s", l, i, h, part))
                    k0 = 0
                    for part, nk in enumerate(keys_of(i)):
                        key = ("pt", l, i, h, part)
                        b = claim(key)
                        for j in range(nk):
                            m = pe.transpose(b[:, j * P:(j + 1) * P], PR[:, (k0 + j) * P:(k0 + j + 1) * P],
                                             ident[:, :])
                        done(m, key)
                        k0 += nk
                    next(gate, None)
                    for part in range(len(keys_of(i))):
                        evacuated(pe, ("pt", l, i, h, part))
                    for j in range(k0):
                        m = pe.matmul(obank[:, h * DV:(h + 1) * DV], lhsT=PT[:, j, :],
                                      rhs=V[:, j, h * DV:(h + 1) * DV], start=j == 0, stop=j == k0 - 1)
                    if h < H - 1:
                        m.then_inc(s["pv"], 1)
                    else:
                        done(m, ("o", l, i))
                        held.remove(where[("o", l, i)][0])
                        key = ("at", l, i)
                        b = claim(key)
                        evacuated(pe, ("o", l, i))
                        for c in range(2):
                            m = pe.transpose(b[:, c * P:(c + 1) * P], att_of(i)[:, c, :], ident[:, :])
                        done(m, key)

                for c in range(2):
                    for g in segs:
                        key = ("pm", l, c, g)
                        b = claim(key)
                        pe.wait_ge(s["pool"], c + 1)
                        t0, n = SEGS[g]
                        done(pe.matmul(b[:, 0:n], lhsT=poolw[:, c, :], rhs=dT[:, c, t0:t0 + n], start=True,
                                       stop=True), key)

                pe.wait_ge(s_const, 16 * CONST_DMAS)
                b = claim(("gc", l))
                pe.wait_ge(s["att"], 1)
                pe.wait_ge(s["gbd"], 1)
                for d in range(2):
                    for i in range(NT):
                        c0 = (d * NT + i) * GH
                        m = pe.matmul(b[:, c0:c0 + GH], lhsT=tri[:, d, :], rhs=gb[:, 0, i, d * GH:(d + 1) * GH],
                                      start=True, stop=True)
                done(m, ("gc", l))
                pe.wait_ge(s["lmul"], 2 * GH)

                def heads(key, f, wait=None):
                    b = claim(key)
                    for h in range(GH):
                        m = f(b[:, h * P:(h + 1) * P], h)
                    done(m, key)

                for j in range(NT):
                    ti = [tile_of(d, j) for d in range(2)]
                    tt = [slice(i * P, (i + 1) * P) for i in ti]
                    use_o = [need_ctx or i >= CT for i in ti]
                    for d in range(2):
                        key = ("g", l, j, d)
                        b = claim(key)
                        pe.wait_ge(s["tg"], 2 * j + d + 1)
                        done(pe.matmul(b, lhsT=ones[:, :], rhs=gML[d].rearrange("p h c -> p (h c)"), start=True,
                                       stop=True), key)
                    for d in range(2):
                        heads(("kk", l, j, d), lambda o, h: pe.matmul(
                            o, lhsT=qkvT[:, GH + h, tt[d]], rhs=qkvT[:, GH + h, tt[d]], start=True, stop=True))
                        if use_o[d]:
                            heads(("qk", l, j, d), lambda o, h: pe.matmul(
                                o, lhsT=qkvT[:, GH + h, tt[d]], rhs=qkvT[:, h, tt[d]], start=True, stop=True))
                    if l == 0 and j:
                        ada_columns(("am", j), dTrow, ada_keys(j - 1))
                    for d in range(2):
                        evacuated(pe, ("kk", l, j, d))
                        heads(("at2", l, j, d), lambda o, h: pe.transpose(o, gY[d][:, h, :], ident[:, :]))
                    for n in range(1, LEVELS):
                        for d in range(2):
                            if n == 1:
                                pe.wait_ge(s["x0"], 2 * j + d + 1)
                                pe.wait_ge(s["x1"], 2 * j + d + 1)
                            else:
                                for q in range(2):
                                    evacuated(pe, ("xx", l, j, d, n - 1, q))
                            pe.wait_ge(s["ml"], 2 * (j * (LEVELS - 1) + n - 1) + d + 1)
                            heads(("y", l, j, d, n), lambda o, h: pe.matmul(
                                o, lhsT=gML[d][:, h, :], rhs=gX[d][:, h, 0, :], start=True, stop=True))
                        if l == 0:
                            ada_later(0)
                        for d in range(2):
                            evacuated(pe, ("y", l, j, d, n))
                            for q in range(2):
                                key = ("xx", l, j, d, n, q)
                                b = claim(key)
                                for e in range(2):
                                    h = 2 * q + e
                                    if n < LEVELS - 1:
                                        pe.matmul(b[:, 2 * e * P:(2 * e + 1) * P], lhsT=gX[d][:, h, 1, :],
                                                  rhs=gY[d][:, h, :], start=True, stop=True)
                                    m = pe.matmul(b[:, (2 * e + 1) * P:(2 * e + 2) * P], lhsT=gY[d][:, h, :],
                                                  rhs=gX[d][:, h, 1, :], start=True, stop=True)
                                done(m, key)
                        if l == 0:
                            ada_later(1)
                    if j == 0:
                        pe.wait_ge(s["qkv"], 24)
                    for d in range(2):
                        heads(("kr", l, j, d), lambda o, h: pe.transpose(o, qkvT[:, GH + h, tt[d]], ident[:, :]))
                        heads(("vr", l, j, d), lambda o, h: pe.transpose(o, qkvT[:, 2 * GH + h, tt[d]], ident[:, :]))
                    for d in range(2):
                        evacuated(pe, ("kr", l, j, d))
                        for q in range(2):
                            evacuated(pe, ("xx", l, j, d, LEVELS - 1, q))
                        heads(("wt", l, j, d), lambda o, h: pe.matmul(
                            o, lhsT=gAT[d][:, h, :], rhs=gX[d][:, h, 1, :], start=True, stop=True))
                    for d in range(2):
                        evacuated(pe, ("wt", l, j, d))
                        evacuated(pe, ("vr", l, j, d))
                        if j:
                            evacuated(pe, ("st", l, j - 1, d))
                        key = ("v", l, j, d)
                        b = claim(key)
                        for h in range(GH):
                            o = b[:, h * P:(h + 1) * P]
                            m = pe.matmul(o, lhsT=gX[d][:, h, 1, :], rhs=gY[d][:, h, :], start=True, stop=j == 0)
                            if j:
                                m = pe.matmul(o, lhsT=gML[d][:, h, :], rhs=S[:, d, h, :], start=False, stop=True)
                        done(m, key)
                    for d in range(2):
                        evacuated(pe, ("v", l, j, d))
                        if use_o[d]:
                            key = ("go", l, j, d)
                            b = claim(key)
                            if j:
                                pe.wait_ge(s["qg"], 2 * j + d + 1)
                            evacuated(pe, ("qk", l, j, d))
                            for h in range(GH):
                                o = b[:, h * P:(h + 1) * P]
                                if j:
                                    pe.matmul(o, lhsT=S[:, d, h, :], rhs=gQG[d][:, h, :], start=True, stop=False)
                                m = pe.matmul(o, lhsT=gY[d][:, h, :], rhs=gQK[d][:, h, :], start=j == 0, stop=True)
                            done(m, key)
                        if j < NT - 1:
                            heads(("st", l, j, d), lambda o, h: pe.matmul(
                                o, lhsT=gKD[d][:, h, :], rhs=gY[d][:, h, :], start=True, stop=True))

                if l == 0:
                    ada_columns(("am", NT), dTrow, ada_keys(NT - 1))
                    for n in range(ADA_GROUP * NT, len(ADA_LATER)):
                        ada_later(0)
                        ada_later(1)
                    ada_columns(("am", NT + 1), dTrow, ada_keys(NT))

                for h in range(GH):
                    pe.wait_ge(s["osq"], h + 1)
                    for g in segs:
                        t0, n = SEGS[g]
                        key = ("on", l, h, g)
                        b = claim(key)
                        done(pe.matmul(b[:, 0:n], lhsT=ones[:, :], rhs=sqb[:, h % 2, t0:t0 + n], start=True,
                                       stop=True), key)

                for c in range(2):
                    for g in segs:
                        evacuated(pe, ("pm", l, c, g))
                pe.wait_ge(s["mixd"], GH)
                for j in range(4):
                    w = weights(("out", l, j))
                    for c in range(2):
                        for g in segs:
                            t0, n = SEGS[g]
                            key = ("y", l, 2 * j + c, g)
                            b = claim(key)
                            for k in range(KD):
                                m = pe.matmul(b[:, 0:n], lhsT=w[:, k, c * P:(c + 1) * P], rhs=mixT[:, k, t0:t0 + n],
                                              start=k == 0, stop=k == KD - 1)
                            done(m, key)
                    last_use(None, ("y", l, 2 * j + 1, 1))

                sum_over_partitions(l, 2, "sq2", "sqd2")

                bs = [(g, claim(("rtT", l, g))) for g in segs]
                for k in range(KD):
                    pe.wait_ge(s["h2"], k + 1)
                    for g, b in bs:
                        t0, n = SEGS[g]
                        m = pe.matmul(b[0:N_EXP, 0:n], lhsT=router[:, k, :], rhs=hT[:, k, t0:t0 + n], start=k == 0,
                                      stop=k == KD - 1)
                        if k == KD - 1:
                            done(m, ("rtT", l, g))
                for g in segs:
                    evacuated(pe, ("rtT", l, g))
                token_rows(("rt", l), rtrow, tiles)
                for i in tiles:
                    for q in range(2):
                        key = ("hr", l, i, q)
                        b = claim(key)
                        for j in range(4):
                            m = pe.transpose(b[:, j * P:(j + 1) * P], hT[:, 4 * q + j, i * P:(i + 1) * P],
                                             ident[:, :])
                        done(m, key)
                pe.wait_ge(s["aff"], 1)
                for g in segs:
                    key = ("aT", l, g)
                    b = claim(key)
                    t0, n = SEGS[g]
                    for i in range(n // P):
                        m = pe.transpose(b[0:N_EXP, i * P:(i + 1) * P], aff[:, t0 // P + i, :], ident[:, :])
                    done(m, key)
                pe.wait_ge(s["sel"], len(segs))
                key = ("slot", l)
                b = claim(key)
                for i in tiles:
                    m = pe.transpose(b[:, i * N_EXP:(i + 1) * N_EXP], sel[0:N_EXP, i * P:(i + 1) * P],
                                     ident[0:N_EXP, 0:N_EXP])
                done(m, key)

                parts = [(0, range(CT, NT), 0, 8), (1, range(CT, NT), 8, 16)]
                if need_ctx:
                    parts.append((2, range(CT), 0, 16))
                bs = {x: claim(("mr", l, x)) for x, _, _, _ in parts}
                order = list(range(CT, NT)) + (list(range(CT)) if need_ctx else [])
                for x, ts, e0, e1 in parts:
                    for t in ts:
                        pe.wait_ge(s["G"], order.index(t) + 1)
                        g = G[t - CT] if t >= CT else G[SEQ // P + t]
                        m = pe.matmul(bs[x][0:NW, :], lhsT=tokaff[:, t, :],
                                      rhs=g[:, e0:e1, :].rearrange("p e c -> p (e c)"), start=t == ts[0],
                                      stop=t == ts[-1])
                    done(m, ("mr", l, x))
                for g in reversed(segs):
                    for x, _, _, _ in parts:
                        if (x < 2) == (g == 1):
                            evacuated(pe, ("mr", l, x))
                    key = ("mc", l, g)
                    b = claim(key)
                    c0 = 0 if g else N_EXP * CAP_L
                    for p in range(PAIRS):
                        m = pe.transpose(b[:, p * NW:(p + 1) * NW], mrow[:, c0 + p * P:c0 + (p + 1) * P],
                                         ident[0:NW, 0:NW])
                    done(m, key)

                outs = ["y0", "y1"] + (["yc"] if need_ctx else [])
                seq = ["g0", "u0", "g1", "h0", "u1"] + outs + ["h1", "x0", "x1", "x2", "x3"]
                seq += ["c%d%d" % (k, g) for k in range(KD) for g in reversed(segs)]

                def pair(claim_, done_, weights_, free_, here, i, nxt):
                    def by_slot(n, name):
                        w = [weights_(n + e, KD) for e in range(2)]
                        b = claim_(name)
                        for k in range(KD):
                            for e in range(2):
                                m = pe.matmul(b[e * CAP_L:(e + 1) * CAP_L, 0:2 * P], lhsT=xs[:, k, e, 0:CAP_L],
                                              rhs=w[e][:, k, :], start=k == 0, stop=k == KD - 1)
                        if need_ctx:
                            for k in range(KD):
                                for e in range(2):
                                    for f in range(2):
                                        r = (2 * e + f) * CAP_C
                                        m = pe.matmul(b[r:r + CAP_C, 2 * P:3 * P], lhsT=xs[:, k, e, CAP_L:CAP],
                                                      rhs=w[e][:, k, f * P:(f + 1) * P], start=k == 0,
                                                      stop=k == KD - 1)
                        done_(m, name)
                        free_(None, name)
                        free_(None, name)

                    def turn_hidden(q):
                        b = claim_("h%d" % q)
                        evacuated(pe, here("u%d" % q), i)
                        for j in range(3 if need_ctx else 2):
                            m = pe.transpose(b[:, j * P:(j + 1) * P], hid[:, q, j * P:(j + 1) * P], ident[:, :])
                        done_(m, "h%d" % q)

                    def down(q, ys):
                        w = [weights_(8 + 2 * q + e, 2) for e in range(2)]
                        evacuated(pe, here("h%d" % q), i)
                        for c in range(2):
                            for f in range(2):
                                for e in range(2):
                                    m = pe.matmul(ys[c][e * CAP_L:(e + 1) * CAP_L, :],
                                                  lhsT=hidT[:, q, f * P + e * CAP_L:f * P + (e + 1) * CAP_L],
                                                  rhs=w[e][:, f, c * 512:(c + 1) * 512], start=q == 0 and f == 0,
                                                  stop=q == 1 and f == 1)
                            if q == 1:
                                done_(m, "y%d" % c)
                        if need_ctx:
                            for f in range(2):
                                for c in range(2):
                                    for e in range(2):
                                        r = (2 * c + e) * CAP_C
                                        h0 = 2 * P + (2 * e + f) * CAP_C
                                        m = pe.matmul(ys[2][r:r + CAP_C, :], lhsT=hidT[:, q, h0:h0 + CAP_C],
                                                      rhs=w[e][:, f, c * 512:(c + 1) * 512],
                                                      start=q == 0 and f == 0, stop=q == 1 and f == 1)
                            if q == 1:
                                done_(m, "yc")
                        free_(m if q == 0 else None, None if q == 0 else outs[-1])
                        free_(None, None if q == 0 else outs[-1])

                    by_slot(0, "g0")
                    by_slot(2, "u0")
                    by_slot(4, "g1")
                    turn_hidden(0)
                    by_slot(6, "u1")
                    ys = [claim_(name) for name in outs]
                    down(0, ys)
                    turn_hidden(1)
                    if nxt is not None:
                        pe.wait_ge(s["gath"], nxt)
                        turn_tokens(claim_, done_, (0, 1))
                    down(1, ys)
                    if nxt is not None:
                        turn_tokens(claim_, done_, (2, 3))
                    for name in outs:
                        evacuated(pe, here(name), i)
                    pe.wait_ge(s["S"], plus(1, 1, i) if i is not None else PAIRS)
                    for k in range(KD):
                        for g in reversed(segs):
                            name = "c%d%d" % (k, g)
                            b = claim_(name)
                            if g:
                                m = pe.matmul(b[:, 0:SEQ], lhsT=ylat[:, k * P:(k + 1) * P], rhs=Sl[:, :], start=True,
                                              stop=True)
                            else:
                                r = slice(64 * (k // 4), 64 * (k // 4) + 2 * CAP_C)
                                m = pe.matmul(b[:, 0:CTX], lhsT=yctx[r, k % 4 * P:(k % 4 + 1) * P], rhs=Sc[r, :],
                                              start=True, stop=True)
                            done_(m, name)
                    if nxt is not None:
                        for q in range(4):
                            evacuated(pe, here("x%d" % q), i)

                def turn_tokens(claim_, done_, qs):
                    for q in qs:
                        b = claim_("x%d" % q)
                        for e in range(2):
                            k = 2 * q + e
                            o = b[:, e * 2 * CAP:(e + 1) * 2 * CAP]
                            m = pe.transpose(o[:, 0:2 * CAP_L], xlat[:, k * P:(k + 1) * P], ident[:, :])
                            if need_ctx:
                                m = pe.transpose(o[:, 2 * CAP_L:2 * CAP], xctx[0:2 * CAP_C, k * P:(k + 1) * P],
                                                 ident[0:2 * CAP_C, 0:2 * CAP_C])
                        done_(m, "x%d" % q)

                per_pair = 16 * len(segs)
                pe.wait_ge(s["gath"], per_pair)
                turn_tokens(lambda name: claim(("first", l, name)), lambda m, name: done(m, ("first", l, name)),
                            range(4))
                for q in range(4):
                    evacuated(pe, ("first", l, "x%d" % q))

                per = [0] * BANKS
                for n in range(len(seq)):
                    per[(turn[0] + n) % BANKS] += 1
                seen = [0] * BANKS
                for n, name in enumerate(seq):
                    b = (turn[0] + n) % BANKS
                    where[("moe", l, name)] = (b, uses[b] + seen[b], per[b])
                    seen[b] += 1
                r0 = len(loads)

                with pe.Fori(0, PAIRS - 1) as i:
                    def claim2(name):
                        b, n, per = where[("moe", l, name)]
                        pe.wait_ge(bank_free[b], i * per + n)
                        return psum[:, b, :]

                    def done2(ins, name):
                        ins.then_inc(bank_full[where[("moe", l, name)][0]], 1)

                    def weights2(n, k):
                        m = r0 + n
                        pe.wait_ge(slot_full[m % SLOTS], i * (16 * 12 // SLOTS) + 16 * (m // SLOTS + 1))
                        return ring[:, m % SLOTS, :].rearrange("p (k c) -> p k c", k=k)

                    def free2(ins, name):
                        if ins is not None:
                            ins.then_inc(slot_used, 1)

                    pair(claim2, done2, weights2, free2, lambda name: ("moe", l, name), i,
                         i * per_pair + 2 * per_pair)
                for b in range(BANKS):
                    uses[b] += (PAIRS - 1) * per[b]
                for i in range(PAIRS - 1):
                    freed[0] += 1
                    for n in range(12):
                        e, m = expert_part(n)
                        loads.append(("moe", l, 2 * i + e, m))
                        name = ("g0", "u0", "g1", "u1", None, outs[-1])[m]
                        freed_by.append((("moe", l, name), i) if name else freed[0])

                def weights1(n, k):
                    e, m = expert_part(n)
                    w = weights(("moe", l, N_EXP - 2 + e, m))
                    return w.rearrange("p k c -> p (k c)").rearrange("p (k c) -> p k c", k=k)

                def last(name):
                    return ("last", l, name)

                def free1(ins, name):
                    if ins is not None:
                        last_use(ins)
                    else:
                        freed_by.append((last(name), None) if name else freed[0])

                pair(lambda name: claim(last(name)), lambda m, name: done(m, last(name)), weights1, free1, last,
                     None, None)

            evacuated(pe, ("last", DEPTH - 1, "c%d1" % (KD - 1)))
            for i in range(CT, NT):
                for q in range(2):
                    key = ("out", i, q)
                    b = claim(key)
                    for j in range(4):
                        m = pe.transpose(b[:, j * P:(j + 1) * P], xT[:, 4 * q + j, i * P:(i + 1) * P], ident[:, :])
                    done(m, key)

        @block.sync
        def _(sp):
            sp.dma_start(big[:, 0:CT * D].rearrange("p (i d) -> p i d", i=CT),
                         A["ctx"][0].rearrange("(i p) d -> p i d", p=P)).then_inc(s_xin, 16)
            sp.dma_start(big[:, CT * D:NT * D].rearrange("p (i d) -> p i d", i=NT - CT),
                         A["x"][0].rearrange("(i p) d -> p i d", p=P)).then_inc(s_xin, 16)

            def slot(n, k, c):
                return ring[:, n % SLOTS, :].rearrange("p (k c) -> p k c", k=k)[:, :, 0:c]

            def slot_free(n):
                if n >= SLOTS:
                    how = freed_by[n - SLOTS]
                    if isinstance(how, int):
                        sp.wait_ge(slot_used, how)
                    else:
                        product_ready(sp, how[0], how[1])

            def columns(n, src, c0, c1):
                slot_free(n)
                sp.dma_start(slot(n, KD, c1 - c0), src.rearrange("(k p) c -> p k c", p=P)[:, :, c0:c1]
                             ).then_inc(slot_full[n % SLOTS], 16)

            def expert(n, l, e, m):
                if m < 4:
                    w = A["moe_w_gate"] if m % 2 == 0 else A["moe_w_up"]
                    c0 = (m // 2) * SLOT_COLS
                    src = w[l, e].rearrange("(k p) f -> p k f", p=P)[:, :, c0:c0 + SLOT_COLS]
                    dst = slot(n, KD, SLOT_COLS)
                else:
                    src = A["moe_w_down"][l, e].rearrange("(k p) d -> p k d", p=P)[:, 2 * (m - 4):2 * (m - 4) + 2, :]
                    dst = slot(n, 2, D)
                sp.dma_start(dst, src).then_inc(slot_full[n % SLOTS], 16)

            n = 0
            for l in range(DEPTH):
                while loads[n][0] in ("ada", "in", "out"):
                    kind, m, g = loads[n]
                    if kind == "in":
                        columns(n, A["w_in"][m], *IN_LOADS[g][1:])
                    else:
                        columns(n, A["ada_w" if kind == "ada" else "w_out"][m], g * SLOT_COLS, (g + 1) * SLOT_COLS)
                    n += 1
                for m in range(6):
                    slot_free(n + m)
                    expert(n + m, l, *expert_part(m))
                with sp.Fori(0, PAIRS - 1) as i:
                    for m in range(12):
                        if m == 1 or m % 2 == 0 and m != 2:
                            how = freed_by[n + (2 if m == 1 else m)]
                            if isinstance(how, int):
                                sp.wait_ge(slot_used, i + how)
                            else:
                                product_ready(sp, how[0], i)
                        e, part = expert_part((m + 6) % 12)
                        expert(n + 6 + m, l, 2 * i + (e + 2 if m >= 6 else e), part)
                n += 12 * (PAIRS - 1)
                for m in range(6, 12):
                    slot_free(n + m)
                    e, part = expert_part(m)
                    expert(n + m, l, N_EXP - 2 + e, part)
                n += 12
            assert n == len(loads)
            orow = big[:, 0:(NT - CT) * D].rearrange("p (i d) -> p i d", i=NT - CT)
            for i in range(NT - CT):
                for q in range(2):
                    evacuated(sp, ("out", CT + i, q))
                sp.dma_start(out[0, i * P:(i + 1) * P, :], orow[:, i, :]).then_inc(s_out, 16)
            sp.wait_ge(s_out, 16 * (NT - CT))

        @block.scalar
        def _(act):
            act.dma_start(ident[:, :], A["k_ident"]).then_inc(s_ident, 16)
            act.dma_start(arena[0:8, 11 * T:11 * T + P], A["c"].rearrange("b (k p) -> (b k) p", p=P)).then_inc(s_ident, 16)
            act.dma_start(arena[8:16, 11 * T:11 * T + P], A["c_ctx"].rearrange("(k p) -> k p", p=P)).then_inc(s_ident, 16)
            act.wait_ge(sems[0]["zero"], 1)
            channel_parameters(act, 0)
            act.dma_start(iota[:, :], A["k_iota"]).then_inc(s_sum, 16)
            for dst, name in ((tri[:, :, :], "k_tri"), (rope[:, :, :, :], "k_rope"),
                              (poolc[:, :, :], "k_pool"), (lev[:, :, :, :], "k_lev")):
                act.dma_start(dst, A[name]).then_inc(s_const, 16)

            def squares(l, which, k):
                s = sems[l]
                t0 = 0 if which == 1 or l == 0 else CTX
                if k >= 2:
                    act.wait_ge(s["sqd%d" % which], k - 1)
                act.activation(sqb[:, k % 2, t0:T], xT[:, k, t0:T], ACT.Square).then_inc(s["sq%d" % which], 1)

            def inverse_roots(l, dst, keys, bias, scale):
                for key in keys:
                    t0, n = SEGS[key[-1]]
                    b = product_ready(act, key)
                    read_out(act.activation(dst[:, t0:t0 + n], b[:, 0:n], ACT.Ln, bias=bias, scale=scale), key)
                for key in keys:
                    evacuated(act, key)
                t0 = min(SEGS[key[-1]][0] for key in keys)
                act.activation(dst[:, t0:T], dst[:, t0:T], ACT.Exp, scale=-0.5).then_inc(sems[l]["rinv"], 1)

            def ada_rows(row, keys):
                for n, key in enumerate(keys):
                    b = product_ready(act, key)
                    for r in range(0, ADA_ROWS, 32):
                        m = act.copy(row[r:r + 2, n * SLOT_COLS:(n + 1) * SLOT_COLS], b[r:r + 2, 0:SLOT_COLS])
                    read_out(m, key)

            def ada_group(group):
                key = ("am", group + 1)
                m0 = 2 * (ADA_FIRST + group * ADA_GROUP)
                n = 2 * len(ada_keys(group))
                b = product_ready(act, key)
                read_out(act.copy(modraw[:, m0:m0 + n, :].rearrange("p m c -> p (m c)"), b[:, 0:2 * n]), key)

            def norm(l, which):
                s = sems[l]
                segs = (1, 0) if which == 1 or l == 0 else (1,)
                inverse_roots(l, rstd, [("ss", l, which, g) for g in segs], eps[:, 0:1], 1.0 / D)
                if l == 0 and which == 1:
                    act.wait_ge(s["zrow"], 1)
                    ada_rows(szrow, [("ar", 0, g) for g in range(ADA_FIRST)])
                act.wait_ge(s["mods%d" % which], 1)
                for k in range(KD):
                    act.wait_ge(s["hx%d" % which], k + 1)
                    for g in segs:
                        t0, n = SEGS[g]
                        c = 1 - g
                        m = act.activation(hT[:, k, t0:t0 + n], hT[:, k, t0:t0 + n], ACT.Identity,
                                           bias=mods_of[l][:, (0 if which == 1 else 3) * KD + k, c:c + 1],
                                           scale=amod_of[l][:, which - 1, k, c:c + 1])
                    m.then_inc(s["h%d" % which], 1)

            def narrow(l, name, dst, gs):
                for g in gs:
                    t0, n = SEGS[g]
                    key = ("in", l, name, g) if name != "rtT" else ("rtT", l, g)
                    b = product_ready(act, key)
                    read_out(act.copy(dst[:, t0:t0 + n], b[0:dst.shape[0], 0:n]), key)

            act.wait_ge(s_ones, 1)
            for k in range(KD):
                b = product_ready(act, ("x", k, 1))
                read_out(act.copy(xT[:, k, 512:T], b[:, 0:256]), ("x", k, 1))
            b = product_ready(act, "c")
            read_out(act.activation(scol[:, :, :].rearrange("p a b -> p (a b)"), b[:, 0:16], ACT.Silu), "c")

            for l in range(DEPTH):
                s = sems[l]
                need_ctx = l < DEPTH - 1
                tiles = range(NT) if need_ctx else range(CT, NT)
                segs = (0, 1) if need_ctx else (1,)
                t_first = tiles[0] * P

                if l == 0:
                    for k in range(KD):
                        evacuated(act, ("x", k, 0))
                        evacuated(act, ("x", k, 1))
                        squares(l, 1, k)
                else:
                    for k in range(KD):
                        for g in (0, 1):
                            evacuated(act, ("last", l - 1, "c%d%d" % (k, g)))
                        squares(l, 1, k)
                norm(l, 1)

                act.wait_ge(s["upad"], 1)
                for c in range(2):
                    for g in segs:
                        key = ("in", l, "pool%d" % c, g)
                        b = product_ready(act, key)
                        n = SEGS[g][1]
                        read_out(act.copy(U[:, c, UO[g]:UO[g] + n], b[:, 0:n]), key)
                narrow(l, "ab", abrow, (0, 1))
                for name, dst, m, gs in (("ql0", SQ0, P, segs), ("ql1", SQ1, 64, segs), ("kv", SQK, P, (0, 1))):
                    for g in gs:
                        t0, n = SEGS[g]
                        b = product_ready(act, ("in", l, name, g))
                        act.activation(dst[0:m, t0:t0 + n], b[0:m, 0:n], ACT.Square).then_inc(s["sqm"], 1)
                narrow(l, "krp", krow, (0, 1))
                b = product_ready(act, ("rs", l))[:, 0:2 * NT].rearrange("p (i w) -> p i w", w=2)
                act.activation(rs12[:, tiles[0]:NT, 0:1], b[:, tiles[0]:NT, 0:1], ACT.Sqrt, bias=eps[:, 0:1],
                               scale=1.0 / Q_LORA)
                read_out(act.activation(rs12[:, :, 1:2], b[:, :, 1:2], ACT.Sqrt, bias=eps[:, 0:1],
                                        scale=1.0 / KV_LORA), ("rs", l))
                b = product_ready(act, ("krp", l))
                read_out(act.copy(krp.rearrange("p i c -> p (i c)"), b[:, 0:NT * ROPE]), ("krp", l))

                jobs = [("k", i) for i in range(NT)] + [("q", i) for i in tiles]

                def turned(n):
                    kind, i = jobs[n]
                    key = (kind + "t", l, i)
                    b = product_ready(act, key)
                    dst = (KT if kind == "k" else QT)[0:QK, :, i * P:(i + 1) * P]
                    read_out(act.copy(dst, b[0:QK, :].rearrange("p (h c) -> p h c", h=H)), key)

                def middle_tap(m):
                    for g in (0, 1):
                        t0, w = SEGS[g]
                        b = product_ready(act, ("in", l, "qkv%d" % m, g))
                        cc = COL_CONV + 12 + m
                        act.activation(qkvT[:, m, t0:t0 + w], b[:, 0:w], ACT.Copy, scale=cols[:, cc:cc + 1]
                                       ).then_inc(s["cv1"], 1)

                def silu(m):
                    for g in (0, 1):
                        t0, w = SEGS[g]
                        evacuated(act, ("in", l, "qkv%d" % m, g))
                        act.activation(qkvT[:, m, t0:t0 + w], qkvT[:, m, t0:t0 + w], ACT.Silu).then_inc(s["qkv"], 1)

                for n in range(len(jobs)):
                    act.wait_ge(s["row1"], n + 1)
                    act.activation(ss4[:, n % 2, :], ss4[:, n % 2, :], ACT.Sqrt, bias=eps[:, 0:1],
                                   scale=1.0 / QK).then_inc(s["rowr"], 1)
                    if n:
                        turned(n - 1)
                    if n == 2:
                        act.wait_ge(s["pool"], 2)
                        middle_tap(0)
                    for m in chunks_after(n - 1, len(jobs)):
                        middle_tap(m)
                turned(len(jobs) - 1)

                act.wait_ge(s["abraw"], 1)
                act.activation(abe[:, :, :], abe[:, :, :], ACT.Exp, scale=-1.0).then_inc(s["abexp"], 1)
                act.activation(abw[:, 1, :, :], abw[:, 1, :, :], ACT.Exp, scale=-1.0)
                act.activation(ealog, gpar[:, 0, :], ACT.Exp)
                act.wait_ge(s["abexp"], 1)
                act.activation(abe[:, :, :], abe[:, :, :], ACT.Ln, bias=ones[:, 0:1]).then_inc(s["abln"], 1)

                def lsquare(c):
                    act.wait_ge(s["qkv"], 2 * (c + 1))
                    if c >= 2:
                        act.wait_ge(s["lmul"], c - 1)
                    act.activation(l2b[:, c % 2, :], qkvT[:, c, :], ACT.Square).then_inc(s["lsq"], 1)

                for m in range(8):
                    silu(m)
                for m in range(7, 12):
                    if m > 7:
                        middle_tap(m)
                        for c in (2 * m - 16, 2 * m - 15):
                            q = c < GH
                            inverse_roots(l, l2b[:, c % 2, :], [("ln", l, c, g) for g in (0, 1)],
                                          eps[:, 1:2] if q else eps[:, 0:1], 128.0 if q else 1.0)
                    if m < 11:
                        lsquare(2 * m - 14)
                        lsquare(2 * m - 13)
                calls = [(i, h) for i in tiles for h in range(H)]

                def turned_att(i):
                    b = product_ready(act, ("at", l, i))
                    read_out(act.copy(QT[:, 0:2, i * P:(i + 1) * P],
                                      b[:, 0:2 * P].rearrange("p (c t) -> p c t", c=2)), ("at", l, i))

                def gate_out(m):
                    for g in segs:
                        t0, w = SEGS[g]
                        key = ("in", l, "z%d" % m, g)
                        b = product_ready(act, key)
                        read_out(act.copy(szT[:, m, t0:t0 + w], b[:, 0:w]), key)

                for n, (i, h) in enumerate(calls):
                    parts = (CT,) if i < CT else (4, 2)
                    if n and n % 4 == 0 and n <= 16:
                        gate_out(n // 4 - 1)
                    act.wait_ge(s["nm"], n + 1)
                    if n:
                        pi, ph = calls[n - 1]
                        product_ready(act, ("pt", l, pi, ph, 0 if pi < CT else 1))
                    if h == 0 and i - tiles[0] >= 2:
                        evacuated(act, ("o", l, i - 2))
                    k0 = 0
                    for part, nk in enumerate(parts):
                        key = ("s", l, i, h, part)
                        b = product_ready(act, key)
                        read_out(act.activation(PR[:, k0 * P:(k0 + nk) * P], b[:, 0:nk * P], ACT.Exp,
                                                bias=nm[:, n % 2:n % 2 + 1], scale=QK ** -0.5,
                                                accum_out=sm[:, i % 2, h, part:part + 1]), key)
                        k0 += nk
                    if h == 0 and n:
                        turned_att(i - 1)
                    if len(parts) == 2:
                        key = ("pt", l, i, h, 1)
                        b = product_ready(act, key)
                        if n:
                            attended(act, l, calls, n - 1)
                        read_out(act.copy(PT[:, 4:6, :].rearrange("p j c -> p (j c)"), b[:, 0:2 * P]), key)
                if len(calls) <= 16:
                    gate_out(3)
                turned_att(NT - 1)
                for i in tiles:
                    evacuated(act, ("at", l, i))
                act.copy(mixT[:, 0:2, t_first:T], QT[:, 0:2, t_first:T]).then_inc(s["att"], 1)
                def gate_silu(m):
                    for g in segs:
                        evacuated(act, ("in", l, "z%d" % m, g))
                    act.activation(szT[:, m, t_first:T], szT[:, m, t_first:T], ACT.Silu)

                evacuated(act, ("gc", l))
                act.activation(bg[:, :, :, :], gc[:, :, :, :], ACT.Exp).then_inc(s["egc"], 1)

                if l == 0:
                    act.wait_ge(s["zrow"], 2)
                for j in range(NT):
                    ti = [tile_of(d, j) for d in range(2)]
                    use_o = [need_ctx or i >= CT for i in ti]
                    for d in range(2):
                        b = product_ready(act, ("g", l, j, d))
                        if j and (need_ctx or tile_of(d, j - 1) >= CT):
                            product_ready(act, ("go", l, j - 1, d))
                        act.wait_ge(s["xg"], 2 * j + d + 1)
                        read_out(act.activation(gQG[d].rearrange("p h c -> p (h c)"), b, ACT.Exp), ("g", l, j, d))
                        act.activation(gD[d], gD[d], ACT.Exp, scale=-1.0)
                        act.activation(gQK[d], gQK[d], ACT.Exp)
                        act.activation(gt4[:, d, :, :], gt4[:, d, :, :], ACT.Exp).then_inc(s["dex"], 1)
                    for d in range(2):
                        b = product_ready(act, ("at2", l, j, d))
                        read_out(act.copy(gAT[d].rearrange("p h c -> p (h c)"), b), ("at2", l, j, d))
                    for n in range(1, LEVELS):
                        if l == 0 and n == 1 and j:
                            ada_group(j - 1)
                        if l == 0 and n > 1:
                            ada_rows(dTrow[:, (n - 2) * SLOT_COLS:], ada_keys(j)[n - 2:n - 1])
                        for d in range(2):
                            key = ("xx", l, j, d, n, 0)
                            b = product_ready(act, key).rearrange("p (e x c) -> p e x c", e=2, x=2)
                            x0 = 0 if n < LEVELS - 1 else 1
                            read_out(act.copy(gX[d][:, 0:2, x0:2, :], b[:, :, x0:2, :]), key)
                        if j == 0 and n <= 4:
                            silu(7 + n)
                        if j == 0 and n > 2:
                            gate_silu(n - 3)
                    if l == 0:
                        ada_rows(dTrow[:, (LEVELS - 2) * SLOT_COLS:], ada_keys(j)[LEVELS - 2:LEVELS - 1])
                    for d in range(2):
                        b = product_ready(act, ("wt", l, j, d))
                        read_out(act.mul(gML[d].rearrange("p h c -> p (h c)"), b, -1.0), ("wt", l, j, d))

                if l == 0:
                    ada_group(NT - 1)
                    ada_rows(dTrow, ada_keys(NT))
                    ada_group(NT)

                for d in range(2):
                    evacuated(act, ("go", l, NT - 1, d))

                def osquare(h):
                    if h >= 2:
                        product_ready(act, ("on", l, h - 2, 1))
                    act.activation(sqb[:, h % 2, t_first:T], mixT[:, 2 + h, t_first:T], ACT.Square
                                   ).then_inc(s["osq"], 1)

                osquare(0)
                osquare(1)
                for h in range(GH):
                    if h >= 2:
                        act.wait_ge(s["mixd"], h - 1)
                    inverse_roots(l, rs_gdn[:, h % 2, :], [("on", l, h, g) for g in segs], eps[:, 0:1], 1.0 / P)
                    if h + 2 < GH:
                        osquare(h + 2)

                for k in range(KD):
                    for g in segs:
                        evacuated(act, ("y", l, k, g))
                    squares(l, 2, k)
                norm(l, 2)

                narrow(l, "rtT", rtrow, segs)
                act.wait_ge(s["rmax"], 1)
                act.activation(aff[:, tiles[0]:NT, :], aff[:, tiles[0]:NT, :], ACT.Exp).then_inc(s["rexp"], 1)
                for i in tiles:
                    b = product_ready(act, ("hr", l, i, 0))
                    read_out(act.copy(hrow[:, i, 0:512], b), ("hr", l, i, 0))

                for g in segs:
                    t0, n = SEGS[g][0] // P, SEGS[g][1] // P
                    for i in range(t0, t0 + n):
                        evacuated(act, ("hr", l, i, 0))
                        evacuated(act, ("hr", l, i, 1))
                    act.dma_start(hD[g].rearrange("(i p) d -> p i d", p=P), hrow[:, t0:t0 + n, :]
                                  ).then_inc(s["hrow"], 16)
                for x in range(3 if need_ctx else 2):
                    b = product_ready(act, ("mr", l, x))
                    if x < 2:
                        m = act.copy(mrow[:, x * 512:(x + 1) * 512], b[0:NW, :])
                    else:
                        m = act.copy(mrow[:, 1024:2048].rearrange("p (i t c) -> p i t c", i=PAIRS, t=2),
                                     b[0:NW, :].rearrange("p (i c) -> p i c", i=PAIRS).unsqueeze(2).to_broadcast(
                                         [NW, PAIRS, 2, 2 * CAP_C]))
                    read_out(m, ("mr", l, x))

                hw = 3 * P if need_ctx else 2 * P

                def tokens(name_of, i, q):
                    key = name_of("x%d" % q)
                    b = product_ready(act, key, i)[:, 0:4 * CAP].rearrange("p (k c) -> p k c", k=2)
                    copy_slots(act.copy, b, xs, q, need_ctx, lambda m: read_out(m, key))

                def pair(here, i, nxt):
                    def copy_out(name, dst):
                        b = product_ready(act, here(name), i)
                        read_out(act.copy(dst, b[:, 0:dst.shape[1]]), here(name))

                    for q in range(2):
                        b = product_ready(act, here("g%d" % q), i)
                        read_out(act.activation(sg[:, q, 0:hw], b[:, 0:hw], ACT.Silu), here("g%d" % q))
                    copy_out("h0", hidT[:, 0, 0:hw])
                    copy_out("h1", hidT[:, 1, 0:hw])
                    if nxt:
                        tokens(here, i, 0)
                    copy_out("y0", ylat[:, 0:512])
                    if need_ctx:
                        copy_out("yc", yctx[:, :])
                    if nxt:
                        tokens(here, i, 2)

                for q in (0, 2):
                    tokens(lambda name: ("first", l, name), None, q)
                with act.Fori(0, PAIRS - 1) as i:
                    pair(lambda name: ("moe", l, name), i, True)
                pair(lambda name: ("last", l, name), None, False)

            orow = big[:, 0:(NT - CT) * D].rearrange("p (i d) -> p i d", i=NT - CT)
            for i in range(CT, NT):
                b = product_ready(act, ("out", i, 0))
                read_out(act.copy(orow[:, i - CT, 0:512], b), ("out", i, 0))

        @block.vector
        def _(dve):
            chain = [0, 0]

            def link(ins, l):
                chain[l] += 1
                ins.then_inc(sems[l]["dve"], 1)
                dve.wait_ge(sems[l]["dve"], chain[l])

            def norm(l, which):
                s = sems[l]
                segs = (1, 0) if which == 1 or l == 0 else (1,)
                t0 = 0 if len(segs) == 2 else CTX
                dve.wait_ge(s["rinv"], 1 if which == 1 else 2 + 3 * GH)
                for k in range(KD):
                    dve.tensor_tensor(hT[:, k, t0:T], xT[:, k, t0:T], rstd[:, t0:T], ALU.mult
                                      ).then_inc(s["hx%d" % which], 1)

            def modulation(l, part):
                m0, m1 = ((0, 2 * KD), (2 * KD, 6 * KD))[part]
                x = mods_of[l][:, m0:m1, :]
                link(dve.tensor_tensor(x, x, cols[:, m0:m1].unsqueeze(2).to_broadcast([P, m1 - m0, 2]), ALU.add), l)
                m0, c0 = ((KD, COL_N1), (4 * KD, COL_N2))[part]
                dve.scalar_tensor_tensor(
                    out=amod_of[l][:, part, :, :], in0=mods_of[l][:, m0:m0 + KD, :], scalar=1.0,
                    in1=cols[:, c0:c0 + KD].unsqueeze(2).to_broadcast([P, KD, 2]), op0=ALU.add,
                    op1=ALU.mult).then_inc(sems[l]["mods%d" % (part + 1)], 1)

            for k in range(KD):
                b = product_ready(dve, ("x", k, 0))
                read_out(dve.tensor_copy(xT[:, k, 0:512], b), ("x", k, 0))

            for l in range(DEPTH):
                s = sems[l]
                need_ctx = l < DEPTH - 1
                tiles = range(NT) if need_ctx else range(CT, NT)
                segs = (0, 1) if need_ctx else (1,)
                i0 = tiles[0]
                t_first = i0 * P

                b = product_ready(dve, ("cols", l))
                read_out(dve.tensor_copy(cols[:, :], b[:, 0:N_COLS]), ("cols", l))
                evacuated(dve, ("cols", l))
                if l == 0:
                    norm(l, 1)
                    b = product_ready(dve, ("am", 0))
                    read_out(dve.tensor_copy(modraw[:, 0:2 * ADA_FIRST, :].rearrange("p m c -> p (m c)"),
                                             b[:, 0:4 * ADA_FIRST]), ("am", 0))
                    evacuated(dve, ("am", 0))
                    modulation(0, 0)
                else:
                    evacuated(dve, ("am", ADA_GROUPS))
                    modulation(l, 0)
                    modulation(l, 1)
                    norm(l, 1)

                b = product_ready(dve, ("ab", l))[:, 0:NT * 16].rearrange("p (i c) -> p i c", i=NT)
                dve.wait_ge(s["par"], 16 * PAR_DMAS)
                link(dve.tensor_tensor(abw[:, 0, :, :], b[:, :, 0:8], gpar[:, 1, :].unsqueeze(1).to_broadcast(
                    [P, NT, 8]), ALU.add), l)
                read_out(dve.tensor_copy(abw[:, 1, :, :], b[:, :, 8:16]), ("ab", l))
                evacuated(dve, ("ab", l))
                dve.scalar_tensor_tensor(out=abe[:, :, :], in0=abw[:, 0, :, :], scalar=-1.0, in1=abw[:, 0, :, :],
                                         op0=ALU.mult, op1=ALU.max).then_inc(s["abraw"], 1)

                n = 0
                for name, dst, m, c, gs in (("ql0", QG0, P, COL_Q, segs), ("ql1", QG1, 64, COL_Q + 1, segs),
                                            ("kv", KVG, P, COL_KV, (0, 1))):
                    for g in gs:
                        t0, w = SEGS[g]
                        n += 1
                        b = product_ready(dve, ("in", l, name, g))
                        dve.wait_ge(s["sqm"], n)
                        read_out(dve.tensor_scalar(dst[0:m, t0:t0 + w], b[0:m, 0:w], cols[0:m, c:c + 1], None,
                                                   ALU.mult), ("in", l, name, g))
                evacuated(dve, ("rs", l))
                link(dve.reciprocal(rs12[:, :, 1:2], rs12[:, :, 1:2]), l)
                link(dve.reciprocal(rs12[:, i0:NT, 0:1], rs12[:, i0:NT, 0:1]), l)
                evacuated(dve, ("krp", l))

                jobs = [("k", i) for i in range(NT)] + [("q", i) for i in tiles]

                def scale_rows(n):
                    kind, i = jobs[n]
                    key = (kind, l, i)
                    r = rows[:, n % 2, :, :]
                    b = product_ready(dve, key)
                    if n >= 2:
                        pk, pi = jobs[n - 2]
                        product_ready(dve, (pk + "t", l, pi))
                    if kind == "q":
                        read_out(dve.tensor_scalar(r, b[:, 0:H * QK].rearrange("p (h c) -> p h c", h=H),
                                                   rs12[:, i, 0:1], None, ALU.mult), key)
                    else:
                        v = b.rearrange("p (h c) -> p h c", h=H)
                        dve.tensor_scalar(V[:, i, :].rearrange("p (h c) -> p h c", h=H), v[:, :, NOPE:NOPE + DV],
                                          rs12[:, i, 1:2], None, ALU.mult)
                        link(dve.tensor_copy(r[:, :, NOPE:QK], krp[:, i, :].unsqueeze(1).to_broadcast([P, H, ROPE])),
                             l)
                        read_out(dve.tensor_scalar(r[:, :, 0:NOPE], v[:, :, 0:NOPE], rs12[:, i, 1:2], None, ALU.mult),
                                 key)
                    evacuated(dve, key)
                    link(dve.tensor_tensor(rtmp, r, r, ALU.mult), l)
                    dve.tensor_reduce(ss4[:, n % 2, :], rtmp, AX.X, ALU.add).then_inc(s["row1"], 1)

                def norm_rows(n):
                    dve.wait_ge(s["rowr"], n + 1)
                    link(dve.reciprocal(ss4[:, n % 2, :], ss4[:, n % 2, :]), l)
                    r = rows[:, n % 2, :, :]
                    dve.tensor_tensor(r, r, ss4[:, n % 2, :].unsqueeze(2).to_broadcast([P, H, QK]), ALU.mult
                                      ).then_inc(s["rowa"], 1)

                def outer_taps(m):
                    for g in (0, 1):
                        t0, n = SEGS[g]
                        key = ("in", l, "qkv%d" % m, g)
                        b = product_ready(dve, key)
                        dve.wait_ge(s["cv1"], 2 * m + g + 1)
                        a = qkvT[:, m, t0 + 1:t0 + n]
                        link(dve.scalar_tensor_tensor(out=a, in0=b[:, 0:n - 1], scalar=cols[:, COL_CONV + m:
                                                      COL_CONV + m + 1], in1=a, op0=ALU.mult, op1=ALU.add), l)
                        a = qkvT[:, m, t0:t0 + n - 1]
                        cc = COL_CONV + 24 + m
                        read_out(dve.scalar_tensor_tensor(out=a, in0=b[:, 1:n], scalar=cols[:, cc:cc + 1], in1=a,
                                                          op0=ALU.mult, op1=ALU.add), key)

                scale_rows(0)
                for n in range(len(jobs)):
                    if n + 1 < len(jobs):
                        scale_rows(n + 1)
                    norm_rows(n)
                    if n == 2:
                        outer_taps(0)
                    for m in chunks_after(n - 1, len(jobs)):
                        outer_taps(m)

                dve.wait_ge(s["abln"], 1)
                link(dve.scalar_tensor_tensor(out=abe[:, :, :], in0=abw[:, 0, :, :], scalar=0.0, in1=abe[:, :, :],
                                              op0=ALU.max, op1=ALU.add), l)
                dve.scalar_tensor_tensor(out=gb[:, 0, :, :], in0=abe[:, :, :], scalar=-1.0,
                                         in1=ealog.unsqueeze(1).to_broadcast([P, NT, 8]), op0=ALU.mult, op1=ALU.mult)
                link(dve.tensor_scalar(abw[:, 1, :, :], abw[:, 1, :, :], 1.0, None, ALU.add), l)
                dve.reciprocal(gb[:, 1, :, :], abw[:, 1, :, :]).then_inc(s["gbd"], 1)

                for m in range(8, 12):
                    outer_taps(m)
                    for c in (2 * m - 16, 2 * m - 15):
                        dve.wait_ge(s["rinv"], 2 + c)
                        dve.tensor_tensor(qkvT[:, c, :], qkvT[:, c, :], l2b[:, c % 2, :], ALU.mult
                                          ).then_inc(s["lmul"], 1)

                calls = [(i, h) for i in tiles for h in range(H)]

                def row_max(n):
                    i, h = calls[n]
                    parts = (CT,) if i < CT else (4, 2)
                    if n >= 2:
                        pi, ph = calls[n - 2]
                        for part in range(1 if pi < CT else 2):
                            evacuated(dve, ("s", l, pi, ph, part))
                    for part, nk in enumerate(parts):
                        b = product_ready(dve, ("s", l, i, h, part))
                        link(dve.reduce_max(mx[:, n % 2, part:part + 1], b[:, 0:nk * P], AX.X), l)
                    w = len(parts) - 1
                    dve.tensor_scalar(nm[:, n % 2:n % 2 + 1], mx[:, n % 2, 0:1], mx[:, n % 2, w:w + 1],
                                      -(QK ** -0.5), ALU.max, ALU.mult).then_inc(s["nm"], 1)

                row_max(0)
                for n, (i, h) in enumerate(calls):
                    if n + 1 < len(calls):
                        row_max(n + 1)
                    nk = CT if i < CT else 4
                    key = ("pt", l, i, h, 0)
                    b = product_ready(dve, key)
                    if n:
                        attended(dve, l, calls, n - 1)
                    read_out(dve.tensor_copy(PT[:, 0:nk, :].rearrange("p j c -> p (j c)"), b[:, 0:nk * P]), key)
                    if h == H - 1:
                        if i >= CT:
                            link(dve.tensor_tensor(rden, sm[:, i % 2, :, 0], sm[:, i % 2, :, 1], ALU.add), l)
                        else:
                            link(dve.tensor_copy(rden, sm[:, i % 2, :, 0]), l)
                        link(dve.reciprocal(rden, rden), l)
                        b = product_ready(dve, ("o", l, i))
                        for c in range(2):
                            m = dve.tensor_tensor(
                                att_of(i)[:, c, :].rearrange("p (h c) -> p h c", h=2),
                                b[:, c * P:(c + 1) * P].rearrange("p (h c) -> p h c", h=2),
                                rden[:, 2 * c:2 * c + 2].unsqueeze(2).to_broadcast([P, 2, DV]), ALU.mult)
                        read_out(m, ("o", l, i))

                for c in range(2):
                    for g in segs:
                        t0, n = SEGS[g]
                        b = product_ready(dve, ("pm", l, c, g))
                        read_out(dve.tensor_scalar(mixT[:, 6 + c, t0:t0 + n], b[:, 0:n],
                                                   cols[:, COL_PS + c:COL_PS + c + 1], None, ALU.mult),
                                 ("pm", l, c, g))

                b = product_ready(dve, ("gc", l))
                read_out(dve.tensor_copy(gc.rearrange("p d i h -> p (d i h)"), b[:, 0:2 * NT * GH]), ("gc", l))
                dve.wait_ge(s["egc"], 1)
                for d in range(2):
                    link(dve.tensor_tensor(bg[:, d, :, :], bg[:, d, :, :], gb[:, 1, :, d * GH:(d + 1) * GH],
                                           ALU.mult), l)

                dve.wait_ge(s_const, 16 * CONST_DMAS)
                dve.wait_ge(s_sum, 16)
                for j in range(NT):
                    ti = [tile_of(d, j) for d in range(2)]
                    tt = [slice(i * P, (i + 1) * P) for i in ti]
                    use_o = [need_ctx or i >= CT for i in ti]
                    for d in range(2):
                        b = product_ready(dve, ("g", l, j, d)).rearrange("p (h c) -> p h c", h=GH)
                        g1 = gc[:, d, ti[d], :]
                        if j:
                            evacuated(dve, ("st", l, j - 1, d))
                        for h in range(GH):
                            dve.tensor_scalar(gD[d][:, h, :], b[:, h, :], g1[:, h:h + 1], 0.0, ALU.subtract, ALU.max)
                            dve.tensor_scalar(gQK[d][:, h, :], b[:, h, :], g1[:, h:h + 1], 0.0, ALU.subtract,
                                              ALU.min)
                        last = P - 1 if d == 0 else 0
                        dve.tensor_tensor(gt4[:, d, 0, :], b[:, :, last], g1, ALU.subtract)
                        dve.tensor_copy(gt4[:, d, 1, :], b[:, :, last]).then_inc(s["xg"], 1)
                    for d in range(2):
                        key = ("kk", l, j, d)
                        b = product_ready(dve, key).rearrange("p (h c) -> p h c", h=GH)
                        dve.wait_ge(s["dex"], 2 * j + d + 1)
                        if j:
                            product_ready(dve, ("st", l, j - 1, d))
                        for h in range(GH):
                            c = d * GH + h
                            m = dve.scalar_tensor_tensor(out=gY[d][:, h, :], in0=b[:, h, :],
                                                         scalar=gb[:, 1, ti[d], c:c + 1], in1=gD[d][:, h, :],
                                                         op0=ALU.mult, op1=ALU.mult)
                        read_out(m, key)
                        evacuated(dve, key)
                        x = gX[d][:, :, 0, :]
                        link(dve.tensor_tensor(x, gY[d], lev[:, 1 - d, 0, :].unsqueeze(1).to_broadcast([P, GH, P]),
                                               ALU.mult), l)
                        dve.tensor_tensor(x, ident[:, :].unsqueeze(1).to_broadcast([P, GH, P]), x, ALU.subtract
                                          ).then_inc(s["x0"], 1)
                    for d in range(2):
                        if use_o[d]:
                            key = ("qk", l, j, d)
                            b = product_ready(dve, key)
                            dve.wait_ge(s["dm"], 2 * j + d + 1)
                            x = gQK[d].rearrange("p h c -> p (h c)")
                            read_out(dve.tensor_tensor(x, b, x, ALU.mult), key)
                    for n in range(1, LEVELS):
                        for d in range(2):
                            key = ("y", l, j, d, n)
                            b = product_ready(dve, key).rearrange("p (h c) -> p h c", h=GH)
                            read_out(dve.tensor_tensor(gY[d], ident[:, :].unsqueeze(1).to_broadcast([P, GH, P]), b,
                                                       ALU.subtract), key)
                        for d in range(2):
                            key = ("xx", l, j, d, n, 1)
                            b = product_ready(dve, key).rearrange("p (e x c) -> p e x c", e=2, x=2)
                            x0 = 0 if n < LEVELS - 1 else 1
                            read_out(dve.tensor_copy(gX[d][:, 2:4, x0:2, :], b[:, :, x0:2, :]), key)
                    for d in range(2):
                        key = ("kr", l, j, d)
                        b = product_ready(dve, key).rearrange("p (h c) -> p h c", h=GH)
                        dve.tensor_tensor(gAT[d], b, bg[:, d, ti[d], :].unsqueeze(2).to_broadcast([P, GH, P]),
                                          ALU.mult)
                        read_out(dve.tensor_tensor(gKD[d], b, gt4[:, d, 0, :].unsqueeze(2).to_broadcast([P, GH, P]),
                                                   ALU.mult), key)
                        key = ("vr", l, j, d)
                        b = product_ready(dve, key).rearrange("p (h c) -> p h c", h=GH)
                        be = gb[:, 1, ti[d], d * GH:(d + 1) * GH]
                        read_out(dve.tensor_tensor(gY[d], b, be.unsqueeze(2).to_broadcast([P, GH, P]), ALU.mult), key)
                    for d in range(2):
                        key = ("v", l, j, d)
                        b = product_ready(dve, key)
                        read_out(dve.tensor_copy(gY[d].rearrange("p h c -> p (h c)"), b), key)
                    for d in range(2):
                        if use_o[d]:
                            key = ("go", l, j, d)
                            b = product_ready(dve, key).rearrange("p (h c) -> p h c", h=GH)
                            o = mixT[:, 2:2 + GH, tt[d]]
                            first = [tile_of(1 - d, x) for x in range(NT)].index(ti[d]) > j
                            if first:
                                read_out(dve.tensor_copy(o, b), key)
                            else:
                                read_out(dve.tensor_tensor(o, b, o, ALU.add), key)
                        if j < NT - 1:
                            key = ("st", l, j, d)
                            b = product_ready(dve, key)
                            if j == 0:
                                read_out(dve.tensor_copy(S[:, d, :, :].rearrange("p h c -> p (h c)"), b), key)
                            else:
                                for h in range(GH):
                                    m = dve.scalar_tensor_tensor(out=S[:, d, h, :], in0=S[:, d, h, :],
                                                                 scalar=gt4[:, d, 1, h:h + 1],
                                                                 in1=b[:, h * P:(h + 1) * P], op0=ALU.mult,
                                                                 op1=ALU.add)
                                read_out(m, key)

                if l == 0:
                    evacuated(dve, ("am", ADA_GROUPS))
                    modulation(0, 1)

                for h in range(GH):
                    dve.wait_ge(s["rinv"], 2 + 2 * GH + h)
                    r = rs_gdn[:, h % 2, t_first:T]
                    o = mixT[:, 2 + h, t_first:T]
                    link(dve.tensor_tensor(o, o, r, ALU.mult), l)
                    dve.scalar_tensor_tensor(out=o, in0=o, scalar=cols[:, COL_GN:COL_GN + 1],
                                             in1=szT[:, h, t_first:T], op0=ALU.mult, op1=ALU.mult
                                             ).then_inc(s["mixd"], 1)

                for k in range(KD):
                    for g in segs:
                        t0, n = SEGS[g]
                        key = ("y", l, k, g)
                        b = product_ready(dve, key)
                        x = xT[:, k, t0:t0 + n]
                        read_out(dve.scalar_tensor_tensor(out=x, in0=b[:, 0:n], scalar=mods_of[l][:, 2 * KD + k, 1 - g:2 - g],
                                                          in1=x, op0=ALU.mult, op1=ALU.add), key)
                norm(l, 2)

                b = product_ready(dve, ("rt", l))[:, 0:NT * N_EXP].rearrange("p (i e) -> p i e", i=NT)[:, i0:NT, :]
                nt = NT - i0
                link(dve.tensor_reduce(rt6[:, i0:NT], b, AX.X, ALU.max), l)
                a = aff[:, i0:NT, :]
                r = rt6[:, i0:NT].unsqueeze(2).to_broadcast([P, nt, N_EXP])
                link(dve.tensor_tensor(a, b, r, ALU.subtract), l)
                read_out(dve.tensor_copy(rt6[:, i0:NT], b[:, :, 0]), ("rt", l))
                evacuated(dve, ("rt", l))
                dve.tensor_copy(rt6[:, i0:NT], rt6[:, i0:NT]).then_inc(s["rmax"], 1)
                for i in tiles:
                    b = product_ready(dve, ("hr", l, i, 1))
                    read_out(dve.tensor_copy(hrow[:, i, 512:1024], b), ("hr", l, i, 1))
                dve.wait_ge(s["rexp"], 1)
                link(dve.tensor_reduce(rt6[:, i0:NT], a, AX.X, ALU.add), l)
                link(dve.reciprocal(rt6[:, i0:NT], rt6[:, i0:NT]), l)
                dve.tensor_tensor(a, a, r, ALU.mult).then_inc(s["aff"], 1)

                for g in segs:
                    t0, n = SEGS[g]
                    cap = CAP_L if g else CAP_C
                    b = product_ready(dve, ("aT", l, g))
                    E = slice(0, N_EXP)
                    w, av, se, cs = (x[E, t0:t0 + n] for x in (tkw, affT, sel, csum))
                    link(dve.tensor_copy(av, b[E, 0:n]), l)
                    read_out(dve.tensor_copy(w, b[E, 0:n]), ("aT", l, g))
                    evacuated(dve, ("aT", l, g))
                    for r8 in range(cap // 8):
                        link(dve.max(top8[:, :], w), l)
                        if r8 < cap // 8 - 1:
                            link(dve.match_replace(w, top8[:, :], w, -1.0), l)
                    thr = top8[:, 7:8]
                    link(dve.tensor_scalar(se, av, thr, None, ALU.is_gt), l)
                    link(dve.tensor_scalar(w, av, thr, None, ALU.is_equal), l)
                    link(dve.tensor_reduce(tkn[:, 0:1], se, AX.X, ALU.add), l)
                    link(dve.tensor_scalar(tkn[:, 1:2], tkn[:, 0:1], -1.0, float(cap), ALU.mult, ALU.add), l)
                    link(dve.tensor_tensor_scan(cs, w, w, 0.0, ALU.add, ALU.max), l)
                    link(dve.scalar_tensor_tensor(out=w, in0=cs, scalar=tkn[:, 1:2], in1=w, op0=ALU.is_le,
                                                  op1=ALU.mult), l)
                    link(dve.tensor_tensor(se, se, w, ALU.add), l)
                    link(dve.tensor_tensor_scan(cs, se, se, 0.0, ALU.add, ALU.max), l)
                    link(dve.tensor_tensor(se, cs, se, ALU.mult), l)
                    dve.tensor_scalar(se, se, -1.0, None, ALU.add).then_inc(s["sel"], 1)
                b = product_ready(dve, ("slot", l))
                read_out(dve.tensor_copy(slotc[:, i0:NT, :].rearrange("p i e -> p (i e)"),
                                         b[:, i0 * N_EXP:NT * N_EXP]), ("slot", l))
                evacuated(dve, ("slot", l))

                dve.tensor_copy(tokaff[:, CT:NT, 0:1], iota[:, CAP_L:CAP_L + SEQ // P].unsqueeze(2))
                if need_ctx:
                    dve.tensor_copy(tokaff[:, 0:CT, 0:1], iota[:, CAP_L:CAP_L + CT].unsqueeze(2))
                dve.tensor_copy(tokaff[:, i0:NT, 1:NW], aff[:, i0:NT, :])
                for t in list(range(CT, NT)) + (list(range(CT)) if need_ctx else []):
                    g, cap = (G[t - CT], CAP_L) if t >= CT else (G[SEQ // P + t], CAP_C)
                    dve.tensor_tensor(g, iota[:, 0:cap].unsqueeze(1).to_broadcast([P, N_EXP, cap]),
                                      slotc[:, t, :].unsqueeze(2).to_broadcast([P, N_EXP, cap]), ALU.is_equal
                                      ).then_inc(s["G"], 1)
                for g in reversed(segs):
                    b = product_ready(dve, ("mc", l, g))
                    cap, w = (CAP_L, 0) if g else (CAP_C, 2)
                    number = b[:, 0:PAIRS * NW].rearrange("p (i c) -> p i c", c=NW)[:, :, 0:1]
                    dve.tensor_copy(idx[:, g, :].unsqueeze(2), number).then_inc(s["idx"], 1)
                    dve.tensor_copy(gcol[:, :, w:w + 1], number)
                    for r in range(0, P, cap):
                        e = r // cap % 2
                        r = slice(r, r + cap)
                        m = dve.tensor_copy(gcol[r, :, w + 1:w + 2], b[r, 1 + e:2 + e + (NW + 2) * (PAIRS - 1):NW + 2]
                                            .unsqueeze(2))
                    read_out(m, ("mc", l, g))
                    evacuated(dve, ("mc", l, g))

                hw = 3 * P if need_ctx else 2 * P
                dve.wait_ge(s["tok"], 1)

                def tokens(name_of, i, q):
                    key = name_of("x%d" % q)
                    b = product_ready(dve, key, i)[:, 0:4 * CAP].rearrange("p (k c) -> p k c", k=2)
                    copy_slots(dve.tensor_copy, b, xs, q, need_ctx, lambda m: read_out(m, key))

                def pair(here, i, nxt):
                    now = gcol[:, bass.ds(i, 1), :] if i is not None else gcol[:, PAIRS - 1:PAIRS, :]
                    dve.tensor_copy(gnow.unsqueeze(1), now).then_inc(s["cur"], 1)
                    dve.wait_ge(s["cur"], plus(1, 1, i) if i is not None else PAIRS)
                    m = dve.tensor_scalar(Sl, tokrow, gnow[:, 0:1], gnow[:, 1:2], ALU.is_equal, ALU.mult)
                    if need_ctx:
                        m = dve.tensor_scalar(Sc, tokrow[:, 0:CTX], gnow[:, 2:3], gnow[:, 3:4], ALU.is_equal,
                                              ALU.mult)
                    m.then_inc(s["S"], 1)
                    for q in range(2):
                        key = here("u%d" % q)
                        b = product_ready(dve, key, i)
                        evacuated(dve, here("g%d" % q), i)
                        read_out(dve.tensor_tensor(hid[:, q, 0:hw], sg[:, q, 0:hw], b[:, 0:hw], ALU.mult), key)
                    if nxt:
                        tokens(here, i, 1)
                    b = product_ready(dve, here("y1"), i)
                    read_out(dve.tensor_copy(ylat[:, 512:1024], b), here("y1"))
                    if nxt:
                        tokens(here, i, 3)
                    for k in range(KD):
                        for g in reversed(segs):
                            t0, n = SEGS[g]
                            key = here("c%d%d" % (k, g))
                            b = product_ready(dve, key, i)
                            x = xT[:, k, t0:t0 + n]
                            read_out(dve.scalar_tensor_tensor(out=x, in0=b[:, 0:n],
                                                              scalar=mods_of[l][:, 5 * KD + k, 1 - g:2 - g], in1=x,
                                                              op0=ALU.mult, op1=ALU.add), key)

                for q in (1, 3):
                    tokens(lambda name: ("first", l, name), None, q)
                with dve.Fori(0, PAIRS - 1) as i:
                    pair(lambda name: ("moe", l, name), i, True)
                pair(lambda name: ("last", l, name), None, False)

            orow = big[:, 0:(NT - CT) * D].rearrange("p (i d) -> p i d", i=NT - CT)
            for i in range(CT, NT):
                b = product_ready(dve, ("out", i, 1))
                read_out(dve.tensor_copy(orow[:, i - CT, 512:1024], b), ("out", i, 1))

        @block.gpsimd
        def _(pool):
            chain = [0, 0]

            def link(ins, l):
                chain[l] += 1
                ins.then_inc(sems[l]["pool_e"], 1)
                pool.wait_ge(sems[l]["pool_e"], chain[l])

            pool.memset(pstage[:, :], 0.0)
            pool.memset(poolw[:, :, :], 0.0).then_inc(sems[0]["zero"], 1)
            pool.memset(ones[:, :], 1.0)
            pool.memset(eps[:, 0:1], EPS)
            pool.memset(eps[:, 1:2], 128.0 * EPS).then_inc(s_ones, 1)
            pool.memset(szrow, 0.0).then_inc(sems[0]["zrow"], 1)
            pool.wait_ge(sems[0]["zero"], 1)

            def parameters(l):
                s = sems[l]
                for dst, src in (
                        (wuq[:, 0, :], A["mla_w_uq"][l, 0:P, :]),
                        (wuq[0:64, 1, :], A["mla_w_uq"][l, P:Q_LORA, :]),
                        (wukv[:, :], A["mla_w_ukv"][l]),
                        (poolw[0:64, 0, 0:64], A["pool_w"][l, 0]),
                        (poolw[64:128, 0, 64:128], A["pool_w"][l, 1]),
                        (poolw[0:64, 1, 0:64], A["pool_w"][l, 2]),
                        (poolw[64:128, 1, 64:128], A["pool_w"][l, 3]),
                        (router[:, :, :], A["moe_router"][l].rearrange("(k p) e -> p k e", p=P)),
                        (rown[:, 0, :], A["mla_k_norm"][l].partition_broadcast(P)),
                        (rown[:, 1, :], A["mla_q_norm"][l].partition_broadcast(P)),
                        (gpar[:, 0, :], A["gdn_a_log"][l].rearrange("d h -> (d h)").partition_broadcast(P)),
                        (gpar[:, 1, :], A["gdn_dt_bias"][l].rearrange("d h -> (d h)").partition_broadcast(P))):
                    pool.dma_start(dst, src).then_inc(s["par"], 16)

            parameters(0)
            for l in range(DEPTH):
                s = sems[l]
                need_ctx = l < DEPTH - 1
                tiles = range(NT) if need_ctx else range(CT, NT)
                segs = (0, 1) if need_ctx else (1,)

                if l == 0:
                    product_ready(pool, ("x", KD - 1, 1))
                else:
                    product_ready(pool, ("last", l - 1, "c%d0" % (KD - 1)))
                pool.memset(at(big, 0, (2 * UW,)), 0.0).then_inc(s["upad"], 1)

                pool.wait_ge(s_const, 16 * CONST_DMAS)
                pool.wait_ge(s_sum, 16)
                def add_shift(dst, src, a, n):
                    return pool.tensor_tensor(dst[:, a:UW - n], src[:, 0:UW - n - a], src[:, a + n:UW], ALU.add)

                for c in range(2):
                    for g in segs:
                        evacuated(pool, ("in", l, "pool%d" % c, g))
                    u = U[:, c, :]
                    link(pool.tensor_tensor(BA[:, 1:UW], u[:, 1:UW], u[:, 0:UW - 1], ALU.add), l)
                    link(pool.tensor_tensor(BB[:, 2:UW - 1], BA[:, 1:UW - 2], BA[:, 3:UW], ALU.add), l)
                    if c == 1:
                        link(pool.tensor_tensor(BA[:, 4:UW - 3], BB[:, 2:UW - 5], BB[:, 6:UW - 1], ALU.add), l)
                        link(pool.tensor_tensor(BB[:, 8:UW - 7], BA[:, 4:UW - 11], BA[:, 12:UW - 3], ALU.add), l)
                    for half, src in ((0, BA), (1, BB)):
                        r = slice(64 * half, 64 * half + 64)
                        for g in segs:
                            t0, n = SEGS[g]
                            link(pool.tensor_scalar(dT[r, c, t0:t0 + n], src[r, UO[g]:UO[g] + n], poolc[r, c, 16:17],
                                                    None, ALU.mult), l)
                    for g in segs:
                        t0, n = SEGS[g]
                        x = dT[:, c, t0:t0 + 8]
                        link(pool.tensor_tensor(x, x, poolc[:, c, 0:8], ALU.mult), l)
                        x = dT[:, c, t0 + n - 8:t0 + n]
                        link(pool.tensor_tensor(x, x, poolc[:, c, 8:16], ALU.mult), l)
                        x = dT[:, c, t0:t0 + n]
                        m = pool.tensor_tensor(x, x, u[:, UO[g]:UO[g] + n], ALU.subtract)
                        if g == 1:
                            m.then_inc(s["pool"], 1)
                        else:
                            link(m, l)

                pool.wait_ge(s["par"], 16 * PAR_DMAS)
                jobs = [("k", i) for i in range(NT)] + [("q", i) for i in tiles]
                for n, (kind, i) in enumerate(jobs):
                    pool.wait_ge(s["rowa"], n + 1)
                    r = rows[:, n % 2, :, :]
                    w = rown[:, 0 if kind == "k" else 1, :].unsqueeze(1).to_broadcast([P, H, QK])
                    m = pool.tensor_tensor(r, r, w, ALU.mult)
                    if i >= CT:
                        link(m, l)
                        x = r[:, :, NOPE:QK]
                        link(pool.tensor_tensor(rot1, x, rope[:, i - CT, 0, :].unsqueeze(1).to_broadcast(
                            [P, H, ROPE]), ALU.mult), l)
                        x4 = x.rearrange("p h (g a e) -> p h g a e", g=2, a=2)
                        s4 = rope[:, i - CT, 1, :].rearrange("p (g a e) -> p g a e", g=2, a=2)
                        for a in range(2):
                            link(pool.tensor_tensor(rot2[:, :, :, a, :], x4[:, :, :, 1 - a, :],
                                                    s4[:, :, a, :].unsqueeze(1).to_broadcast([P, H, 2, ROPE // 4]),
                                                    ALU.mult), l)
                        m = pool.tensor_tensor(x, rot1, rot2.rearrange("p h g a e -> p h (g a e)"), ALU.add)
                    m.then_inc(s["row2"], 1)

                if l == 0:
                    for c in range(2):
                        for g in segs:
                            product_ready(pool, ("pm", l, c, g))
                    pool.memset(dTrow, 0.0).then_inc(s["zrow"], 1)
                pool.wait_ge(s["gbd"], 1)
                pool.wait_ge(s["lmul"], 2 * GH)
                product_ready(pool, ("gc", l))
                for j in range(NT):
                    ti = [tile_of(d, j) for d in range(2)]
                    tt = [slice(i * P, (i + 1) * P) for i in ti]
                    for d in range(2):
                        if j:
                            product_ready(pool, ("v", l, j - 1, d))
                        pool.tensor_tensor(gML[d], tri[:, d, :].unsqueeze(1).to_broadcast([P, GH, P]),
                                           gb[:, 0, ti[d], d * GH:(d + 1) * GH].unsqueeze(2).to_broadcast(
                                               [P, GH, P]), ALU.mult).then_inc(s["tg"], 1)
                    for d in range(2):
                        pool.wait_ge(s["dex"], 2 * j + d + 1)
                        pool.tensor_tensor(gQK[d], gQK[d], tri[:, d, :].unsqueeze(1).to_broadcast([P, GH, P]),
                                           ALU.mult).then_inc(s["dm"], 1)
                    for d in range(2):
                        evacuated(pool, ("kk", l, j, d))
                        evacuated(pool, ("at2", l, j, d))
                        x = gX[d][:, :, 1, :]
                        link(pool.tensor_tensor(x, gAT[d], lev[:, d, 0, :].unsqueeze(1).to_broadcast([P, GH, P]),
                                                ALU.mult), l)
                        pool.tensor_tensor(x, ident[:, :].unsqueeze(1).to_broadcast([P, GH, P]), x, ALU.subtract
                                           ).then_inc(s["x1"], 1)
                        pool.tensor_tensor(gML[d], gAT[d], lev[:, d, 1, :].unsqueeze(1).to_broadcast([P, GH, P]),
                                           ALU.mult).then_inc(s["ml"], 1)
                    for n in range(2, LEVELS):
                        for d in range(2):
                            product_ready(pool, ("y", l, j, d, n - 1))
                            pool.tensor_tensor(gML[d], gAT[d], lev[:, d, n, :].unsqueeze(1).to_broadcast(
                                [P, GH, P]), ALU.mult).then_inc(s["ml"], 1)
                    for d in range(2):
                        evacuated(pool, ("g", l, j, d))
                        pool.tensor_tensor(gQG[d], gQG[d], qkvT[:, 0:GH, tt[d]], ALU.mult).then_inc(s["qg"], 1)

                product_ready(pool, ("rtT", l, 1))
                for j in range(SEQ // CAP_L):
                    m = pool.tensor_scalar(tokrow[:, j * CAP_L:(j + 1) * CAP_L], iota[:, 0:CAP_L], float(j * CAP_L),
                                           None, ALU.add)
                m.then_inc(s["tok"], 1)

                pool.wait_ge(s["hrow"], 16 * len(segs))
                pool.wait_ge(s["idx"], len(segs))
                for p in range(PAIRS):
                    if p == 1:
                        product_ready(pool, ("first", l, "x3"))
                    elif p:
                        product_ready(pool, ("moe", l, "x3"), p - 2)
                    for g in reversed(segs):
                        dst, n = (xlat, 2 * CAP_L) if g else (xctx, 2 * CAP_C)
                        pool.indirect_dma_start(dst[0:n, :], None, hD[g],
                                                bass.IndirectOffsetOnAxis(ap=idx[0:n, g, p:p + 1], axis=0)
                                                ).then_inc(s["gath"], 16)
                    if p == 1 and l + 1 < DEPTH:
                        evacuated(pool, ("cols", l))
                        channel_parameters(pool, l + 1)
                        parameters(l + 1)
    return where


def copy_slots(copy, b, xs, q, need_ctx, finish):
    lat = b[:, :, 0:2 * CAP_L].rearrange("p k (e c) -> p k e c", e=2)
    m = copy(xs[:, 2 * q:2 * q + 2, :, 0:CAP_L], lat)
    if need_ctx:
        con = b[:, :, 2 * CAP_L:2 * CAP].rearrange("p k (e c) -> p k e c", e=2)
        m = copy(xs[:, 2 * q:2 * q + 2, :, CAP_L:CAP], con)
    finish(m)


_INS = ["x", "c", "ctx", "c_ctx", "ada_w", "ada_b", "norm1_g", "norm2_g", "w_in", "mla_q_a_norm", "mla_w_uq",
        "mla_kv_a_norm", "mla_w_ukv", "mla_q_norm", "mla_k_norm", "gdn_conv_w", "gdn_a_log", "gdn_dt_bias",
        "gdn_norm_g", "pool_w", "pool_scale", "w_out", "moe_router", "moe_w_gate", "moe_w_up", "moe_w_down"]


def kernel(**inputs):
    import concourse.bacc as _bacc
    from concourse.bass_utils import run_bass_kernel_spmd as _run

    nc = _bacc.Bacc("TRN2", target_bir_lowering=False, num_devices=1)
    arrays, args = {}, {}
    for name, a in [(n, inputs[n]) for n in _INS] + list(shape_constants().items()):
        a = np.ascontiguousarray(a)
        arrays["in_" + name] = a
        args[name] = nc.dram_tensor("in_" + name, a.shape, mybir.dt.from_np(a.dtype), kind="ExternalInput").ap()
    out = nc.dram_tensor("out", (1, SEQ, D), F32, kind="ExternalOutput").ap()
    build_program(nc, args, out)
    r = _run(nc, [arrays], core_ids=[0])
    return r.results[0]["out"]
```
